# Optimizing a Trainium2 kernel written in Bass

```python
import jax, jax.numpy as jnp
from jax import lax
import numpy as np

D_MODEL = 2048
BATCH = 1
SEQ = 512
DEPTH = 1
DEC_BATCH = 8
DEC_SEQ = 1
PAST_LEN = 2048
PAGE_SIZE = 128

D_ATT = D_MODEL // 2
D_LRU = D_MODEL - D_ATT
HEAD_DIM = 128
N_ATT_HEADS = D_ATT // HEAD_DIM
N_LRU_BLOCKS = 8
LRU_BLOCK = D_LRU // N_LRU_BLOCKS
CONV_W = 4
LRU_C = 8.0
D_FF = 4 * D_MODEL
Q_BLOCK = 128
D_IN_COLS = 3 * D_ATT + N_ATT_HEADS + 2 * D_LRU
EPS = 1e-6
NEG_INF = -1e30

kernel_name = 'hymba_rglru_fox_decode_step'

def rms_norm(x, g):
    xf = x.astype(jnp.float32)
    y = xf * lax.rsqrt(jnp.mean(xf * xf, axis=-1, keepdims=True) + EPS)
    return (y * g.astype(jnp.float32)).astype(x.dtype)

def causal_conv(x, buf, w, b):
    T = x.shape[1]
    xp = jnp.concatenate([buf.astype(x.dtype), x], axis=1)
    out = b
    for j in range(CONV_W):
        out = out + w[j] * xp[:, j:j + T]
    return out.astype(x.dtype), xp[:, T:]

def rg_lru(x, h0, wa, ba, wx, bx, lam):
    B, T, _ = x.shape
    xb = x.reshape(B, T, N_LRU_BLOCKS, LRU_BLOCK)
    r = jax.nn.sigmoid((jnp.einsum('btnc,ncd->btnd', xb, wa).reshape(B, T, D_LRU) + ba).astype(jnp.float32))
    i = jax.nn.sigmoid((jnp.einsum('btnc,ncd->btnd', xb, wx).reshape(B, T, D_LRU) + bx).astype(jnp.float32))
    log_a = -LRU_C * r * jax.nn.softplus(-lam.astype(jnp.float32))
    a = jnp.exp(log_a)
    b_in = jnp.sqrt(-jnp.expm1(2.0 * log_a)) * i * x.astype(jnp.float32)

    def step(h, ab):
        a_t, b_t = ab
        h = a_t * h + b_t
        return h, h

    h_T, hs = lax.scan(step, h0.astype(jnp.float32), (a.swapaxes(0, 1), b_in.swapaxes(0, 1)))
    return hs.swapaxes(0, 1).astype(x.dtype), h_T.astype(x.dtype)

def fox_block(q_blk, q_pos, Fq, k_all, v_all, Fk, k_pos):
    s = jnp.einsum('bqhd,bkhd->bhqk', q_blk.astype(jnp.float32), k_all.astype(jnp.float32)) * (HEAD_DIM ** -0.5)
    s = s + (Fq.transpose(0, 2, 1)[:, :, :, None] - Fk.transpose(0, 2, 1)[:, :, None, :])
    mask = k_pos[None, :] <= q_pos[:, None]
    s = jnp.where(mask[None, None], s, NEG_INF)
    p = jax.nn.softmax(s, axis=-1)
    return jnp.einsum('bhqk,bkhd->bqhd', p, v_all.astype(jnp.float32))

def forgetting_attention(q, k_all, v_all, logf_all, n_past):
    B, Tq = q.shape[0], q.shape[1]
    Tk = k_all.shape[1]
    F = jnp.cumsum(logf_all.astype(jnp.float32), axis=1)
    Fq = F[:, n_past:]
    k_pos = jnp.arange(Tk)
    q_pos = n_past + jnp.arange(Tq)
    qb = Q_BLOCK if Tq % Q_BLOCK == 0 else Tq
    nb = Tq // qb
    qs = q.reshape(B, nb, qb, N_ATT_HEADS, HEAD_DIM).swapaxes(0, 1)
    Fqs = Fq.reshape(B, nb, qb, N_ATT_HEADS).swapaxes(0, 1)
    qps = q_pos.reshape(nb, qb)
    out = lax.map(lambda a: fox_block(a[0], a[2], a[1], k_all, v_all, F, k_pos), (qs, Fqs, qps))
    return out.swapaxes(0, 1).reshape(B, Tq, D_ATT).astype(q.dtype)

def hybrid_layer(x, past_k, past_v, past_logf, conv_buf, h0,
                 g_mix, w_in, b_f, w_conv, b_conv, w_gate_a, b_gate_a, w_gate_x, b_gate_x,
                 lru_lambda, g_att_out, g_lru_out, w_out, g_ffn, w_up, w_down):
    B, T, _ = x.shape
    xn = rms_norm(x, g_mix)
    z = jnp.einsum('btd,dc->btc', xn, w_in)
    cuts = [D_ATT, 2 * D_ATT, 3 * D_ATT, 3 * D_ATT + N_ATT_HEADS, 3 * D_ATT + N_ATT_HEADS + D_LRU]
    q, k, v, f_logit, xl, gl = jnp.split(z, cuts, axis=-1)
    q = q.reshape(B, T, N_ATT_HEADS, HEAD_DIM)
    k = k.reshape(B, T, N_ATT_HEADS, HEAD_DIM)
    v = v.reshape(B, T, N_ATT_HEADS, HEAD_DIM)
    logf = jax.nn.log_sigmoid((f_logit + b_f).astype(jnp.float32)).astype(x.dtype)
    if past_k is None:
        n_past = 0
        k_all, v_all, logf_all = k, v, logf
    else:
        n_past = past_k.shape[1]
        k_all = jnp.concatenate([past_k.astype(k.dtype), k], axis=1)
        v_all = jnp.concatenate([past_v.astype(v.dtype), v], axis=1)
        logf_all = jnp.concatenate([past_logf.astype(logf.dtype), logf], axis=1)
    att = forgetting_attention(q, k_all, v_all, logf_all, n_past)

    xc, new_buf = causal_conv(xl, conv_buf, w_conv, b_conv)
    hs, h_T = rg_lru(xc, h0, w_gate_a, b_gate_a, w_gate_x, b_gate_x, lru_lambda)
    lru = jax.nn.gelu(gl) * hs

    mix = jnp.concatenate([rms_norm(att, g_att_out), rms_norm(lru, g_lru_out)], axis=-1)
    x = x + jnp.einsum('btc,cd->btd', mix, w_out)
    hf = jnp.einsum('btd,df->btf', rms_norm(x, g_ffn), w_up)
    x = x + jnp.einsum('btf,fd->btd', jnp.square(jax.nn.relu(hf)), w_down)
    return x, k, v, logf, new_buf, h_T

def setup_inputs(seed: int = 0) -> dict:
    key = jax.random.key(seed)
    ks = jax.random.split(key, 32)
    n_pages = PAST_LEN // PAGE_SIZE
    n_used = DEC_BATCH * n_pages
    n_pool = (n_used * 5) // 4
    f32 = jnp.float32

    def nrm(k, shape, scale):
        return jax.random.normal(k, shape, f32) * scale

    x_prompt = nrm(ks[0], (BATCH, SEQ, D_MODEL), 1.0)
    x_sample = nrm(ks[1], (DEC_BATCH, DEC_SEQ, D_MODEL), 1.0)
    cache_k = nrm(ks[2], (DEPTH, n_pool, PAGE_SIZE, N_ATT_HEADS, HEAD_DIM), 1.0)
    cache_v = nrm(ks[3], (DEPTH, n_pool, PAGE_SIZE, N_ATT_HEADS, HEAD_DIM), 1.0)
    cache_logf = jax.nn.log_sigmoid(3.0 + nrm(ks[4], (DEPTH, n_pool, PAGE_SIZE, N_ATT_HEADS), 0.5))
    state_conv = nrm(ks[5], (DEPTH, DEC_BATCH, CONV_W - 1, D_LRU), 1.0)
    state_h = nrm(ks[6], (DEPTH, DEC_BATCH, D_LRU), 0.5)
    page_table = jax.random.permutation(ks[7], n_pool)[:n_used].reshape(DEC_BATCH, n_pages).astype(jnp.int32)

    g_mix = 1.0 + nrm(ks[8], (DEPTH, D_MODEL), 0.02)
    w_in = nrm(ks[9], (DEPTH, D_MODEL, D_IN_COLS), D_MODEL ** -0.5)
    b_f = 3.0 + nrm(ks[10], (DEPTH, N_ATT_HEADS), 0.3)
    w_conv = nrm(ks[11], (DEPTH, CONV_W, D_LRU), CONV_W ** -0.5)
    b_conv = nrm(ks[12], (DEPTH, D_LRU), 0.02)
    w_gate_a = nrm(ks[13], (DEPTH, N_LRU_BLOCKS, LRU_BLOCK, LRU_BLOCK), LRU_BLOCK ** -0.5)
    b_gate_a = nrm(ks[14], (DEPTH, D_LRU), 0.02)
    w_gate_x = nrm(ks[15], (DEPTH, N_LRU_BLOCKS, LRU_BLOCK, LRU_BLOCK), LRU_BLOCK ** -0.5)
    b_gate_x = nrm(ks[16], (DEPTH, D_LRU), 0.02)
    a_c = jax.random.uniform(ks[17], (DEPTH, D_LRU), f32, 0.9, 0.999)
    s = a_c ** (1.0 / LRU_C)
    lru_lambda = jnp.log(s) - jnp.log1p(-s)
    g_att_out = 1.0 + nrm(ks[18], (DEPTH, D_ATT), 0.02)
    g_lru_out = 1.0 + nrm(ks[19], (DEPTH, D_LRU), 0.02)
    w_out = nrm(ks[20], (DEPTH, D_ATT + D_LRU, D_MODEL), (D_ATT + D_LRU) ** -0.5)
    g_ffn = 1.0 + nrm(ks[21], (DEPTH, D_MODEL), 0.02)
    w_up = nrm(ks[22], (DEPTH, D_MODEL, D_FF), D_MODEL ** -0.5)
    w_down = nrm(ks[23], (DEPTH, D_FF, D_MODEL), D_FF ** -0.5)
    g_final = 1.0 + nrm(ks[24], (D_MODEL,), 0.02)
    return {'x_prompt': x_prompt, 'x_sample': x_sample, 'cache_k': cache_k, 'cache_v': cache_v,
            'cache_logf': cache_logf, 'state_conv': state_conv, 'state_h': state_h,
            'page_table': page_table, 'g_mix': g_mix, 'w_in': w_in, 'b_f': b_f,
            'w_conv': w_conv, 'b_conv': b_conv, 'w_gate_a': w_gate_a, 'b_gate_a': b_gate_a,
            'w_gate_x': w_gate_x, 'b_gate_x': b_gate_x, 'lru_lambda': lru_lambda,
            'g_att_out': g_att_out, 'g_lru_out': g_lru_out, 'w_out': w_out, 'g_ffn': g_ffn,
            'w_up': w_up, 'w_down': w_down, 'g_final': g_final}

def reference(x_prompt, x_sample, cache_k, cache_v, cache_logf, state_conv, state_h, page_table,
              g_mix, w_in, b_f, w_conv, b_conv, w_gate_a, b_gate_a, w_gate_x, b_gate_x,
              lru_lambda, g_att_out, g_lru_out, w_out, g_ffn, w_up, w_down, g_final):
    n_pages = page_table.shape[1]
    past_len = n_pages * cache_k.shape[2]
    xp, xs = x_prompt, x_sample
    pk, pv, pf, pc, ph = [], [], [], [], []
    sk, sv, sf, sc, sh = [], [], [], [], []
    for l in range(DEPTH):
        w = (g_mix[l], w_in[l], b_f[l], w_conv[l], b_conv[l], w_gate_a[l], b_gate_a[l],
             w_gate_x[l], b_gate_x[l], lru_lambda[l], g_att_out[l], g_lru_out[l], w_out[l],
             g_ffn[l], w_up[l], w_down[l])
        zero_buf = jnp.zeros((xp.shape[0], CONV_W - 1, D_LRU), xp.dtype)
        zero_h = jnp.zeros((xp.shape[0], D_LRU), xp.dtype)
        xp, k1, v1, f1, c1, h1 = hybrid_layer(xp, None, None, None, zero_buf, zero_h, *w)
        dec_b = xs.shape[0]
        past_k = cache_k[l][page_table].reshape(dec_b, past_len, N_ATT_HEADS, HEAD_DIM)
        past_v = cache_v[l][page_table].reshape(dec_b, past_len, N_ATT_HEADS, HEAD_DIM)
        past_f = cache_logf[l][page_table].reshape(dec_b, past_len, N_ATT_HEADS)
        xs, k2, v2, f2, c2, h2 = hybrid_layer(xs, past_k, past_v, past_f, state_conv[l], state_h[l], *w)
        pk.append(k1); pv.append(v1); pf.append(f1); pc.append(c1); ph.append(h1)
        sk.append(k2); sv.append(v2); sf.append(f2); sc.append(c2); sh.append(h2)
    y_prompt = rms_norm(xp, g_final)
    y_sample = rms_norm(xs, g_final)
    return (y_prompt, y_sample,
            jnp.stack(pk), jnp.stack(pv), jnp.stack(pf), jnp.stack(pc), jnp.stack(ph),
            jnp.stack(sk), jnp.stack(sv), jnp.stack(sf), jnp.stack(sc), jnp.stack(sh))


_drawn_inputs = setup_inputs


def setup_inputs(seed=0):
    import zlib

    import numpy as np

    out = dict(_drawn_inputs(seed))
    spreads = {}
    factors = {'b_gate_a': 8.0,
     'b_gate_x': 7.28,
     'g_att_out': 5.419,
     'g_lru_out': 5.305,
     'g_ffn': 3.652,
     'g_final': 2.783}
    for name, (base, spread) in spreads.items():
        noise = np.random.default_rng([zlib.crc32(name.encode()), seed]).standard_normal(out[name].shape)
        drawn = base * np.exp(spread * noise) if base else spread * noise
        out[name] = __import__('jax').numpy.asarray(drawn.astype(out[name].dtype))
    for name, factor in factors.items():
        out[name] = (out[name] * factor).astype(out[name].dtype)
    return out
```

```python
from contextlib import ExitStack

import concourse.bass as bass
from concourse import mybir

F32 = mybir.dt.float32
F32R = mybir.dt.float32r
I32 = mybir.dt.int32
U32 = mybir.dt.uint32
ALU = mybir.AluOpType
ACT = mybir.ActivationFunctionType
AX = mybir.AxisListType
RED = bass.bass_isa.ReduceOp

P = 128
EPS = 1e-6
NEG = -1e30
LRU_C = 8.0


def hymba_step(nc, x_prompt, x_sample, cache_k, cache_v, cache_logf, state_conv, state_h, page_table,
               g_mix, w_in, b_f, w_conv, b_conv, w_gate_a, b_gate_a, w_gate_x, b_gate_x, lru_lambda,
               g_att_out, g_lru_out, w_out, g_ffn, w_up, w_down, g_final,
               y_prompt, y_sample, new_k_p, new_v_p, new_f_p, new_conv_p, new_h_p,
               new_k_s, new_v_s, new_f_s, new_conv_s, new_h_s):
    SEQ, D = x_prompt.shape[1], x_prompt.shape[2]
    NB = x_sample.shape[0]
    T = SEQ + NB
    HT = T // 2
    HB = SEQ - HT
    KD = D // P
    NH, HD = cache_k.shape[3], cache_k.shape[4]
    DA = NH * HD
    NL = (D - DA) // P
    NPG = page_table.shape[1]
    FF = w_up.shape[2]
    CW = w_conv.shape[1]
    TT = SEQ // P
    SCALE = float(HD) ** -0.5
    CH = 8
    NC = FF // P // CH
    assert HD == P and NH == NL == NB == CH == 8 and KD == 16 and T % 4 == 0 and NPG % 4 == 0 and TT == 4

    w_in_v = w_in[0].rearrange("(k p) c -> p k c", p=P)
    w_out_v = w_out[0].rearrange("(k p) c -> p k c", p=P)
    w_up_v = w_up[0].rearrange("(k p) c -> p k c", p=P)
    w_down_v = w_down[0].rearrange("(g k p) c -> g p k c", p=P, k=CH)
    k_pages = cache_k[0].rearrange("g p h d -> g p (h d)")
    v_pages = cache_v[0].rearrange("g p h d -> g p (h d)")
    COL_F, COL_X, COL_G = 3 * DA, 3 * DA + NH, 3 * DA + NH + NL * P

    U_Q, U_L = 1, 1 + NH
    U_O = U_L + 4 * NH
    U_F = U_O + KD
    UC = 2 * CH
    TC = CH + 2 * CH
    N_UNITS = U_F + NC * UC

    R_CONV, R_BCONV = 0, CW * NL
    R_BA, R_BX, R_LAM = R_BCONV + NL, R_BCONV + 2 * NL, R_BCONV + 3 * NL
    R_GATT, R_GLRU = R_LAM + NL, R_LAM + 2 * NL
    R_GMIX = R_GLRU + NL
    R_GFFN, R_GFIN = R_GMIX + KD, R_GMIX + 2 * KD
    assert R_GFIN + KD == P

    xT_spill = nc.dram_tensor("xT_spill", [P, KD, T], F32, kind="Internal").ap()

    with ExitStack() as ctx:
        def sb(name, shape, dt=F32, scope=ctx):
            return scope.enter_context(nc.sbuf_tensor(name, shape, dt))

        def sem(name):
            return ctx.enter_context(nc.semaphore(name))

        PS = ctx.enter_context(nc.psum_tensor("PS", [P, 8, 512], F32))

        XH = sb("XH", [P, KD, T], F32R)
        XL = sb("XL", [P, KD, T], F32R)
        A = sb("A", [P, KD, T])
        RAW = sb("RAW", [P, 2, 2048])
        WH = [sb(f"WH{s}", [P, 2048], F32R) for s in range(2)]
        WL = [sb(f"WL{s}", [P, 2048], F32R) for s in range(2)]
        ident = sb("ident", [P, P])
        ones = sb("ones", [P, P])
        PRM = sb("PRM", [P, P])

        first_scope, mix_scope, ffn_scope, out_scope = ExitStack(), ExitStack(), ExitStack(), ExitStack()
        loop_scope = ExitStack()
        PGT = sb("PGT", [1, NB * NPG], I32, loop_scope)
        SUF = sb("SUF", [P, NH, NB, NPG], scope=loop_scope)
        maskneg = sb("maskneg", [P, P], scope=loop_scope)
        FT = sb("FT", [P, TT, NH], scope=loop_scope)
        LS = sb("LS", [P, TT + 2, NH], scope=loop_scope)
        CPOS = sb("CPOS", [P, NL], scope=loop_scope)
        CNEG = sb("CNEG", [P, NL], scope=loop_scope)
        H0 = sb("H0", [P, NL, NB], scope=loop_scope)
        CST = sb("CST", [P, NL, NB * (CW - 1)], scope=loop_scope)

        XT = sb("XT", [P, TT, D], scope=first_scope)
        XS = sb("XS", [NB, D], scope=first_scope)
        PRW = sb("PRW", [P, P], scope=first_scope)
        nbuf0 = (sb("SQ0", [P, 2, T], scope=first_scope), sb("XN0", [P, 2, T], scope=first_scope),
                 sb("RS0", [P, 1, T], scope=first_scope))
        first_scope.close()
        LG = sb("LG", [P, P, NH], scope=first_scope)
        LT = sb("LT", [P, NH, P], scope=first_scope)
        MT = sb("MT", [P, NH, P], scope=first_scope)
        SHW = sb("SHW", [NB, NL * P], scope=first_scope)
        SCW = sb("SCW", [NB * (CW - 1), NL * P], scope=first_scope)
        YH = sb("YH", [NH, T], scope=first_scope)
        IDX = sb("IDX", [P, 1], U32, first_scope)
        TOT = sb("TOT", [P, NH], scope=first_scope)
        low = sb("low", [P, P], scope=first_scope)
        tri = sb("tri", [P, P], scope=first_scope)
        later = sb("later", [P, P], scope=first_scope)
        YF = sb("YF", [P, TT + 2, NH], scope=first_scope)
        Z0, Z1, Z2 = (sb(f"Z{n}", [P, TT + 2, NH], scope=first_scope) for n in range(3))
        BF = sb("BF", [NH, 1], scope=first_scope)
        first_scope.close()

        KR = sb("KR", [P, 2, NH * HD], scope=mix_scope)
        VR = sb("VR", [P, 2, NH * HD], scope=mix_scope)
        QB = sb("QB", [P, NH * HD], scope=mix_scope)
        DQ = sb("DQ", [P, NH * HD], scope=mix_scope)
        GW = sb("GW", [P, 2, P], scope=mix_scope)
        qcur = sb("qcur", [P, SEQ], scope=mix_scope)
        kT = sb("kT", [P, SEQ], scope=mix_scope)
        vT = sb("vT", [P, SEQ], scope=mix_scope)
        ktok = sb("ktok", [P, TT, HD], scope=mix_scope)
        vtok = sb("vtok", [P, TT, HD], scope=mix_scope)
        PR = sb("PR", [P, 1280], scope=mix_scope)
        PT = sb("PT", [P, 1280], scope=mix_scope)
        XC = sb("XC", [P, T], scope=mix_scope)
        XW = sb("XW", [P, CW - 1 + SEQ + NB * CW], scope=mix_scope)
        SC = sb("SC", [P, NH, NPG], scope=mix_scope)
        PP = sb("PP", [P, NH, NPG], scope=mix_scope)
        KS = sb("KS", [P, NH, NB], scope=mix_scope)
        VS = sb("VS", [P, NH, NB], scope=mix_scope)
        MX = sb("MX", [P, NH, NB], scope=mix_scope)
        M8 = sb("M8", [P, NH], scope=mix_scope)
        MALL = sb("MALL", [P, NH], scope=mix_scope)
        DEN = sb("DEN", [P, NH, NB], scope=mix_scope)
        PVS = sb("PVS", [P, NH, NB], scope=mix_scope)
        NM = sb("NM", [P, TT], scope=mix_scope)
        NMS = sb("NMS", [P, TT], scope=mix_scope)
        SUMS = sb("SUMS", [P, TT], scope=mix_scope)
        RSUM = sb("RSUM", [P, TT], scope=mix_scope)
        HALL = sb("HALL", [P, 1 + NB, NL], scope=mix_scope)
        CVALL = sb("CVALL", [P, (1 + NB) * (CW - 1), NL], scope=mix_scope)
        mix_scope.close()
        loop_scope.close()

        nbuf1 = (sb("SQ1", [P, 2, T], scope=ffn_scope), sb("XN1", [P, 2, T], scope=ffn_scope),
                 sb("RS1", [P, 2, T], scope=ffn_scope))
        RT = sb("RT", [P, T], scope=ffn_scope)
        HF = sb("HF", [P, T], scope=ffn_scope)
        HH = sb("HH", [P, CH, T], F32R, out_scope)
        HL = sb("HL", [P, CH, T], F32R, out_scope)
        out_scope.close()
        YT = sb("YT", [P, TT, D], scope=out_scope)
        YS = sb("YS", [NB, D], scope=out_scope)
        out_scope.close()
        ffn_scope.close()
        raw_full = [sem(f"raw_full{s}") for s in range(2)]
        hi_done, lo_done = sem("hi_done"), sem("lo_done")
        tile_done = sem("tile_done")
        tile_out = [sem(f"tile_out{s}") for s in range(2)]
        consts_ready, params_in, x_in, table_in = sem("consts_ready"), sem("params_in"), sem("x_in"), sem("table_in")
        table_t, table_ready = sem("table_t"), sem("table_ready")
        x_t, x_ready = sem("x_t"), [sem(f"x_ready{s}") for s in range(2)]
        xs_ready = sem("xs_ready")
        spilled, respilled = sem("spilled"), sem("respilled")
        sq_ready, sq_used, ss_done, root_ready = sem("sq_ready"), sem("sq_used"), sem("ss_done"), sem("root_ready")
        xn_ready, xh_ready, xl_ready = sem("xn_ready"), sem("xh_ready"), sem("xl_ready")
        setup_in, gather_in, bf_in = sem("setup_in"), sem("gather_in"), sem("bf_in")
        masks_ready = sem("masks_ready")
        yh_ready, logit_t, state_t, past_t = sem("yh_ready"), sem("logit_t"), sem("state_t"), sem("past_t")
        absneg_ready, expneg_ready, logf_ready = sem("absneg_ready"), sem("expneg_ready"), sem("logf_ready")
        state_ready, past_ready, tot_ready = sem("state_ready"), sem("past_ready"), sem("tot_ready")
        cum_ps, suf_ps, cum_ready = sem("cum_ps"), sem("suf_ps"), sem("cum_ready")
        logf_out, pgt_in = sem("logf_out"), sem("pgt_in")
        diag_ready, qb_ps, qb_ready = sem("diag_ready"), sem("qb_ps"), sem("qb_ready")
        k_full = [sem(f"k_full{s}") for s in range(2)]
        v_full = [sem(f"v_full{s}") for s in range(2)]
        pool_prod, k_scored, v_used = sem("pool_prod"), sem("k_scored"), sem("v_used")
        dve_prod = sem("dve_prod")
        qdf_ready, s_done, nm_ready, exp_done = sem("qdf_ready"), sem("s_done"), sem("nm_ready"), sem("exp_done")
        p_norm, pt_ps, pt_ready, att_ps, att_ready = sem("p_norm"), sem("pt_ps"), sem("pt_ready"), sem("att_ps"), sem("att_ready")
        ktr_ps, vtr_ps, ktok_ready, vtok_ready = sem("ktr_ps"), sem("vtr_ps"), sem("ktok_ready"), sem("vtok_ready")
        k_out, v_out = sem("k_out"), sem("v_out")
        gw_full, conv_done, gates_ps = sem("gw_full"), sem("conv_done"), sem("gates_ps")
        sig_done, decay_done, ratio_ready, root_done, lru_done = (
            sem("sig_done"), sem("decay_done"), sem("ratio_ready"), sem("root_done"), sem("lru_done"))
        m8_ready, mall_ready, shifted, pp_ready, pvs_ready = (
            sem("m8_ready"), sem("mall_ready"), sem("shifted"), sem("pp_ready"), sem("pvs_ready"))
        m8_seen = sem("m8_seen")
        merge_in, merge_ps, merge_sub, merge_exp, merged = (
            sem("merge_in"), sem("merge_ps"), sem("merge_sub"), sem("merge_exp"), sem("merged"))
        tail_t, tail_ready, tail_rows, tail_out = sem("tail_t"), sem("tail_ready"), sem("tail_rows"), sem("tail_out")
        h_ready, sq_h_ready = sem("h_ready"), sem("sq_h_ready")
        yn_ready, y_t, ys_t, yt_ready, ys_ready, y_out = (
            sem("yn_ready"), sem("y_t"), sem("ys_t"), [sem(f"yt_ready{s}") for s in range(2)], sem("ys_ready"), sem("y_out"))

        def at(n, half):
            return n % 2, n // 2 + half

        def out_of_banks(t):
            return [(tile_out[0], (t + 1) // 2), (tile_out[1], t // 2)]

        def one(i):
            return bass.ds(i, 1)

        def pair_view(pair):
            return PS[:, 2 * pair:2 * pair + 2, 0:HT]

        S_AT = [(4, 0), (4, 128), (5, 0), (6, 0)]
        P_AT = [0, 128, 384, 768]
        PT_BANK = [(4, 0), (5, 0), (6, 0), (6, 256)]
        PT_AT = [0, 512, 896, 1152]
        K_Q = NPG // 4

        mrg = [qcur[:, 64 * n:64 * n + 64].rearrange("p (h b) -> p h b", h=NH) for n in range(8)]
        merge_e = qcur[:, 5 * 64:7 * 64]

        block = ctx.enter_context(nc.Block())

        @block.sync
        def _(sp):
            def load_unit(n, half, src, peeled=False):
                slot, w = at(n, half)
                if not peeled:
                    sp.wait_ge(lo_done, 2 * w + slot - 1)
                dst = RAW[:, slot, :].rearrange("p (k c) -> p k c", c=src.shape[2])
                sp.dma_start(dst, src).then_inc(raw_full[slot], 16)

            def cols(view, c):
                return view[:, :, bass.ds(c, P)]

            rows = [(w_conv[0], R_CONV), (b_conv, R_BCONV), (b_gate_a, R_BA), (b_gate_x, R_BX), (lru_lambda, R_LAM),
                    (g_att_out, R_GATT), (g_lru_out, R_GLRU), (g_mix, R_GMIX), (g_ffn, R_GFFN),
                    (g_final.rearrange("(a n) -> a n", a=1), R_GFIN)]
            for j in range(TT):
                sp.dma_start(XT[:, j, :], x_prompt[0, j * P:(j + 1) * P, :]).then_inc(x_in, 16)
            sp.dma_start(XS[:, :], x_sample[:, 0, :]).then_inc(x_in, 16)
            for src, r in rows:
                n = src.shape[0] * src.shape[1] // P
                sp.dma_start(PRW[r:r + n, :], src.rearrange("a (n q) -> (a n) q", q=P)).then_inc(table_in, 16)
            load_unit(0, 0, cols(w_in_v, COL_F), True)
            load_unit(1, 0, cols(w_in_v, 0), True)
            sp.dma_start(PGT[:, :], page_table.rearrange("(a b) n -> a (b n)", a=1)).then_inc(pgt_in, 16)
            sp.wait_ge(x_ready[0], KD // 2)
            sp.wait_ge(x_ready[1], KD // 2)
            sp.wait_ge(xs_ready, 1)
            sp.dma_start(xT_spill, A[:, :, :]).then_inc(spilled, 16)
            sp.dma_start(SHW[:, :], state_h[0]).then_inc(setup_in, 16)
            sp.dma_start(SCW[:, :], state_conv[0].rearrange("b j c -> (b j) c")).then_inc(setup_in, 16)
            sp.dma_start(BF[:, :], b_f.rearrange("a h -> h a")).then_inc(bf_in, 16)
            with sp.Fori(0, (NH - 2) // 2) as j:
                load_unit(2, j, cols(w_in_v, P * (2 * j + 1)))
                load_unit(3, j, cols(w_in_v, P * (2 * j + 2)))
            load_unit(U_Q + NH - 1, 0, cols(w_in_v, P * (NH - 1)))
            load_unit(U_L, 0, cols(w_in_v, DA))
            load_unit(U_L + 1, 0, cols(w_in_v, 2 * DA))
            sp.wait_ge(logf_ready, 1)
            sp.dma_start(new_f_p[0, 0].rearrange("(j p) h -> p j h", p=P), LS[:, 0:TT, :]).then_inc(logf_out, 16)
            sp.dma_start(new_f_s[0, :, 0, :], LS[0:NB, TT, :]).then_inc(logf_out, 16)
            sp.wait_ge(cum_ready, 3)
            sp.wait_ge(state_ready, 2)
            sp.wait_ge(pgt_in, 16)

            def page(i, b):
                return sp.value_load(PGT[0:1, one(i * NPG + b)], min_val=0, max_val=cache_k.shape[1] - 1)

            def step(i, head, prev, nxt, first_v=False):
                for q in range(4):
                    if head:
                        src = [lambda: cols(w_in_v, COL_X + P * i), lambda: cols(w_in_v, COL_G + P * i),
                               lambda: cols(w_in_v, DA + P * (i + 1)) if nxt else cols(w_out_v, 0),
                               lambda: cols(w_in_v, 2 * DA + P * (i + 1)) if nxt else cols(w_out_v, P)][q]
                        load_unit(U_L + 2 + q, 2 * i, src())
                    if head and q == 1:
                        if prev:
                            sp.wait_ge(gates_ps, i)
                        sp.dma_start(GW[:, 0, :], w_gate_a[0, one(i), :, :].rearrange("a p c -> p (a c)")).then_inc(gw_full, 16)
                        sp.dma_start(GW[:, 1, :], w_gate_x[0, one(i), :, :].rearrange("a p c -> p (a c)")).then_inc(gw_full, 16)
                    for b in range(K_Q * q, K_Q * (q + 1)):
                        if head:
                            if prev or b >= 2:
                                sp.wait_ge(k_scored, NPG * i + b - 1)
                            sp.dma_start(KR[:, b % 2, :], k_pages[one(page(i, b)), :, :].rearrange("a p f -> p (a f)"))\
                              .then_inc(k_full[b % 2], 16)
                        if prev:
                            if not first_v or b >= 2:
                                sp.wait_ge(v_used, NPG * (i - 1) + b - 1)
                            sp.dma_start(VR[:, b % 2, :], v_pages[one(page(i - 1, b)), :, :].rearrange("a p f -> p (a f)"))\
                              .then_inc(v_full[b % 2], 16)

            step(0, True, False, True)
            step(1, True, True, True, True)
            with sp.Fori(2, NB - 1) as i:
                step(i, True, True, True)
            step(NB - 1, True, True, False)
            step(NB, False, True, False)

            sp.wait_ge(tail_ready, 1)
            sp.wait_ge(tail_rows, 1)
            hr = (CW - 1) * NL
            sp.dma_start(new_k_s[0, :, 0, :, :].rearrange("b h d -> b (h d)"), KR[0:NB, 0, :]).then_inc(tail_out, 16)
            sp.dma_start(new_v_s[0, :, 0, :, :].rearrange("b h d -> b (h d)"), VR[0:NB, 0, :]).then_inc(tail_out, 16)
            sp.dma_start(new_h_p[0].rearrange("a (n q) -> (a n) q", q=P), KR[0:NL, 1, 0:P]).then_inc(tail_out, 16)
            sp.dma_start(new_h_s[0].rearrange("a (n q) -> (a n) q", q=P), KR[NL:NL * (NB + 1), 1, 0:P]).then_inc(tail_out, 16)
            cv_rows = new_conv_s[0].rearrange("b j (n q) -> (b j n) q", q=P)
            half = hr * (NB + 1) // 2
            sp.dma_start(new_conv_p[0].rearrange("b j (n q) -> (b j n) q", q=P), KR[0:hr, 1, P:2 * P]).then_inc(tail_out, 16)
            sp.dma_start(cv_rows[0:half - hr, :], KR[hr:half, 1, P:2 * P]).then_inc(tail_out, 16)
            sp.dma_start(cv_rows[half - hr:, :], KR[0:half, 1, 2 * P:3 * P]).then_inc(tail_out, 16)
            sp.wait_ge(xn_ready, 2 * KD)
            sp.dma_start(A[:, :, :], xT_spill).then_inc(respilled, 16)
            with sp.Fori(0, (KD - 2) // 2) as j:
                load_unit(U_O + 2, j, cols(w_out_v, P * (2 * j + 2)))
                load_unit(U_O + 3, j, cols(w_out_v, P * (2 * j + 3)))
            with sp.Fori(0, NC) as c:
                with sp.Fori(0, CH // 2) as j:
                    load_unit(U_F, c * (UC // 2) + j, cols(w_up_v, P * (CH * c + 2 * j)))
                    load_unit(U_F + 1, c * (UC // 2) + j, cols(w_up_v, P * (CH * c + 2 * j + 1)))
                with sp.Fori(0, CH // 2) as j:
                    for s in range(2):
                        load_unit(U_F + CH + s, c * (UC // 2) + j,
                                  w_down_v[one(c), :, :, bass.ds(2 * P * (2 * j + s), 2 * P)].rearrange("a p k c -> p (a k) c"))
            for g in range(4):
                sp.wait_ge(yt_ready[0], 2 * (g + 1))
                sp.wait_ge(yt_ready[1], 2 * (g + 1))
                sp.wait_ge(ys_ready, g + 1)
                f = slice(g * D // 4, (g + 1) * D // 4)
                sp.dma_start(y_prompt[0, :, f].rearrange("(j p) f -> p j f", p=P), YT[:, :, f]).then_inc(y_out, 16)
                sp.dma_start(y_sample[:, 0, f], YS[:, f]).then_inc(y_out, 16)
            sp.wait_ge(y_out, 8 * 16)
            sp.wait_ge(logf_out, 2 * 16)
            sp.wait_ge(tail_out, 7 * 16)
            sp.wait_ge(k_out, NH * 16)
            sp.wait_ge(v_out, NH * 16)

        @block.gpsimd
        def _(pool):
            pool.memset(ident[:, :], 0.0).then_inc(consts_ready, 1)
            pool.memset(ones[:, :], 1.0).then_inc(consts_ready, 1)
            pool.memset(maskneg[:, :], 0.0).then_inc(consts_ready, 1)
            pool.wait_ge(consts_ready, 3)
            pool.affine_select(out=ident[:, :], in_=ident[:, :], compare_op=ALU.not_equal, fill=1.0, base=0,
                               pattern=[[-1, P]], channel_multiplier=1).then_inc(consts_ready, 1)
            pool.affine_select(out=maskneg[:, :], in_=maskneg[:, :], compare_op=ALU.is_ge, fill=NEG, base=0,
                               pattern=[[-1, P]], channel_multiplier=1).then_inc(consts_ready, 1)
            pool.wait_ge(x_t, KD + 1)
            pool.affine_select(out=low[:, :], in_=ones[:, :], compare_op=ALU.is_gt, fill=0.0, base=0,
                               pattern=[[-1, P]], channel_multiplier=1).then_inc(masks_ready, 1)
            pool.affine_select(out=tri[:, :], in_=ones[:, :], compare_op=ALU.is_ge, fill=0.0, base=0,
                               pattern=[[1, P]], channel_multiplier=-1).then_inc(masks_ready, 1)
            later_v = later[:, :].rearrange("p (b n) -> p b n", b=NB)
            pool.wait_ge(masks_ready, 2)
            pool.affine_select(out=later_v, in_=low[:, :].rearrange("p (b n) -> p b n", b=NB), compare_op=ALU.is_gt,
                               fill=0.0, base=NPG, pattern=[[NPG, NB], [0, NPG]], channel_multiplier=-1)\
                .then_inc(masks_ready, 1)
            pool.dma_start(IDX[:, :], page_table.rearrange("b (n a) -> (b n) a", a=1).bitcast(U32)).then_inc(gather_in, 16)
            pool.wait_ge(gather_in, 16)
            pool.indirect_dma_start(LG[:, :, :].rearrange("p k h -> p (k h)"), None,
                                    cache_logf[0].rearrange("g k h -> g (k h)"),
                                    bass.IndirectOffsetOnAxis(ap=IDX[:, 0:1], axis=0)).then_inc(gather_in, 16)

            def step(i):
                pool.wait_ge(qb_ready, i + 1)
                for q in range(4):
                    b = K_Q * q + K_Q - 1
                    pool.wait_ge(k_full[b % 2], 16 * (NPG // 2 * i + b // 2 + 1))
                    pool.tensor_tensor(KR[:, b % 2, :], KR[:, b % 2, :], QB[:, :], ALU.mult).then_inc(pool_prod, 1)
                pool.wait_ge(m8_ready, i + 1)
                pool.sem_inc(m8_seen, 1)
                pool.partition_all_reduce(MALL[:, :], M8[:, :], P, RED.max).then_inc(mall_ready, 1)

            with pool.Fori(0, NB) as i:
                step(i)

        @block.scalar
        def _(act):
            def split_hi(n, half, tiles=None, peeled=False):
                slot, w = at(n, half)
                act.wait_ge(raw_full[slot], 16 * (w + 1))
                if not peeled:
                    act.wait_ge(tile_done, 2 * w + slot - 1 if tiles is None else tiles)
                nc.scalar.activation(WH[slot][:, :], RAW[:, slot, :], ACT.Copy).then_inc(hi_done, 1)

            def tile_wait(n, half):
                slot, w = at(n, half)
                act.wait_ge(tile_done, 2 * w + slot + 1)
                return slot

            def norm(n, bufs, first, last, groups, sources=()):
                SQ, XN, RS = bufs
                for s, v in sources:
                    act.wait_ge(s, v)
                for g, (k0, k1) in enumerate(groups):
                    def pair(j, start):
                        for s in range(2):
                            if not start:
                                act.wait_ge(sq_used, KD * n + 2 * j + s - 1)
                            nc.scalar.activation(SQ[:, s, :], A[:, one(2 * j + s), :], ACT.Square).then_inc(sq_ready, 1)
                    pair(k0 // 2, k0 == 0 and first)
                    with act.Fori(k0 // 2 + 1, k1 // 2) as j:
                        pair(j, False)
                for g, (k0, k1) in enumerate(groups):
                    act.wait_ge(ss_done, n + g + (n > 1) + 1)
                    nc.scalar.activation(RS[:, g, :].rearrange("p (a t) -> p a t", a=2), PS[:, 4 + 2 * g:6 + 2 * g, 0:HT],
                                         ACT.Sqrt, scale=1.0 / (P * (k1 - k0)), bias=EPS).then_inc(root_ready, 1)
                if not last:
                    with act.Fori(0, KD // 2) as j:
                        for s in range(2):
                            act.wait_ge(xn_ready, KD * n + 2 * j + s + 1)
                            nc.scalar.activation(XH[:, one(2 * j + s), :], XN[:, s, :], ACT.Copy).then_inc(xh_ready, 1)

            act.wait_ge(table_t, 1)
            nc.scalar.activation(PRM[:, :], PS[:, 7, 0:P], ACT.Copy).then_inc(table_ready, 1)
            for k in range(0, KD, 2):
                act.wait_ge(x_t, k + 1)
                nc.scalar.activation(A[:, k, 0:SEQ], PS[:, 4, :], ACT.Copy).then_inc(x_ready[0], 1)
            act.wait_ge(x_t, KD + 1)
            nc.scalar.activation(A[:, :, SEQ:T], PS[:, 6, 0:KD * NB].rearrange("p (k b) -> p k b", k=KD), ACT.Copy)\
                .then_inc(xs_ready, 1)
            split_hi(0, 0, peeled=True)
            norm(0, nbuf0, True, False, [(0, KD)], [(x_ready[0], KD // 2), (x_ready[1], KD // 2), (xs_ready, 1)])

            split_hi(1, 0, peeled=True)
            act.wait_ge(absneg_ready, 1)
            nc.scalar.activation(Z1[:, :, :], Z0[:, :, :], ACT.Exp).then_inc(expneg_ready, 1)
            act.wait_ge(spilled, 16)
            with act.Fori(0, NH // 2) as j:
                for s in range(2):
                    split_hi(U_Q + 1 + s, j)
                    slot = tile_wait(U_Q + s, j)
                    nc.scalar.activation(A[:, one(2 * j + s), :].rearrange("p a (c t) -> p (a c) t", c=2),
                                         pair_view(slot), ACT.Copy).then_inc(tile_out[slot], 1)
            for g in range(2):
                act.wait_ge(past_t, g + 1)
                nc.scalar.activation(LT[:, 4 * g:4 * g + 4, :], PS[:, 4 + g, :], ACT.Copy).then_inc(past_ready, 1)
            for g in range(2):
                act.wait_ge(suf_ps, g + 1)
                nc.scalar.activation(SUF[:, 4 * g:4 * g + 4, :, :], PS[:, 4 + g, :].rearrange("p (h b n) -> p h b n", h=4, b=NB),
                                     ACT.Copy).then_inc(cum_ready, 1)
            act.wait_ge(cum_ps, 1)
            nc.scalar.activation(FT[:, :, :], PS[:, 6, 0:TT * NH].rearrange("p (j h) -> p j h", j=TT), ACT.Copy,
                                 scale=-1.0 / SCALE).then_inc(cum_ready, 1)
            act.wait_ge(state_ready, 2)

            def gates(h):
                act.wait_ge(gates_ps, h + 1)
                act.wait_ge(pt_ps, 3 * h)
                act.wait_ge(att_ps, h)
                ba, bx = PRM[:, one(R_BA + h)], PRM[:, one(R_BX + h)]
                nc.scalar.activation(PR[:, 0:SEQ], PS[:, 4, :], ACT.Sigmoid, bias=ba)
                nc.scalar.activation(PR[:, SEQ:T], PS[:, 6, 0:NB], ACT.Sigmoid, bias=ba)
                nc.scalar.activation(PR[:, T:T + SEQ], PS[:, 5, :], ACT.Sigmoid, bias=bx)
                nc.scalar.activation(PR[:, T + SEQ:2 * T], PS[:, 6, NB:2 * NB], ACT.Sigmoid, bias=bx).then_inc(sig_done, 1)
                act.wait_ge(sig_done, h + 1)
                nc.scalar.activation(PT[:, 0:T], PR[:, 0:T], ACT.Tanh, scale=CPOS[:, one(h)])
                nc.scalar.activation(PR[:, 0:T], PR[:, 0:T], ACT.Exp, scale=CNEG[:, one(h)]).then_inc(decay_done, 1)
                act.wait_ge(ratio_ready, h + 1)
                nc.scalar.activation(PT[:, 0:T], PT[:, 0:T], ACT.Sqrt, scale=2.0).then_inc(root_done, 1)

            def softmax(h):
                act.wait_ge(nm_ready, h + 1)
                for t in range(TT):
                    bank, c = S_AT[t]
                    n = (t + 1) * P
                    ins = nc.scalar.activation(PR[:, P_AT[t]:P_AT[t] + n], PS[:, bank, c:c + n], ACT.Exp,
                                               scale=SCALE, bias=NMS[:, t:t + 1], accum_out=SUMS[:, t:t + 1])
                ins.then_inc(exp_done, 1)
                for n, (c0, c1, bank) in enumerate(((0, 512, 4), (512, 896, 5), (896, 1280, 6))):
                    act.wait_ge(pt_ps, 3 * h + n + 1)
                    nc.scalar.activation(PT[:, c0:c1], PS[:, bank, 0:c1 - c0], ACT.Copy).then_inc(pt_ready, 1)
                act.wait_ge(att_ps, h + 1)
                nc.scalar.activation(A[:, one(h), 0:SEQ].rearrange("p a t -> p (a t)"), PS[:, 4, :], ACT.Copy)\
                    .then_inc(att_ready, 1)

            def rows_out(full, dst, samples, i):
                nc.scalar.activation(dst[:, 0:HT], PS[:, 2 * full, 0:HT], ACT.Copy)
                nc.scalar.activation(dst[:, HT:SEQ], PS[:, 2 * full + 1, 0:HB], ACT.Copy)
                nc.scalar.activation(samples[:, one(i), :].rearrange("p a b -> p (a b)"), PS[:, 2 * full + 1, HB:HT], ACT.Copy)\
                    .then_inc(tile_out[full], 1)

            def step(i, head, prev):
                if head:
                    split_hi(U_L + 1, 2 * i)
                if prev:
                    gates(i - 1)
                if head:
                    act.wait_ge(qb_ps, i + 1)
                    if prev:
                        act.wait_ge(k_scored, NPG * i)
                    nc.scalar.activation(QB[:, :].rearrange("p (a n) -> p a n", a=2), PS[:, 4:6, :], ACT.Copy,
                                         scale=SCALE).then_inc(qb_ready, 1)
                    slot = tile_wait(U_L, 2 * i)
                    if prev:
                        act.wait_ge(s_done, i)
                    rows_out(slot, kT, KS, i)
                    split_hi(U_L + 2, 2 * i)
                if prev:
                    softmax(i - 1)
                if head:
                    rows_out(tile_wait(U_L + 1, 2 * i), vT, VS, i)
                    split_hi(U_L + 3, 2 * i)
                    slot = tile_wait(U_L + 2, 2 * i)
                    if prev:
                        act.wait_ge(lru_done, i)
                    W3 = CW - 1
                    nc.scalar.activation(XW[:, W3:W3 + HT], PS[:, 2 * slot, 0:HT], ACT.Copy)
                    nc.scalar.activation(XW[:, W3 + HT:W3 + SEQ], PS[:, 2 * slot + 1, 0:HB], ACT.Copy)
                    nc.scalar.activation(XW[:, W3 + SEQ:].rearrange("p (b j) -> p b j", j=CW)[:, :, W3],
                                         PS[:, 2 * slot + 1, HB:HT], ACT.Copy).then_inc(tile_out[slot], 1)
                    for tr, tok, ready, stored, bank, dst in ((ktr_ps, ktok, ktok_ready, k_out, 5, new_k_p),
                                                              (vtr_ps, vtok, vtok_ready, v_out, 6, new_v_p)):
                        act.wait_ge(tr, i + 1)
                        if prev:
                            act.wait_ge(stored, 16 * i)
                        nc.scalar.activation(tok[:, :, :], PS[:, bank, :].rearrange("p (j d) -> p j d", j=TT), ACT.Copy)\
                            .then_inc(ready, 1)
                        act.wait_ge(ready, i + 1)
                        act.dma_start(dst[0, 0, :, one(i), :].rearrange("(j p) a d -> p j (a d)", p=P), tok[:, :, :])\
                            .then_inc(stored, 16)
                    split_hi(U_L + 4, 2 * i)
                    slot = tile_wait(U_L + 3, 2 * i)
                    if prev:
                        act.wait_ge(lru_done, i)
                    nc.scalar.activation(PT[:, T:2 * T].rearrange("p (a t) -> p a t", a=2), pair_view(slot),
                                         ACT.Gelu_apprx_tanh).then_inc(tile_out[slot], 1)
                if prev:
                    act.wait_ge(v_used, NPG * i)
                    nc.scalar.activation(PVS[:, :, one(i - 1)].rearrange("p h a -> p (h a)"), PS[:, 7, 0:NH], ACT.Copy)\
                        .then_inc(pvs_ready, 1)
                if head:
                    act.wait_ge(shifted, i + 1)
                    nc.scalar.activation(PP[:, :, :], SC[:, :, :], ACT.Exp).then_inc(pp_ready, 1)

            step(0, True, False)
            with act.Fori(1, NH) as i:
                step(i, True, True)
            step(NH, False, True)

            act.wait_ge(merge_sub, 1)
            nc.scalar.activation(merge_e[:, :], merge_e[:, :], ACT.Exp).then_inc(merge_exp, 1)
            act.wait_ge(tail_t, 1)
            nc.scalar.activation(KR[0:NB, 0, :].rearrange("p (a n) -> p a n", a=2), PS[0:NB, 4:6, :], ACT.Copy)
            nc.scalar.activation(VR[0:NB, 0, :].rearrange("p (a n) -> p a n", a=2), PS[0:NB, 6:8, :], ACT.Copy)\
                .then_inc(tail_ready, 1)
            norm(1, nbuf1, False, False, [(0, NH), (NH, KD)], [(merged, 1), (att_ready, NH), (lru_done, NL), (tail_out, 7 * 16),
                  (k_out, 16 * NH), (v_out, 16 * NH), (logf_out, 2 * 16)])
            with act.Fori(0, KD // 2) as j:
                for s in range(2):
                    split_hi(U_O + 1 + s, j)
            norm(2, nbuf1, False, False, [(0, KD)], out_of_banks(U_F))

            def up(c, j):
                for s in range(2):
                    split_hi(U_F + 1 + s, c * (UC // 2) + j, TC * c + 2 * j + (U_F + s))
                    slot = tile_wait(U_F + s, c * (TC // 2) + j)
                    nc.scalar.activation(RT[:, :].rearrange("p (a t) -> p a t", a=2), pair_view(slot), ACT.Relu)\
                        .then_inc(tile_out[slot], 1)
                    act.drain()
                    act.wait_ge(sq_h_ready, CH * c + 2 * j + s)
                    nc.scalar.activation(HF[:, :], RT[:, :], ACT.Square)
                    act.drain()
                    nc.scalar.activation(HH[:, one(2 * j + s), :].rearrange("p a t -> p (a t)"), HF[:, :], ACT.Copy)\
                        .then_inc(h_ready, 1)

            with act.Fori(0, NC - 1) as c:
                with act.Fori(0, CH // 2) as j:
                    up(c, j)
                with act.Fori(0, CH // 2) as j:
                    for s in range(2):
                        split_hi(U_F + CH + 1 + s, c * (UC // 2) + j, TC * c + 4 * j + (U_F + CH + 2 * s))
            with act.Fori(0, CH // 2) as j:
                up(NC - 1, j)
            for n in range(CH - 1):
                split_hi(U_F + CH + 1 + n, (NC - 1) * (UC // 2), TC * (NC - 1) + U_F + CH + 2 * n)
            norm(3, nbuf1, False, True, [(0, KD)], out_of_banks(U_F + NC * TC))
            for k in range(0, KD, 2):
                act.wait_ge(y_t, k + 1)
                nc.scalar.activation(YT[:, :, k * P:(k + 1) * P], PS[:, 4, :].rearrange("p (j f) -> p j f", j=TT), ACT.Copy)\
                    .then_inc(yt_ready[0], 1)
                if k % 4 == 2:
                    g = k // 4
                    act.wait_ge(ys_t, g + 1)
                    nc.scalar.activation(YS[:, g * 512:(g + 1) * 512], PS[0:NB, 6 + g % 2, :], ACT.Copy).then_inc(ys_ready, 1)

        @block.vector
        def _(dve):
            V = nc.vector

            def split_lo(n, half):
                slot, w = at(n, half)
                dve.wait_ge(hi_done, 2 * w + slot + 1)
                V.tensor_tensor(WL[slot][:, :], RAW[:, slot, :], WH[slot][:, :].bitcast(F32), ALU.subtract)\
                    .then_inc(lo_done, 1)

            def tile_wait(n, half):
                slot, w = at(n, half)
                dve.wait_ge(tile_done, 2 * w + slot + 1)
                return slot

            def norm(n, bufs, groups, col):
                SQ, XN, RS = bufs
                for g, (k0, k1) in enumerate(groups):
                    dve.wait_ge(root_ready, n + g + (n > 1) + 1)
                    V.reciprocal(RS[:, g, :], RS[:, g, :])
                dve.drain()
                for g, (k0, k1) in enumerate(groups):
                    with dve.Fori(k0 // 2, k1 // 2) as j:
                        dve.wait_ge(xl_ready, KD * n + 2 * j)
                        for s in range(2):
                            k = 2 * j + s
                            V.scalar_tensor_tensor(XN[:, s, :], A[:, one(k), :].rearrange("p a t -> p (a t)"),
                                                   PRM[:, one(col + k)], RS[:, g, :], ALU.mult, ALU.mult).then_inc(xn_ready, 1)
                        for s in range(2):
                            k = 2 * j + s
                            dve.wait_ge(xh_ready, KD * n + k + 1)
                            V.tensor_tensor(XL[:, one(k), :].rearrange("p a t -> p (a t)"), XN[:, s, :],
                                            XH[:, one(k), :].rearrange("p a t -> p (a t)").bitcast(F32), ALU.subtract)\
                                .then_inc(xl_ready, 1)

            for k in range(1, KD, 2):
                dve.wait_ge(x_t, k + 1)
                V.tensor_copy(A[:, k, 0:SEQ], PS[:, 5, :]).then_inc(x_ready[1], 1)
            split_lo(0, 0)
            dve.wait_ge(table_ready, 1)
            norm(0, nbuf0, [(0, KD)], R_GMIX)
            split_lo(1, 0)

            V.memset(YF[:, :, :], 0.0)
            slot = tile_wait(0, 0)
            dve.wait_ge(bf_in, 16)
            V.tensor_scalar(YH[:, :].rearrange("p (a t) -> p a t", a=2), pair_view(slot)[0:NH], BF[:, 0:1], None, ALU.add)\
                .then_inc(tile_out[slot], 1)
            dve.drain()
            V.tensor_copy(YF[:, TT + 1, :], PRM[:, R_LAM:R_LAM + NL]).then_inc(yh_ready, 1)
            dve.wait_ge(logit_t, 1)
            V.tensor_copy(YF[:, 0:TT, :], PS[:, 4, 0:TT * NH].rearrange("p (j h) -> p j h", j=TT))
            V.tensor_copy(YF[0:NB, TT, :], PS[0:NB, 4, TT * NH:(TT + 1) * NH])
            dve.drain()
            V.scalar_tensor_tensor(Z0[:, :, :], YF[:, :, :], -1.0, YF[:, :, :], ALU.mult, ALU.min).then_inc(absneg_ready, 1)
            dve.wait_ge(expneg_ready, 1)
            V.tensor_scalar(Z0[:, :, :], Z1[:, :, :], 2.0, None, ALU.add)
            dve.drain()
            V.reciprocal(Z0[:, :, :], Z0[:, :, :])
            dve.drain()
            V.tensor_tensor(Z1[:, :, :], Z1[:, :, :], Z0[:, :, :], ALU.mult)
            dve.drain()
            V.tensor_tensor(Z0[:, :, :], Z1[:, :, :], Z1[:, :, :], ALU.mult)
            dve.drain()
            V.tensor_scalar(Z2[:, :, :], Z0[:, :, :], 2.0 / 17, None, ALU.mult)
            for n in range(15, 1, -2):
                dve.drain()
                V.scalar_tensor_tensor(Z2[:, :, :], Z2[:, :, :], 2.0 / n, Z0[:, :, :], ALU.add, ALU.mult)
            dve.drain()
            V.scalar_tensor_tensor(Z2[:, :, :], Z2[:, :, :], 2.0, Z1[:, :, :], ALU.add, ALU.mult)
            dve.drain()
            V.scalar_tensor_tensor(LS[:, :, :], YF[:, :, :], 0.0, Z2[:, :, :], ALU.min, ALU.subtract).then_inc(logf_ready, 1)
            dve.drain()
            V.tensor_scalar(CPOS[:, :], LS[:, TT + 1, :], -LRU_C, None, ALU.mult)
            V.tensor_scalar(CNEG[:, :], LS[:, TT + 1, :], LRU_C, None, ALU.mult).then_inc(logf_ready, 1)
            dve.wait_ge(state_t, 1)
            V.tensor_copy(H0[:, :, :], PS[:, 7, 0:NL * NB].rearrange("p (n b) -> p n b", n=NL)).then_inc(state_ready, 1)
            V.tensor_copy(CST[:, :, :], PS[:, 7, NL * NB:NL * NB * CW].rearrange("p (n r) -> p n r", n=NL))\
                .then_inc(state_ready, 1)
            dve.wait_ge(gather_in, 32)
            V.tensor_reduce(TOT[:, :], LG[:, :, :].rearrange("p k h -> p h k"), AX.X, ALU.add)
            dve.drain()
            dve.wait_ge(masks_ready, 3)
            V.tensor_tensor(MT[:, :, :], later[:, :].unsqueeze(1).to_broadcast([P, NH, P]),
                            TOT[:, :].unsqueeze(2).to_broadcast([P, NH, P]), ALU.mult).then_inc(tot_ready, 1)
            with dve.Fori(0, NH // 2) as j:
                for s in range(2):
                    split_lo(U_Q + 1 + s, j)
            dve.wait_ge(cum_ready, 3)
            V.memset(XW[:, 0:CW - 1], 0.0)

            def score(i, b):
                if b % K_Q == K_Q - 1:
                    dve.wait_ge(pool_prod, NPG // K_Q * i + b // K_Q + 1)
                else:
                    dve.wait_ge(k_full[b % 2], 16 * (NPG // 2 * i + b // 2 + 1))
                    V.tensor_tensor(KR[:, b % 2, :], KR[:, b % 2, :], QB[:, :], ALU.mult).then_inc(dve_prod, 1)
                    dve.wait_ge(dve_prod, (NPG - NPG // K_Q) * i + b - b // K_Q + 1)
                V.tensor_reduce(SC[:, :, b], KR[:, b % 2, :].rearrange("p (h d) -> p h d", h=NH), AX.X, ALU.add)\
                    .then_inc(k_scored, 1)

            def recurrence(h):
                R, I, TH, U = PR[:, 0:T], PR[:, T:2 * T], PT[:, 0:T], XW[:, CW - 1:CW - 1 + T]
                dve.wait_ge(sig_done, h + 1)
                V.tensor_tensor(I, I, XC[:, :], ALU.mult)
                dve.wait_ge(decay_done, h + 1)
                V.tensor_scalar(U, TH, 1.0, None, ALU.add)
                dve.drain()
                V.reciprocal(U, U)
                dve.drain()
                V.tensor_tensor(TH, TH, U, ALU.mult).then_inc(ratio_ready, 1)
                dve.wait_ge(root_done, h + 1)
                V.tensor_tensor(I, I, TH, ALU.mult)
                dve.drain()
                V.tensor_tensor_scan(XC[:, 0:SEQ], PR[:, 0:SEQ], PR[:, T:T + SEQ], 0.0, ALU.mult, ALU.add)
                V.tensor_tensor(XC[:, SEQ:T], PR[:, SEQ:T], H0[:, one(h), :].rearrange("p a b -> p (a b)"), ALU.mult)
                dve.drain()
                V.tensor_tensor(XC[:, SEQ:T], XC[:, SEQ:T], PR[:, T + SEQ:2 * T], ALU.add)
                dve.drain()
                dve.wait_ge(tile_out[0], at(U_L + 3, 2 * h)[1] + 1)
                V.tensor_copy(HALL[:, :, one(h)].rearrange("p r a -> p (r a)"), XC[:, SEQ - 1:T])
                V.tensor_tensor(A[:, one(NH + h), :].rearrange("p a t -> p (a t)"), XC[:, :], PT[:, T:2 * T], ALU.mult)\
                    .then_inc(lru_done, 1)

            def conv(i):
                V.tensor_copy(XW[:, CW - 1 + SEQ:].rearrange("p (b j) -> p b j", j=CW)[:, :, 0:CW - 1],
                              CST[:, one(i), :].rearrange("p a (b j) -> p (a b) j", b=NB))
                dve.drain()
                dve.wait_ge(tile_out[1], at(U_L + 2, 2 * i)[1] + 1)
                tails = XW[:, CW - 1 + SEQ:].rearrange("p (b j) -> p b j", j=CW)
                for j in range(CW):
                    w = PRM[:, one(R_CONV + j * NL + i)]
                    for dst, src in ((XC[:, 0:SEQ], XW[:, j:j + SEQ]), (XC[:, SEQ:T], tails[:, :, j])):
                        if j == 0:
                            V.tensor_scalar(dst, src, w, PRM[:, one(R_BCONV + i)], ALU.mult, ALU.add)
                        else:
                            ins = V.scalar_tensor_tensor(dst, src, w, dst, ALU.mult, ALU.add)
                    dve.drain()
                V.tensor_copy(CVALL[:, 0:CW - 1, one(i)].rearrange("p r a -> p (r a)"), XW[:, SEQ:SEQ + CW - 1])
                V.tensor_copy(CVALL[:, CW - 1:, one(i)].rearrange("p (b j) a -> p b (j a)", b=NB), tails[:, :, 1:CW])\
                    .then_inc(conv_done, 1)

            def step(i, head, prev):
                h = i - 1
                if head:
                    split_lo(U_L + 1, 2 * i)
                    if not prev:
                        for s, v in out_of_banks(U_L):
                            dve.wait_ge(s, v)
                    V.tensor_tensor(DQ[:, :].rearrange("p (h d) -> p h d", h=NH), ident[:, :].unsqueeze(1).to_broadcast([P, NH, P]),
                                    A[:, 0:NH, SEQ + i:SEQ + i + 1].to_broadcast([P, NH, P]) if isinstance(i, int) else
                                    A[:, 0:NH, one(SEQ + i)].to_broadcast([P, NH, P]), ALU.mult).then_inc(diag_ready, 1)
                if prev:
                    recurrence(h)
                    V.tensor_tensor(PT[:, 0:SEQ].rearrange("p (j k) -> p j k", j=TT), ident[:, :].unsqueeze(1).to_broadcast([P, TT, P]),
                                    FT[:, :, one(h)].to_broadcast([P, TT, P]), ALU.mult)
                    V.tensor_copy(qcur[:, :], A[:, one(h), 0:SEQ].rearrange("p a t -> p (a t)")).then_inc(qdf_ready, 1)
                    dve.wait_ge(pp_ready, i)
                    V.tensor_reduce(DEN[:, :, one(h)].rearrange("p h a -> p (h a)"), PP[:, :, :], AX.X, ALU.add)
                if head:
                    dve.wait_ge(qb_ready, i + 1)
                    for b in range(K_Q):
                        score(i, b)
                    split_lo(U_L + 2, 2 * i)
                if prev:
                    dve.wait_ge(s_done, h + 1)
                    for t in range(TT):
                        bank, c = S_AT[t]
                        V.tensor_reduce(NM[:, t:t + 1], PS[:, bank, c:c + (t + 1) * P], AX.X, ALU.max, negate=True)
                    dve.drain()
                    V.tensor_scalar(NMS[:, :], NM[:, :], SCALE, None, ALU.mult).then_inc(nm_ready, 1)
                if head:
                    for b in range(K_Q, K_Q + K_Q // 2):
                        score(i, b)
                if prev:
                    dve.wait_ge(exp_done, h + 1)
                    V.reciprocal(RSUM[:, :], SUMS[:, :])
                    dve.drain()
                    for t in range(TT):
                        row = PR[:, P_AT[t]:P_AT[t] + (t + 1) * P]
                        ins = V.tensor_scalar(row, row, RSUM[:, t:t + 1], None, ALU.mult)
                    ins.then_inc(p_norm, 1)
                if head:
                    for b in range(K_Q + K_Q // 2, 2 * K_Q):
                        score(i, b)
                    split_lo(U_L + 3, 2 * i)
                    for b in range(2 * K_Q, 3 * K_Q):
                        score(i, b)
                    split_lo(U_L + 4, 2 * i)
                    conv(i)
                    for b in range(3 * K_Q, NPG):
                        score(i, b)
                    dve.drain()
                    V.tensor_tensor(SC[:, :, :], SC[:, :, :], SUF[:, :, one(i), :].rearrange("p h a n -> p h (a n)"), ALU.add)
                    dve.drain()
                    V.tensor_reduce(M8[:, :], SC[:, :, :], AX.X, ALU.max).then_inc(m8_ready, 1)
                    dve.wait_ge(mall_ready, i + 1)
                    V.tensor_copy(MX[:, :, one(i)].rearrange("p h a -> p (h a)"), MALL[:, :])
                    V.tensor_tensor(SC[:, :, :], SC[:, :, :], MALL[:, :].unsqueeze(2).to_broadcast([P, NH, NPG]), ALU.subtract)\
                        .then_inc(shifted, 1)

            step(0, True, False)
            with dve.Fori(1, NH) as i:
                step(i, True, True)
            step(NH, False, True)

            prod, lfd, SN, DR, MM = mrg[0:5]
            E1, E2 = mrg[5:7]
            tmp = mrg[7]
            q_s = A[:, 0:NH, SEQ:T]
            dve.wait_ge(s_done, NH)
            V.tensor_tensor(prod, q_s, KS[:, :, :], ALU.mult)
            V.tensor_tensor(lfd[0:NB], LS[0:NB, TT, :].unsqueeze(2).to_broadcast([NB, NH, NB]),
                            ident[0:NB, 0:NB].unsqueeze(1).to_broadcast([NB, NH, NB]), ALU.mult)
            dve.drain()
            V.tensor_scalar(lfd[0:NB], lfd[0:NB], -1.0 / SCALE, None, ALU.mult).then_inc(merge_in, 1)
            dve.wait_ge(merge_ps, 1)
            V.tensor_scalar(SN, PS[:, 5, 0:NH * NB].rearrange("p (h b) -> p h b", h=NH), SCALE, None, ALU.mult)
            V.tensor_copy(DR, PS[:, 6, 0:NH * NB].rearrange("p (h b) -> p h b", h=NH)).then_inc(merge_in, 1)
            dve.drain()
            V.tensor_tensor(MM, MX[:, :, :], SN, ALU.max)
            dve.drain()
            V.tensor_tensor(E1, MX[:, :, :], MM, ALU.subtract)
            V.tensor_tensor(E2, SN, MM, ALU.subtract).then_inc(merge_sub, 1)
            dve.wait_ge(merge_exp, 1)
            dve.wait_ge(pvs_ready, NB)
            V.tensor_tensor(DR, DR, E1, ALU.mult)
            V.tensor_tensor(prod, PVS[:, :, :], E1, ALU.mult)
            V.tensor_tensor(tmp, VS[:, :, :], E2, ALU.mult)
            dve.drain()
            V.tensor_tensor(DR, DR, E2, ALU.add)
            V.tensor_tensor(prod, prod, tmp, ALU.add)
            dve.drain()
            V.reciprocal(DR, DR)
            dve.drain()
            V.tensor_tensor(q_s, prod, DR, ALU.mult).then_inc(merged, 1)
            hr = (CW - 1) * NL * (NB + 1) // 2
            dve.wait_ge(tail_t, 1)
            V.tensor_copy(KR[0:NL * (NB + 1), 1, 0:P], PS[0:NL * (NB + 1), 2, 0:P])
            V.tensor_copy(KR[0:hr, 1, P:3 * P], PS[0:hr, 3, 0:2 * P]).then_inc(tail_rows, 1)

            norm(1, nbuf1, [(0, NH), (NH, KD)], R_GATT)
            dve.wait_ge(respilled, 16)
            with dve.Fori(0, KD // 2) as j:
                for s in range(2):
                    split_lo(U_O + 1 + s, j)
                    slot = tile_wait(U_O + s, j)
                    a = A[:, one(2 * j + s), :].rearrange("p a (c t) -> p (a c) t", c=2)
                    V.tensor_tensor(a, pair_view(slot), a, ALU.add).then_inc(tile_out[slot], 1)
            norm(2, nbuf1, [(0, KD)], R_GFFN)

            def up(c, j):
                for s in range(2):
                    split_lo(U_F + 1 + s, c * (UC // 2) + j)
                    dve.wait_ge(h_ready, CH * c + 2 * j + s + 1)
                    V.tensor_tensor(HL[:, one(2 * j + s), :].rearrange("p a t -> p (a t)"), HF[:, :],
                                    HH[:, one(2 * j + s), :].rearrange("p a t -> p (a t)").bitcast(F32), ALU.subtract)\
                        .then_inc(sq_h_ready, 1)

            def down(c, j, units, split):
                for s in units:
                    if split(s):
                        split_lo(U_F + CH + 1 + s, c * (UC // 2) + j)
                    for m in range(2):
                        slot = tile_wait(U_F + CH + 2 * s + m, c * (TC // 2) + 2 * j)
                        a = A[:, one(4 * j + 2 * s + m), :].rearrange("p a (c t) -> p (a c) t", c=2)
                        V.tensor_tensor(a, pair_view(slot), a, ALU.add).then_inc(tile_out[slot], 1)

            with dve.Fori(0, NC - 1) as c:
                with dve.Fori(0, CH // 2) as j:
                    up(c, j)
                with dve.Fori(0, CH // 2) as j:
                    down(c, j, range(2), lambda s: True)
            with dve.Fori(0, CH // 2) as j:
                up(NC - 1, j)
            with dve.Fori(0, CH // 2 - 1) as j:
                down(NC - 1, j, range(2), lambda s: True)
            down(NC - 1, CH // 2 - 1, range(2), lambda s: s == 0)

            SQ, XN, RS = nbuf1
            dve.wait_ge(root_ready, 5)
            V.reciprocal(RS[:, 0, :], RS[:, 0, :])
            dve.drain()
            for k in range(KD + 2):
                if k < KD:
                    if k >= 2:
                        dve.wait_ge(y_t, k - 1)
                    V.scalar_tensor_tensor(XN[:, k % 2, :], A[:, k, :], PRM[:, R_GFIN + k:R_GFIN + k + 1], RS[:, 0, :],
                                           ALU.mult, ALU.mult).then_inc(yn_ready, 1)
                m = k - 2
                if m >= 0 and m % 2:
                    dve.wait_ge(y_t, m + 1)
                    V.tensor_copy(YT[:, :, m * P:(m + 1) * P], PS[:, 5, :].rearrange("p (j f) -> p j f", j=TT))\
                        .then_inc(yt_ready[1], 1)

        @block.tensor
        def _(pe):
            mm = nc.tensor.matmul

            def quarters(xh, xl, wh, wl, dsts, kts, first, last, insert=None):
                for n, k in enumerate(kts):
                    ends = dict(start=n == 0 and first, stop=False)
                    for c in range(2):
                        t = slice(c * HT, (c + 1) * HT)
                        mm(dsts[c], wh(n), xh[:, k, t], **ends)
                    for c in range(2):
                        t = slice(c * HT, (c + 1) * HT)
                        mm(dsts[c], wh(n), xl[:, k, t], start=False, stop=False)
                    for c in range(2):
                        t = slice(c * HT, (c + 1) * HT)
                        ins = mm(dsts[c], wl(n), xh[:, k, t], start=False, stop=last and n == len(kts) - 1)
                    if insert and n % 4 == 3:
                        insert[n // 4]()
                return ins

            def unit(n, half, tile, tile_half, insert=None):
                slot, w = at(n, half)
                pair, tw = at(tile, tile_half)
                pe.wait_ge(lo_done, 2 * w + slot + 1)
                if not (isinstance(tw, int) and tw == 0):
                    pe.wait_ge(tile_out[pair], tw)
                ins = quarters(XH, XL, lambda k: WH[slot][:, k * P:(k + 1) * P], lambda k: WL[slot][:, k * P:(k + 1) * P],
                               [PS[:, 2 * pair + c, 0:HT] for c in range(2)], range(KD), True, True, insert[:-1] + [lambda: None] if insert else None)
                ins.then_inc(tile_done, 1)
                if insert:
                    insert[-1]()
                return pair

            def norm_sums(n, bufs, groups):
                SQ = bufs[0]
                for g, (k0, k1) in enumerate(groups):
                    for k in range(k0, k1):
                        pe.wait_ge(sq_ready, KD * n + k + 1)
                        for c in range(2):
                            ins = mm(PS[:, 4 + 2 * g + c, 0:HT], ones[:, :], SQ[:, k % 2, c * HT:(c + 1) * HT],
                                     start=k == k0, stop=k == k1 - 1)
                        ins.then_inc(sq_used, 1)
                        if k == k1 - 1:
                            pe.wait_ge(sq_used, KD * n + k + 1)
                            pe.sem_inc(ss_done, 1)

            tr = nc.tensor.transpose
            pe.wait_ge(consts_ready, 5)
            pe.wait_ge(table_in, 16 * 10)
            tr(PS[:, 7, 0:P], PRW[:, :], ident[:, :]).then_inc(table_t, 1)
            pe.wait_ge(x_in, 16 * (TT + 1))
            for k in range(KD):
                if k >= 2:
                    pe.wait_ge(x_ready[k % 2], k // 2)
                for j in range(TT):
                    ins = tr(PS[:, 4 + k % 2, j * P:(j + 1) * P], XT[:, j, k * P:(k + 1) * P], ident[:, :])
                ins.then_inc(x_t, 1)
            for k in range(KD):
                ins = tr(PS[:, 6, k * NB:(k + 1) * NB], XS[:, k * P:(k + 1) * P], ident[0:NB, 0:NB])
            ins.then_inc(x_t, 1)
            pe.wait_ge(x_ready[0], KD // 2)
            pe.wait_ge(x_ready[1], KD // 2)
            norm_sums(0, nbuf0, [(0, KD)])
            pe.wait_ge(xl_ready, KD)
            unit(0, 0, 0, 0)
            pe.wait_ge(setup_in, 32)
            for n in range(NL):
                tr(PS[:, 7, n * NB:(n + 1) * NB], SHW[:, n * P:(n + 1) * P], ident[0:NB, 0:NB])
            r = NB * (CW - 1)
            for n in range(NL):
                ins = tr(PS[:, 7, NL * NB + n * r:NL * NB + (n + 1) * r], SCW[:, n * P:(n + 1) * P], ident[0:r, 0:r])
            ins.then_inc(state_t, 1)
            pe.wait_ge(yh_ready, 1)
            pe.wait_ge(root_ready, 1)
            for j in range(TT):
                tr(PS[:, 4, j * NH:(j + 1) * NH], YH[:, j * P:(j + 1) * P], ident[0:NH, 0:NH])
            tr(PS[0:NB, 4, TT * NH:(TT + 1) * NH], YH[:, SEQ:T], ident[0:NH, 0:NH]).then_inc(logit_t, 1)
            with pe.Fori(0, NH // 2) as j:
                for s in range(2):
                    unit(U_Q + s, j, U_Q + s, j)
            pe.wait_ge(gather_in, 32)
            pe.wait_ge(absneg_ready, 1)
            for h in range(NH):
                ins = tr(PS[:, 4 + h // 4, (h % 4) * P:(h % 4 + 1) * P], LG[:, :, h], ident[:, :])
                if h % 4 == 3:
                    ins.then_inc(past_t, 1)
            pe.wait_ge(logf_ready, 1)
            pe.wait_ge(masks_ready, 3)
            cum = PS[:, 6, 0:TT * NH].rearrange("p (j h) -> p j h", j=TT)
            mm(cum, tri[:, :], LS[:, 0:TT, :], start=True, stop=False)
            for j in range(TT - 1):
                n = TT - 1 - j
                ins = mm(cum[:, j + 1:, :], ones[:, :], LS[:, j:j + 1, :].to_broadcast([P, n, NH]), start=False, stop=j == TT - 2)
            ins.then_inc(cum_ps, 1)
            pe.wait_ge(tot_ready, 1)
            for g in range(2):
                pe.wait_ge(past_ready, g + 1)
                mm(PS[:, 4 + g, :], low[:, :], LT[:, 4 * g:4 * g + 4, :].rearrange("p h n -> p (h n)"), start=True, stop=False)
                mm(PS[:, 4 + g, :], ones[:, :], MT[:, 4 * g:4 * g + 4, :].rearrange("p h n -> p (h n)"), start=False, stop=True)\
                    .then_inc(suf_ps, 1)

            def values(h, b):
                if b == 0:
                    pe.wait_ge(pp_ready, h + 1)
                    pe.wait_ge(pvs_ready, h)
                pe.wait_ge(v_full[b % 2], 16 * (NPG // 2 * h + b // 2 + 1))
                for n in range(NH):
                    ins = mm(PS[:, 7, n:n + 1], VR[:, b % 2, n * HD:(n + 1) * HD], PP[:, n, b:b + 1],
                             start=b == 0 and n == 0, stop=b == NPG - 1, skip_group_check=True)
                ins.then_inc(v_used, 1)

            def scores(h):
                pe.wait_ge(qdf_ready, h + 1)
                for t in range(TT):
                    bank, c = S_AT[t]
                    n = (t + 1) * P
                    dst = PS[:, bank, c:c + n]
                    mm(dst, qcur[:, t * P:(t + 1) * P], kT[:, 0:n], start=True, stop=False)
                    mm(dst, ones[:, :], PT[:, 0:n], start=False, stop=False)
                    ins = mm(dst[:, n - P:n], ident[:, :], maskneg[:, :], start=False, stop=True)
                ins.then_inc(s_done, 1)

            def attend(h):
                pe.wait_ge(p_norm, h + 1)
                for j in range(TT):
                    bank, c = PT_BANK[j]
                    for t in range(j, TT):
                        ins = tr(PS[:, bank, c + (t - j) * P:c + (t - j + 1) * P],
                                 PR[:, P_AT[t] + j * P:P_AT[t] + (j + 1) * P], ident[:, :])
                    if j != 2:
                        ins.then_inc(pt_ps, 1)
                pe.wait_ge(vtok_ready, h + 1)
                for j in range(TT):
                    pe.wait_ge(pt_ready, 3 * h + min(j + 1, 3))
                    ins = mm(PS[:, 4, j * P:SEQ], vtok[:, j, :], PT[:, PT_AT[j]:PT_AT[j] + (TT - j) * P],
                             start=j == 0, stop=j == TT - 1)
                ins.then_inc(att_ps, 1)

            def step(i, head, prev):
                def queries():
                    pe.wait_ge(diag_ready, i + 1)
                    if prev:
                        pe.wait_ge(sig_done, i)
                    for g in range(2):
                        ins = mm(PS[:, 4 + g, :], ones[:, :], DQ[:, g * 512:(g + 1) * 512], start=True, stop=True)
                    ins.then_inc(qb_ps, 1)

                def pages(q):
                    def page_of(b):
                        def go():
                            if q == 0 and b == 0 and head:
                                queries()
                            if prev:
                                values(i - 1, K_Q * q + b)
                        return go
                    return [page_of(b) for b in range(4)]

                def quarter(q):
                    ins = pages(q)
                    if head:
                        unit(U_L + q, 2 * i, U_L + q, 2 * i, ins)
                    else:
                        for f in ins:
                            f()

                quarter(0)
                if prev:
                    if head:
                        pe.wait_ge(qb_ready, i + 1)
                    scores(i - 1)
                quarter(1)
                if prev:
                    attend(i - 1)
                quarter(2)
                if head:
                    pe.wait_ge(tile_out[1], at(U_L, 2 * i)[1] + 1)
                    for j in range(TT):
                        ins = tr(PS[:, 5, j * P:(j + 1) * P], kT[:, j * P:(j + 1) * P], ident[:, :])
                    ins.then_inc(ktr_ps, 1)
                    pe.wait_ge(tile_out[0], at(U_L + 1, 2 * i)[1] + 1)
                    for j in range(TT):
                        ins = tr(PS[:, 6, j * P:(j + 1) * P], vT[:, j * P:(j + 1) * P], ident[:, :])
                    ins.then_inc(vtr_ps, 1)
                quarter(3)
                if head:
                    pe.wait_ge(gw_full, 32 * (i + 1))
                    pe.wait_ge(conv_done, i + 1)
                    if prev:
                        pe.wait_ge(att_ready, i)
                    pe.wait_ge(ktok_ready, i + 1)
                    pe.wait_ge(vtok_ready, i + 1)
                    for g in range(2):
                        mm(PS[:, 4 + g, :], GW[:, g, :], XC[:, 0:SEQ], start=True, stop=True)
                    for g in range(2):
                        ins = mm(PS[:, 6, g * NB:(g + 1) * NB], GW[:, g, :], XC[:, SEQ:T], start=True, stop=True)
                    ins.then_inc(gates_ps, 1)

            pe.wait_ge(cum_ready, 3)
            step(0, True, False)
            with pe.Fori(1, NH) as i:
                step(i, True, True)
            step(NH, False, True)

            pe.wait_ge(merge_in, 1)
            new_s = PS[:, 5, 0:NH * NB]
            mm(new_s, ones[:, :], qcur[:, 0:64], start=True, stop=False)
            mm(new_s, ones[0:NB, :], qcur[0:NB, 64:128], start=False, stop=True)
            mm(PS[:, 6, 0:NH * NB], ones[:, :], DEN[:, :, :].rearrange("p h b -> p (h b)"), start=True, stop=True)\
                .then_inc(merge_ps, 1)
            pe.wait_ge(merge_in, 2)
            pe.wait_ge(pvs_ready, NB)
            pe.wait_ge(att_ready, NH)
            pe.wait_ge(lru_done, NL)
            for src, b0 in ((KS, 4), (VS, 6)):
                for h in range(NH):
                    tr(PS[0:NB, b0 + h // 4, (h % 4) * P:(h % 4 + 1) * P], src[:, h, :], ident[:, :])
            hr = (CW - 1) * NL * (NB + 1) // 2
            cv = CVALL[:, :, :].rearrange("p r n -> p (r n)")
            tr(PS[0:NL * (NB + 1), 2, 0:P], HALL[:, :, :].rearrange("p r n -> p (r n)"), ident[:, :])
            for g in range(2):
                ins = tr(PS[0:hr, 3, g * P:(g + 1) * P], cv[:, g * hr:(g + 1) * hr], ident[:, :])
            ins.then_inc(tail_t, 1)
            pe.wait_ge(tail_ready, 1)
            norm_sums(1, nbuf1, [(0, NH), (NH, KD)])
            pe.wait_ge(tail_rows, 1)
            pe.wait_ge(xl_ready, 2 * KD)
            with pe.Fori(0, KD // 2) as j:
                for s in range(2):
                    unit(U_O + s, j, U_O + s, j)
            norm_sums(2, nbuf1, [(0, KD)])
            pe.wait_ge(xl_ready, 3 * KD)
            with pe.Fori(0, NC) as c:
                with pe.Fori(0, CH // 2) as j:
                    for s in range(2):
                        unit(U_F + s, c * (UC // 2) + j, U_F + s, c * (TC // 2) + j)
                with pe.Fori(0, CH // 2) as j:
                    for s in range(2):
                        slot, w = at(U_F + CH + s, c * (UC // 2) + j)
                        pe.wait_ge(lo_done, 2 * w + slot + 1)
                        pe.wait_ge(sq_h_ready, CH * (c + 1))
                        for m in range(2):
                            pair, tw = at(U_F + CH + 2 * s + m, c * (TC // 2) + 2 * j)
                            pe.wait_ge(tile_out[pair], tw)
                            ins = quarters(HH, HL, lambda k: WH[slot][:, (2 * k + m) * P:(2 * k + m + 1) * P],
                                           lambda k: WL[slot][:, (2 * k + m) * P:(2 * k + m + 1) * P],
                                           [PS[:, 2 * pair + c2, 0:HT] for c2 in range(2)], range(CH), True, True)
                            ins.then_inc(tile_done, 1)
            norm_sums(3, nbuf1, [(0, KD)])
            XN = nbuf1[1]
            for k in range(KD):
                pe.wait_ge(yn_ready, k + 1)
                if k >= 2:
                    pe.wait_ge(yt_ready[k % 2], k // 2)
                else:
                    pe.wait_ge(root_ready, 5)
                g = k // 4
                if k % 4 == 0 and g >= 2:
                    pe.wait_ge(ys_ready, g - 1)
                ins = tr(PS[0:NB, 6 + g % 2, (k % 4) * P:(k % 4 + 1) * P], XN[:, k % 2, SEQ:T], ident[:, :])
                if k % 4 == 3:
                    ins.then_inc(ys_t, 1)
                for j in range(TT):
                    ins = tr(PS[:, 4 + k % 2, j * P:(j + 1) * P], XN[:, k % 2, j * P:(j + 1) * P], ident[:, :])
                ins.then_inc(y_t, 1)


_INS = ['x_prompt', 'x_sample', 'cache_k', 'cache_v', 'cache_logf', 'state_conv', 'state_h', 'page_table',
        'g_mix', 'w_in', 'b_f', 'w_conv', 'b_conv', 'w_gate_a', 'b_gate_a', 'w_gate_x', 'b_gate_x', 'lru_lambda',
        'g_att_out', 'g_lru_out', 'w_out', 'g_ffn', 'w_up', 'w_down', 'g_final']


def kernel(**inputs):
    import numpy as np
    import concourse.bacc as bacc
    from concourse.bass_utils import run_bass_kernel_spmd

    a = {n: np.ascontiguousarray(inputs[n]) for n in _INS}
    B, S, D = a['x_prompt'].shape
    NB, S1 = a['x_sample'].shape[:2]
    L, _, _, H, HD = a['cache_k'].shape
    CW1, DL = a['state_conv'].shape[2:]
    outs = [(B, S, D), (NB, S1, D),
            (L, B, S, H, HD), (L, B, S, H, HD), (L, B, S, H), (L, B, CW1, DL), (L, B, DL),
            (L, NB, S1, H, HD), (L, NB, S1, H, HD), (L, NB, S1, H), (L, NB, CW1, DL), (L, NB, DL)]
    nc = bacc.Bacc("TRN2", target_bir_lowering=False, num_devices=1)
    args = [nc.dram_tensor(f"in_{n}", a[n].shape, mybir.dt.from_np(a[n].dtype), kind="ExternalInput").ap() for n in _INS]
    args += [nc.dram_tensor(f"out_{i}", s, F32, kind="ExternalOutput").ap() for i, s in enumerate(outs)]
    hymba_step(nc, *args)
    r = run_bass_kernel_spmd(nc, [{f"in_{n}": a[n] for n in _INS}], core_ids=[0])
    return tuple(r.results[0][f"out_{i}"] for i in range(len(outs)))
```

```python
from contextlib import ExitStack

import concourse.bass as bass
from concourse import mybir

F32 = mybir.dt.float32
F32R = mybir.dt.float32r
I32 = mybir.dt.int32
U32 = mybir.dt.uint32
ALU = mybir.AluOpType
ACT = mybir.ActivationFunctionType
AX = mybir.AxisListType
RED = bass.bass_isa.ReduceOp

P = 128
EPS = 1e-6
NEG = -1e30
LRU_C = 8.0


def hymba_step(nc, x_prompt, x_sample, cache_k, cache_v, cache_logf, state_conv, state_h, page_table,
               g_mix, w_in, b_f, w_conv, b_conv, w_gate_a, b_gate_a, w_gate_x, b_gate_x, lru_lambda,
               g_att_out, g_lru_out, w_out, g_ffn, w_up, w_down, g_final,
               y_prompt, y_sample, new_k_p, new_v_p, new_f_p, new_conv_p, new_h_p,
               new_k_s, new_v_s, new_f_s, new_conv_s, new_h_s):
    SEQ, D = x_prompt.shape[1], x_prompt.shape[2]
    NB = x_sample.shape[0]
    T = SEQ + NB
    HT = T // 2
    HB = SEQ - HT
    KD = D // P
    NH, HD = cache_k.shape[3], cache_k.shape[4]
    DA = NH * HD
    NL = (D - DA) // P
    NPG = page_table.shape[1]
    FF = w_up.shape[2]
    CW = w_conv.shape[1]
    TT = SEQ // P
    SCALE = float(HD) ** -0.5
    CH = 8
    NC = FF // P // CH
    NKS, NVS = 4, 4
    NHH = NH // 2
    assert HD == P and NH == NL == NB == CH == 8 and KD == 16 and T % 4 == 0 and NPG % 4 == 0 and TT == 4

    w_in_v = w_in[0].rearrange("(k p) c -> p k c", p=P)
    w_out_v = w_out[0].rearrange("(k p) c -> p k c", p=P)
    w_up_v = w_up[0].rearrange("(k p) c -> p k c", p=P)
    w_down_v = w_down[0].rearrange("(g k p) c -> g p k c", p=P, k=CH)
    k_pages = cache_k[0].rearrange("g p h d -> g p (h d)")
    v_pages = cache_v[0].rearrange("g p h d -> g p (h d)")
    COL_F, COL_X, COL_G = 3 * DA, 3 * DA + NH, 3 * DA + NH + NL * P

    U_Q, U_L = 1, 1 + NH
    U_O = U_L + 4 * NH
    U_F = U_O + KD
    UC = 2 * CH
    TC = CH + 2 * CH
    N_UNITS = U_F + NC * UC

    R_CONV, R_BCONV = 0, CW * NL
    R_BA, R_BX, R_LAM = R_BCONV + NL, R_BCONV + 2 * NL, R_BCONV + 3 * NL
    R_GATT, R_GLRU = R_LAM + NL, R_LAM + 2 * NL
    R_GMIX = R_GLRU + NL
    R_GFFN, R_GFIN = R_GMIX + KD, R_GMIX + 2 * KD
    assert R_GFIN + KD == P

    xT_spill = nc.dram_tensor("xT_spill", [P, KD, T], F32, kind="Internal").ap()

    with ExitStack() as ctx:
        def sb(name, shape, dt=F32, scope=ctx):
            return scope.enter_context(nc.sbuf_tensor(name, shape, dt))

        def sem(name):
            return ctx.enter_context(nc.semaphore(name))

        PS = ctx.enter_context(nc.psum_tensor("PS", [P, 8, 512], F32))

        XH = sb("XH", [P, KD, T], F32R)
        XL = sb("XL", [P, KD, T], F32R)
        A = sb("A", [P, KD, T])
        RAW = sb("RAW", [P, 2, 2048])
        WH = [sb(f"WH{s}", [P, 2048], F32R) for s in range(2)]
        WL = [sb(f"WL{s}", [P, 2048], F32R) for s in range(2)]
        ident = sb("ident", [P, P])
        ones = sb("ones", [P, P])
        PRM = sb("PRM", [P, P])

        first_scope, mix_scope, ffn_scope, out_scope = ExitStack(), ExitStack(), ExitStack(), ExitStack()
        loop_scope = ExitStack()
        PGT = sb("PGT", [1, NB * NPG], I32, loop_scope)
        SUF = sb("SUF", [P, NH, NB, NPG], scope=loop_scope)
        maskneg = sb("maskneg", [P, P], scope=loop_scope)
        FT = sb("FT", [P, TT, NH], scope=loop_scope)
        LS = sb("LS", [P, TT + 2, NH], scope=loop_scope)
        CPOS = sb("CPOS", [P, NL], scope=loop_scope)
        CNEG = sb("CNEG", [P, NL], scope=loop_scope)
        H0 = sb("H0", [P, NL, NB], scope=loop_scope)
        CST = sb("CST", [P, NL, NB * (CW - 1)], scope=loop_scope)

        XT = sb("XT", [P, TT, D], scope=first_scope)
        XS = sb("XS", [NB, D], scope=first_scope)
        PRW = sb("PRW", [P, P], scope=first_scope)
        nbuf0 = (sb("SQ0", [P, 2, T], scope=first_scope), sb("XN0", [P, 2, T], scope=first_scope),
                 sb("RS0", [P, 1, T], scope=first_scope))
        first_scope.close()
        LG = sb("LG", [P, P, NH], scope=first_scope)
        LT = sb("LT", [P, NH, P], scope=first_scope)
        MT = sb("MT", [P, NH, P], scope=first_scope)
        SHW = sb("SHW", [NB, NL * P], scope=first_scope)
        SCW = sb("SCW", [NB * (CW - 1), NL * P], scope=first_scope)
        YH = sb("YH", [NH, T], scope=first_scope)
        IDX = sb("IDX", [P, 1], U32, first_scope)
        TOT = sb("TOT", [P, NH], scope=first_scope)
        low = sb("low", [P, P], scope=first_scope)
        tri = sb("tri", [P, P], scope=first_scope)
        later = sb("later", [P, P], scope=first_scope)
        YF = sb("YF", [P, TT + 2, NH], scope=first_scope)
        Z0, Z1, Z2 = (sb(f"Z{n}", [P, TT + 2, NH], scope=first_scope) for n in range(3))
        BF = sb("BF", [NH, 1], scope=first_scope)
        first_scope.close()

        KR = sb("KR", [P, NKS, NH * HD], scope=mix_scope)
        VR = sb("VR", [P, NVS, NHH * HD], scope=mix_scope)
        QB = sb("QB", [P, NH * HD], scope=mix_scope)
        QCOL = sb("QCOL", [P, NH], scope=mix_scope)
        GW = sb("GW", [P, 2, P], scope=mix_scope)
        qcur = sb("qcur", [P, SEQ], scope=mix_scope)
        kT = sb("kT", [P, SEQ], scope=mix_scope)
        vT = sb("vT", [P, SEQ], scope=mix_scope)
        ktok = qcur[:, :].rearrange("p (j d) -> p j d", j=TT)
        vtok = sb("vtok", [P, TT, HD], scope=mix_scope)
        PR = sb("PR", [P, 1280], scope=mix_scope)
        PT = sb("PT", [P, 1280], scope=mix_scope)
        XC = sb("XC", [P, T], scope=mix_scope)
        XW = sb("XW", [P, CW - 1 + SEQ + NB * CW], scope=mix_scope)
        SC = sb("SC", [P, NH, NPG], scope=mix_scope)
        KS = sb("KS", [P, NH, NB], scope=mix_scope)
        VS = sb("VS", [P, NH, NB], scope=mix_scope)
        MX = sb("MX", [P, NH, NB], scope=mix_scope)
        M8 = sb("M8", [P, NH], scope=mix_scope)
        MALL = sb("MALL", [P, NH], scope=mix_scope)
        DEN = sb("DEN", [P, NH, NB], scope=mix_scope)
        PVS = sb("PVS", [P, NH, NB], scope=mix_scope)
        NM = sb("NM", [P, TT], scope=mix_scope)
        NMS = sb("NMS", [P, TT], scope=mix_scope)
        SUMS = sb("SUMS", [P, TT], scope=mix_scope)
        RSUM = sb("RSUM", [P, TT], scope=mix_scope)
        HALL = sb("HALL", [P, 1 + NB, NL], scope=mix_scope)
        CVALL = sb("CVALL", [P, (1 + NB) * (CW - 1), NL], scope=mix_scope)
        mix_scope.close()
        loop_scope.close()

        nbuf1 = (sb("SQ1", [P, 2, T], scope=ffn_scope), sb("XN1", [P, 2, T], scope=ffn_scope),
                 sb("RS1", [P, 2, T], scope=ffn_scope))
        RT = sb("RT", [P, T], scope=ffn_scope)
        HF = sb("HF", [P, T], scope=ffn_scope)
        HH = sb("HH", [P, CH, T], F32R, out_scope)
        HL = sb("HL", [P, CH, T], F32R, out_scope)
        out_scope.close()
        YT = sb("YT", [P, TT, D], scope=out_scope)
        YS = sb("YS", [NB, D], scope=out_scope)
        out_scope.close()
        ffn_scope.close()
        raw_full = [sem(f"raw_full{s}") for s in range(2)]
        hi_done, lo_done = sem("hi_done"), sem("lo_done")
        tile_done = sem("tile_done")
        tile_out = [sem(f"tile_out{s}") for s in range(2)]
        consts_ready, params_in, x_in, table_in = sem("consts_ready"), sem("params_in"), sem("x_in"), sem("table_in")
        table_t, table_ready = sem("table_t"), sem("table_ready")
        x_t, x_ready = sem("x_t"), [sem(f"x_ready{s}") for s in range(2)]
        xs_ready = sem("xs_ready")
        spilled, respilled = sem("spilled"), sem("respilled")
        sq_ready, sq_used, ss_done, root_ready = sem("sq_ready"), sem("sq_used"), sem("ss_done"), sem("root_ready")
        xn_ready, xh_ready, xl_ready = sem("xn_ready"), sem("xh_ready"), sem("xl_ready")
        setup_in, gather_in, bf_in = sem("setup_in"), sem("gather_in"), sem("bf_in")
        masks_ready = sem("masks_ready")
        yh_ready, logit_t, state_t, past_t = sem("yh_ready"), sem("logit_t"), sem("state_t"), sem("past_t")
        absneg_ready, expneg_ready, logf_ready = sem("absneg_ready"), sem("expneg_ready"), sem("logf_ready")
        state_ready, past_ready, tot_ready = sem("state_ready"), sem("past_ready"), sem("tot_ready")
        cum_ps, suf_ps, cum_ready = sem("cum_ps"), sem("suf_ps"), sem("cum_ready")
        logf_out, pgt_in = sem("logf_out"), sem("pgt_in")
        diag_ready, qb_ps, qb_ready = sem("diag_ready"), sem("qb_ps"), sem("qb_ready")
        k_full = [sem(f"k_full{s}") for s in range(NKS)]
        v_full = [sem(f"v_full{s}") for s in range(NVS)]
        pool_prod, k_scored, v_used = sem("pool_prod"), sem("k_scored"), sem("v_used")
        dve_prod = sem("dve_prod")
        qdf_ready, s_done, nm_ready, exp_done = sem("qdf_ready"), sem("s_done"), sem("nm_ready"), sem("exp_done")
        p_norm, pt_ps, pt_ready, att_ps, att_ready = sem("p_norm"), sem("pt_ps"), sem("pt_ready"), sem("att_ps"), sem("att_ready")
        ktr_ps, vtr_ps, ktok_ready, vtok_ready = sem("ktr_ps"), sem("vtr_ps"), sem("ktok_ready"), sem("vtok_ready")
        k_out, v_out = sem("k_out"), sem("v_out")
        gw_full, conv_done, gates_ps = sem("gw_full"), sem("conv_done"), sem("gates_ps")
        sig_done, decay_done, ratio_ready, root_done, lru_done = (
            sem("sig_done"), sem("decay_done"), sem("ratio_ready"), sem("root_done"), sem("lru_done"))
        m8_ready, mall_ready, shifted, pp_ready, pvs_ready = (
            sem("m8_ready"), sem("mall_ready"), sem("shifted"), sem("pp_ready"), sem("pvs_ready"))
        m8_seen = sem("m8_seen")
        merge_in, merge_ps, merge_sub, merge_exp, merged = (
            sem("merge_in"), sem("merge_ps"), sem("merge_sub"), sem("merge_exp"), sem("merged"))
        tail_t, tail_ready, tail_rows, tail_out = sem("tail_t"), sem("tail_ready"), sem("tail_rows"), sem("tail_out")
        h_ready, sq_h_ready = sem("h_ready"), sem("sq_h_ready")
        yn_ready, y_t, ys_t, yt_ready, ys_ready, y_out = (
            sem("yn_ready"), sem("y_t"), sem("ys_t"), [sem(f"yt_ready{s}") for s in range(2)], sem("ys_ready"), sem("y_out"))

        def at(n, half):
            return n % 2, n // 2 + half

        def out_of_banks(t):
            return [(tile_out[0], (t + 1) // 2), (tile_out[1], t // 2)]

        def one(i):
            return bass.ds(i, 1)

        def pair_view(pair):
            return PS[:, 2 * pair:2 * pair + 2, 0:HT]

        S_AT = [(4, 0), (4, 128), (5, 0), (6, 0)]
        P_AT = [0, 128, 384, 768]
        PT_BANK = [(4, 0), (5, 0), (6, 0), (6, 256)]
        PT_AT = [0, 512, 896, 1152]
        K_Q = NPG // 4

        mrg = [qcur[:, 64 * n:64 * n + 64].rearrange("p (h b) -> p h b", h=NH) for n in range(8)]
        merge_e = qcur[:, 5 * 64:7 * 64]

        block = ctx.enter_context(nc.Block())

        @block.sync
        def _(sp):
            def load_unit(n, half, src, peeled=False):
                slot, w = at(n, half)
                if not peeled:
                    sp.wait_ge(lo_done, 2 * w + slot - 1)
                for part in range(2):
                    load_part(slot, src, part)

            def load_part(slot, src, part):
                raw = RAW[:, slot, :].rearrange("p (k c) -> p k c", c=src.shape[2])
                n = src.shape[1] // 2
                ks = slice(part * n, (part + 1) * n)
                sp.dma_start(raw[:, ks, :], src[:, ks, :]).then_inc(raw_full[slot], 16)

            def cols(view, c):
                return view[:, :, bass.ds(c, P)]

            rows = [(w_conv[0], R_CONV), (b_conv, R_BCONV), (b_gate_a, R_BA), (b_gate_x, R_BX), (lru_lambda, R_LAM),
                    (g_att_out, R_GATT), (g_lru_out, R_GLRU), (g_mix, R_GMIX), (g_ffn, R_GFFN),
                    (g_final.rearrange("(a n) -> a n", a=1), R_GFIN)]
            for j in range(TT):
                sp.dma_start(XT[:, j, :], x_prompt[0, j * P:(j + 1) * P, :]).then_inc(x_in, 16)
            sp.dma_start(XS[:, :], x_sample[:, 0, :]).then_inc(x_in, 16)
            for src, r in rows:
                n = src.shape[0] * src.shape[1] // P
                sp.dma_start(PRW[r:r + n, :], src.rearrange("a (n q) -> (a n) q", q=P)).then_inc(table_in, 16)
            load_unit(0, 0, cols(w_in_v, COL_F), True)
            load_unit(1, 0, cols(w_in_v, 0), True)
            sp.dma_start(PGT[:, :], page_table.rearrange("(a b) n -> a (b n)", a=1)).then_inc(pgt_in, 16)
            sp.wait_ge(x_ready[0], KD // 2)
            sp.wait_ge(x_ready[1], KD // 2)
            sp.wait_ge(xs_ready, 1)
            sp.dma_start(xT_spill, A[:, :, :]).then_inc(spilled, 16)
            sp.dma_start(SHW[:, :], state_h[0]).then_inc(setup_in, 16)
            sp.dma_start(SCW[:, :], state_conv[0].rearrange("b j c -> (b j) c")).then_inc(setup_in, 16)
            sp.dma_start(BF[:, :], b_f.rearrange("a h -> h a")).then_inc(bf_in, 16)
            with sp.Fori(0, (NH - 2) // 2) as j:
                load_unit(2, j, cols(w_in_v, P * (2 * j + 1)))
                load_unit(3, j, cols(w_in_v, P * (2 * j + 2)))
            load_unit(U_Q + NH - 1, 0, cols(w_in_v, P * (NH - 1)))
            load_unit(U_L, 0, cols(w_in_v, DA))
            load_unit(U_L + 1, 0, cols(w_in_v, 2 * DA))
            sp.wait_ge(logf_ready, 1)
            sp.dma_start(new_f_p[0, 0].rearrange("(j p) h -> p j h", p=P), LS[:, 0:TT, :]).then_inc(logf_out, 16)
            sp.dma_start(new_f_s[0, :, 0, :], LS[0:NB, TT, :]).then_inc(logf_out, 16)
            sp.wait_ge(cum_ready, 3)
            sp.wait_ge(state_ready, 2)
            sp.wait_ge(pgt_in, 16)

            def step(i, head, prev, nxt, first_v=False):
                for q in range(4):
                    if head:
                        src = [lambda: cols(w_in_v, COL_X + P * i), lambda: cols(w_in_v, COL_G + P * i),
                               lambda: cols(w_in_v, DA + P * (i + 1)) if nxt else cols(w_out_v, 0),
                               lambda: cols(w_in_v, 2 * DA + P * (i + 1)) if nxt else cols(w_out_v, P)][q]()
                        slot, w = at(U_L + 2 + q, 2 * i)
                    if head and q == 1:
                        if prev:
                            sp.wait_ge(gates_ps, i)
                        sp.dma_start(GW[:, 0, :], w_gate_a[0, one(i), :, :].rearrange("a p c -> p (a c)")).then_inc(gw_full, 16)
                        sp.dma_start(GW[:, 1, :], w_gate_x[0, one(i), :, :].rearrange("a p c -> p (a c)")).then_inc(gw_full, 16)
                    for part in range(4):
                        if head:
                            if part == 0:
                                sp.wait_ge(lo_done, 2 * w + slot - 1)
                            if part % 2 == 0:
                                load_part(slot, src, part // 2)
                        if prev:
                            b = K_Q * q + part
                            g = page(i - 1, b)
                            for half in range(2):
                                m = 2 * b + half
                                if not first_v or m >= NVS:
                                    sp.wait_ge(v_used, 2 * NPG * (i - 1) + m - NVS + 1)
                                sp.dma_start(VR[:, m % NVS, :],
                                             v_pages[one(g), :, half * NHH * HD:(half + 1) * NHH * HD].rearrange("a p f -> p (a f)"))\
                                  .then_inc(v_full[m % NVS], 16)

            def page(i, b):
                return sp.value_load(PGT[0:1, one(i * NPG + b)], min_val=0, max_val=cache_k.shape[1] - 1)

            step(0, True, False, True)
            step(1, True, True, True, True)
            with sp.Fori(2, NB - 1) as i:
                step(i, True, True, True)
            step(NB - 1, True, True, False)
            step(NB, False, True, False)

            sp.wait_ge(tail_ready, 1)
            sp.wait_ge(tail_rows, 1)
            hr = (CW - 1) * NL
            sp.dma_start(new_k_s[0, :, 0, :, :].rearrange("b h d -> b (h d)"), KR[0:NB, 0, :]).then_inc(tail_out, 16)
            sp.dma_start(new_v_s[0, :, 0, :, :].rearrange("b h d -> b (h d)"), KR[0:NB, 2, :]).then_inc(tail_out, 16)
            sp.dma_start(new_h_p[0].rearrange("a (n q) -> (a n) q", q=P), KR[0:NL, 1, 0:P]).then_inc(tail_out, 16)
            sp.dma_start(new_h_s[0].rearrange("a (n q) -> (a n) q", q=P), KR[NL:NL * (NB + 1), 1, 0:P]).then_inc(tail_out, 16)
            cv_rows = new_conv_s[0].rearrange("b j (n q) -> (b j n) q", q=P)
            half = hr * (NB + 1) // 2
            sp.dma_start(new_conv_p[0].rearrange("b j (n q) -> (b j n) q", q=P), KR[0:hr, 1, P:2 * P]).then_inc(tail_out, 16)
            sp.dma_start(cv_rows[0:half - hr, :], KR[hr:half, 1, P:2 * P]).then_inc(tail_out, 16)
            sp.dma_start(cv_rows[half - hr:, :], KR[0:half, 1, 2 * P:3 * P]).then_inc(tail_out, 16)
            sp.wait_ge(xn_ready, 2 * KD)
            sp.dma_start(A[:, :, :], xT_spill).then_inc(respilled, 16)
            with sp.Fori(0, (KD - 2) // 2) as j:
                load_unit(U_O + 2, j, cols(w_out_v, P * (2 * j + 2)))
                load_unit(U_O + 3, j, cols(w_out_v, P * (2 * j + 3)))
            with sp.Fori(0, NC) as c:
                with sp.Fori(0, CH // 2) as j:
                    load_unit(U_F, c * (UC // 2) + j, cols(w_up_v, P * (CH * c + 2 * j)))
                    load_unit(U_F + 1, c * (UC // 2) + j, cols(w_up_v, P * (CH * c + 2 * j + 1)))
                with sp.Fori(0, CH // 2) as j:
                    for s in range(2):
                        load_unit(U_F + CH + s, c * (UC // 2) + j,
                                  w_down_v[one(c), :, :, bass.ds(2 * P * (2 * j + s), 2 * P)].rearrange("a p k c -> p (a k) c"))
            for g in range(4):
                sp.wait_ge(yt_ready[0], 2 * (g + 1))
                sp.wait_ge(yt_ready[1], 2 * (g + 1))
                sp.wait_ge(ys_ready, g + 1)
                f = slice(g * D // 4, (g + 1) * D // 4)
                sp.dma_start(y_prompt[0, :, f].rearrange("(j p) f -> p j f", p=P), YT[:, :, f]).then_inc(y_out, 16)
                sp.dma_start(y_sample[:, 0, f], YS[:, f]).then_inc(y_out, 16)
            sp.wait_ge(y_out, 8 * 16)
            sp.wait_ge(logf_out, 2 * 16)
            sp.wait_ge(tail_out, 7 * 16)
            sp.wait_ge(k_out, NH * 16)
            sp.wait_ge(v_out, NH * 16)

        @block.gpsimd
        def _(pool):
            pool.memset(ident[:, :], 0.0).then_inc(consts_ready, 1)
            pool.memset(ones[:, :], 1.0).then_inc(consts_ready, 1)
            pool.memset(maskneg[:, :], 0.0).then_inc(consts_ready, 1)
            pool.wait_ge(consts_ready, 3)
            pool.affine_select(out=ident[:, :], in_=ident[:, :], compare_op=ALU.not_equal, fill=1.0, base=0,
                               pattern=[[-1, P]], channel_multiplier=1).then_inc(consts_ready, 1)
            pool.affine_select(out=maskneg[:, :], in_=maskneg[:, :], compare_op=ALU.is_ge, fill=NEG, base=0,
                               pattern=[[-1, P]], channel_multiplier=1).then_inc(consts_ready, 1)
            pool.wait_ge(x_t, KD + 1)
            pool.affine_select(out=low[:, :], in_=ones[:, :], compare_op=ALU.is_gt, fill=0.0, base=0,
                               pattern=[[-1, P]], channel_multiplier=1).then_inc(masks_ready, 1)
            pool.affine_select(out=tri[:, :], in_=ones[:, :], compare_op=ALU.is_ge, fill=0.0, base=0,
                               pattern=[[1, P]], channel_multiplier=-1).then_inc(masks_ready, 1)
            later_v = later[:, :].rearrange("p (b n) -> p b n", b=NB)
            pool.wait_ge(masks_ready, 2)
            pool.affine_select(out=later_v, in_=low[:, :].rearrange("p (b n) -> p b n", b=NB), compare_op=ALU.is_gt,
                               fill=0.0, base=NPG, pattern=[[NPG, NB], [0, NPG]], channel_multiplier=-1)\
                .then_inc(masks_ready, 1)
            pool.dma_start(IDX[:, :], page_table.rearrange("b (n a) -> (b n) a", a=1).bitcast(U32)).then_inc(gather_in, 16)
            pool.wait_ge(gather_in, 16)
            pool.indirect_dma_start(LG[:, :, :].rearrange("p k h -> p (k h)"), None,
                                    cache_logf[0].rearrange("g k h -> g (k h)"),
                                    bass.IndirectOffsetOnAxis(ap=IDX[:, 0:1], axis=0)).then_inc(gather_in, 16)

            def load_keys(i, b):
                g = pool.value_load(PGT[0:1, one(i * NPG + b)], min_val=0, max_val=cache_k.shape[1] - 1)
                pool.dma_start(KR[:, b % NKS, :], k_pages[one(g), :, :].rearrange("a p f -> p (a f)")).then_inc(k_full[b % NKS], 16)

            def step(i, first, last):
                for m in range(NPG // 2):
                    def loads():
                        for b in (2 * m + 2, 2 * m + 3):
                            if last and b >= NPG:
                                continue
                            if not first or b >= NKS:
                                pool.wait_ge(k_scored, NPG * i + b - NKS + 1)
                            load_keys(i, b)
                    if m == 0:
                        loads()
                        pool.wait_ge(qb_ready, i + 1)
                    b = 2 * m + 1
                    pool.wait_ge(k_full[b % NKS], 16 * (NPG // NKS * i + b // NKS + 1))
                    pool.tensor_tensor(KR[:, b % NKS, :], KR[:, b % NKS, :], QB[:, :], ALU.mult).then_inc(pool_prod, 1)
                    if m > 0:
                        loads()
                pool.wait_ge(m8_ready, i + 1)
                pool.sem_inc(m8_seen, 1)
                pool.partition_all_reduce(MALL[:, :], M8[:, :], P, RED.max).then_inc(mall_ready, 1)

            pool.wait_ge(cum_ready, 3)
            pool.wait_ge(state_ready, 2)
            pool.wait_ge(pgt_in, 16)
            load_keys(0, 0)
            load_keys(0, 1)
            step(0, True, False)
            with pool.Fori(1, NB - 1) as i:
                step(i, False, False)
            step(NB - 1, False, True)

        @block.scalar
        def _(act):
            def split_hi(n, half, tiles=None, peeled=False):
                slot, w = at(n, half)
                act.wait_ge(raw_full[slot], 32 * (w + 1))
                if not peeled:
                    act.wait_ge(tile_done, 2 * w + slot - 1 if tiles is None else tiles)
                nc.scalar.activation(WH[slot][:, :], RAW[:, slot, :], ACT.Copy).then_inc(hi_done, 1)

            def tile_wait(n, half):
                slot, w = at(n, half)
                act.wait_ge(tile_done, 2 * w + slot + 1)
                return slot

            def norm(n, bufs, first, last, groups, sources=()):
                SQ, XN, RS = bufs
                for s, v in sources:
                    act.wait_ge(s, v)
                for g, (k0, k1) in enumerate(groups):
                    def pair(j, start):
                        for s in range(2):
                            if not start:
                                act.wait_ge(sq_used, KD * n + 2 * j + s - 1)
                            nc.scalar.activation(SQ[:, s, :], A[:, one(2 * j + s), :], ACT.Square).then_inc(sq_ready, 1)
                    pair(k0 // 2, k0 == 0 and first)
                    with act.Fori(k0 // 2 + 1, k1 // 2) as j:
                        pair(j, False)
                for g, (k0, k1) in enumerate(groups):
                    act.wait_ge(ss_done, n + g + (n > 1) + 1)
                    nc.scalar.activation(RS[:, g, :].rearrange("p (a t) -> p a t", a=2), PS[:, 4 + 2 * g:6 + 2 * g, 0:HT],
                                         ACT.Sqrt, scale=1.0 / (P * (k1 - k0)), bias=EPS).then_inc(root_ready, 1)
                if not last:
                    with act.Fori(0, KD // 2) as j:
                        for s in range(2):
                            act.wait_ge(xn_ready, KD * n + 2 * j + s + 1)
                            nc.scalar.activation(XH[:, one(2 * j + s), :], XN[:, s, :], ACT.Copy).then_inc(xh_ready, 1)

            act.wait_ge(table_t, 1)
            nc.scalar.activation(PRM[:, :], PS[:, 7, 0:P], ACT.Copy).then_inc(table_ready, 1)
            for k in range(0, KD, 2):
                act.wait_ge(x_t, k + 1)
                nc.scalar.activation(A[:, k, 0:SEQ], PS[:, 4, :], ACT.Copy).then_inc(x_ready[0], 1)
            act.wait_ge(x_t, KD + 1)
            nc.scalar.activation(A[:, :, SEQ:T], PS[:, 6, 0:KD * NB].rearrange("p (k b) -> p k b", k=KD), ACT.Copy)\
                .then_inc(xs_ready, 1)
            split_hi(0, 0, peeled=True)
            norm(0, nbuf0, True, False, [(0, KD)], [(x_ready[0], KD // 2), (x_ready[1], KD // 2), (xs_ready, 1)])

            split_hi(1, 0, peeled=True)
            act.wait_ge(absneg_ready, 1)
            nc.scalar.activation(Z1[:, :, :], Z0[:, :, :], ACT.Exp).then_inc(expneg_ready, 1)
            act.wait_ge(spilled, 16)
            with act.Fori(0, NH // 2) as j:
                for s in range(2):
                    split_hi(U_Q + 1 + s, j)
                    slot = tile_wait(U_Q + s, j)
                    nc.scalar.activation(A[:, one(2 * j + s), :].rearrange("p a (c t) -> p (a c) t", c=2),
                                         pair_view(slot), ACT.Copy).then_inc(tile_out[slot], 1)
            for g in range(2):
                act.wait_ge(past_t, g + 1)
                nc.scalar.activation(LT[:, 4 * g:4 * g + 4, :], PS[:, 4 + g, :], ACT.Copy).then_inc(past_ready, 1)
            for g in range(2):
                act.wait_ge(suf_ps, g + 1)
                nc.scalar.activation(SUF[:, 4 * g:4 * g + 4, :, :], PS[:, 4 + g, :].rearrange("p (h b n) -> p h b n", h=4, b=NB),
                                     ACT.Copy).then_inc(cum_ready, 1)
            act.wait_ge(cum_ps, 1)
            nc.scalar.activation(FT[:, :, :], PS[:, 6, 0:TT * NH].rearrange("p (j h) -> p j h", j=TT), ACT.Copy,
                                 scale=-1.0 / SCALE).then_inc(cum_ready, 1)
            act.wait_ge(state_ready, 2)

            def gates(h, between):
                act.wait_ge(gates_ps, h + 1)
                ba, bx = PRM[:, one(R_BA + h)], PRM[:, one(R_BX + h)]
                nc.scalar.activation(PR[:, 0:SEQ], PS[:, 4, :], ACT.Sigmoid, bias=ba)
                nc.scalar.activation(PR[:, SEQ:T], PS[:, 6, 0:NB], ACT.Sigmoid, bias=ba)
                nc.scalar.activation(PR[:, T:T + SEQ], PS[:, 5, :], ACT.Sigmoid, bias=bx)
                nc.scalar.activation(PR[:, T + SEQ:2 * T], PS[:, 6, NB:2 * NB], ACT.Sigmoid, bias=bx).then_inc(sig_done, 1)
                act.wait_ge(sig_done, h + 1)
                nc.scalar.activation(PT[:, 0:T], PR[:, 0:T], ACT.Tanh, scale=CPOS[:, one(h)])
                nc.scalar.activation(PR[:, 0:T], PR[:, 0:T], ACT.Exp, scale=CNEG[:, one(h)]).then_inc(decay_done, 1)
                between()
                act.wait_ge(ratio_ready, h + 1)
                nc.scalar.activation(PT[:, 0:T], PT[:, 0:T], ACT.Sqrt).then_inc(root_done, 1)

            def softmax(h):
                act.wait_ge(nm_ready, h + 1)
                for t in range(TT):
                    bank, c = S_AT[t]
                    n = (t + 1) * P
                    ins = nc.scalar.activation(PR[:, P_AT[t]:P_AT[t] + n], PS[:, bank, c:c + n], ACT.Exp,
                                               scale=SCALE, bias=NMS[:, t:t + 1], accum_out=SUMS[:, t:t + 1])
                ins.then_inc(exp_done, 1)

            def transposed(h):
                for n, (c0, c1, bank) in enumerate(((0, 512, 4), (512, 896, 5), (896, 1280, 6))):
                    act.wait_ge(pt_ps, 3 * h + n + 1)
                    nc.scalar.activation(PT[:, c0:c1], PS[:, bank, 0:c1 - c0], ACT.Copy).then_inc(pt_ready, 1)

            def attended(h):
                act.wait_ge(att_ps, h + 1)
                nc.scalar.activation(A[:, one(h), 0:SEQ].rearrange("p a t -> p (a t)"), PS[:, 4, :], ACT.Copy)\
                    .then_inc(att_ready, 1)

            def rows_out(full, dst, samples, i):
                nc.scalar.activation(dst[:, 0:HT], PS[:, 2 * full, 0:HT], ACT.Copy)
                nc.scalar.activation(dst[:, HT:SEQ], PS[:, 2 * full + 1, 0:HB], ACT.Copy)
                nc.scalar.activation(samples[:, one(i), :].rearrange("p a b -> p (a b)"), PS[:, 2 * full + 1, HB:HT], ACT.Copy)\
                    .then_inc(tile_out[full], 1)

            def step(i, head, prev):
                def broadcast_query():
                    if head:
                        act.wait_ge(qb_ps, i + 1)
                        if prev:
                            act.wait_ge(k_scored, NPG * i)
                        nc.scalar.activation(QB[:, :].rearrange("p (a n) -> p a n", a=2), PS[:, 4:6, :], ACT.Copy,
                                             scale=SCALE).then_inc(qb_ready, 1)

                if head:
                    split_hi(U_L + 1, 2 * i)
                if prev:
                    gates(i - 1, broadcast_query)
                else:
                    broadcast_query()
                if head:
                    slot = tile_wait(U_L, 2 * i)
                    split_hi(U_L + 2, 2 * i)
                    if prev:
                        act.wait_ge(s_done, i)
                    rows_out(slot, kT, KS, i)
                if prev:
                    softmax(i - 1)
                if head:
                    rows_out(tile_wait(U_L + 1, 2 * i), vT, VS, i)
                if prev:
                    transposed(i - 1)
                if head:
                    split_hi(U_L + 3, 2 * i)
                if prev:
                    attended(i - 1)
                if head:
                    slot = tile_wait(U_L + 2, 2 * i)
                    if prev:
                        act.wait_ge(lru_done, i)
                    W3 = CW - 1
                    nc.scalar.activation(XW[:, W3:W3 + HT], PS[:, 2 * slot, 0:HT], ACT.Copy)
                    nc.scalar.activation(XW[:, W3 + HT:W3 + SEQ], PS[:, 2 * slot + 1, 0:HB], ACT.Copy)
                    nc.scalar.activation(XW[:, W3 + SEQ:].rearrange("p (b j) -> p b j", j=CW)[:, :, W3],
                                         PS[:, 2 * slot + 1, HB:HT], ACT.Copy).then_inc(tile_out[slot], 1)
                    split_hi(U_L + 4, 2 * i)
                    for tr, tok, ready, stored, bank, dst in ((ktr_ps, ktok, ktok_ready, k_out, 5, new_k_p),
                                                              (vtr_ps, vtok[:, :, :], vtok_ready, v_out, 6, new_v_p)):
                        act.wait_ge(tr, i + 1)
                        if prev:
                            act.wait_ge(stored, 16 * i)
                        nc.scalar.activation(tok, PS[:, bank, :].rearrange("p (j d) -> p j d", j=TT), ACT.Copy)\
                            .then_inc(ready, 1)
                        act.wait_ge(ready, i + 1)
                        act.dma_start(dst[0, 0, :, one(i), :].rearrange("(j p) a d -> p j (a d)", p=P), tok)\
                            .then_inc(stored, 16)
                    act.wait_ge(shifted, i + 1)
                    nc.scalar.activation(SUF[:, :, one(i), :].rearrange("p h a n -> p h (a n)"), SC[:, :, :], ACT.Exp)\
                        .then_inc(pp_ready, 1)
                    slot = tile_wait(U_L + 3, 2 * i)
                    nc.scalar.activation(PT[:, T:2 * T].rearrange("p (a t) -> p a t", a=2), pair_view(slot),
                                         ACT.Gelu_apprx_tanh).then_inc(tile_out[slot], 1)

            step(0, True, False)
            with act.Fori(1, NH) as i:
                step(i, True, True)
            step(NH, False, True)
            act.wait_ge(v_used, 2 * NPG * NB)
            nc.scalar.activation(PVS[:, :, :], PS[:, 7, 0:NB * NH].rearrange("p (b h) -> p h b", b=NB), ACT.Copy)\
                .then_inc(pvs_ready, 1)

            act.wait_ge(merge_sub, 1)
            nc.scalar.activation(merge_e[:, :], merge_e[:, :], ACT.Exp).then_inc(merge_exp, 1)
            act.wait_ge(tail_t, 1)
            nc.scalar.activation(KR[0:NB, 0, :].rearrange("p (a n) -> p a n", a=2), PS[0:NB, 4:6, :], ACT.Copy)
            nc.scalar.activation(KR[0:NB, 2, :].rearrange("p (a n) -> p a n", a=2), PS[0:NB, 6:8, :], ACT.Copy)\
                .then_inc(tail_ready, 1)
            norm(1, nbuf1, False, False, [(0, NH), (NH, KD)], [(merged, 1), (att_ready, NH), (lru_done, NL), (tail_out, 7 * 16),
                  (k_out, 16 * NH), (v_out, 16 * NH), (logf_out, 2 * 16)])
            with act.Fori(0, KD // 2) as j:
                for s in range(2):
                    split_hi(U_O + 1 + s, j)
            norm(2, nbuf1, False, False, [(0, KD)], out_of_banks(U_F))

            def up(c, j):
                for s in range(2):
                    split_hi(U_F + 1 + s, c * (UC // 2) + j, TC * c + 2 * j + (U_F + s))
                    slot = tile_wait(U_F + s, c * (TC // 2) + j)
                    nc.scalar.activation(RT[:, :].rearrange("p (a t) -> p a t", a=2), pair_view(slot), ACT.Relu)\
                        .then_inc(tile_out[slot], 1)
                    act.drain()
                    act.wait_ge(sq_h_ready, CH * c + 2 * j + s)
                    nc.scalar.activation(HF[:, :], RT[:, :], ACT.Square)
                    act.drain()
                    nc.scalar.activation(HH[:, one(2 * j + s), :].rearrange("p a t -> p (a t)"), HF[:, :], ACT.Copy)\
                        .then_inc(h_ready, 1)

            with act.Fori(0, NC - 1) as c:
                with act.Fori(0, CH // 2) as j:
                    up(c, j)
                with act.Fori(0, CH // 2) as j:
                    for s in range(2):
                        split_hi(U_F + CH + 1 + s, c * (UC // 2) + j, TC * c + 4 * j + (U_F + CH + 2 * s))
            with act.Fori(0, CH // 2) as j:
                up(NC - 1, j)
            for n in range(CH - 1):
                split_hi(U_F + CH + 1 + n, (NC - 1) * (UC // 2), TC * (NC - 1) + U_F + CH + 2 * n)
            norm(3, nbuf1, False, True, [(0, KD)], out_of_banks(U_F + NC * TC))
            for k in range(0, KD, 2):
                act.wait_ge(y_t, k + 1)
                nc.scalar.activation(YT[:, :, k * P:(k + 1) * P], PS[:, 4, :].rearrange("p (j f) -> p j f", j=TT), ACT.Copy)\
                    .then_inc(yt_ready[0], 1)
                if k % 4 == 2:
                    g = k // 4
                    act.wait_ge(ys_t, g + 1)
                    nc.scalar.activation(YS[:, g * 512:(g + 1) * 512], PS[0:NB, 6 + g % 2, :], ACT.Copy).then_inc(ys_ready, 1)

        @block.vector
        def _(dve):
            V = nc.vector

            def split_lo(n, half):
                slot, w = at(n, half)
                dve.wait_ge(hi_done, 2 * w + slot + 1)
                V.tensor_tensor(WL[slot][:, :], RAW[:, slot, :], WH[slot][:, :].bitcast(F32), ALU.subtract)\
                    .then_inc(lo_done, 1)

            def tile_wait(n, half):
                slot, w = at(n, half)
                dve.wait_ge(tile_done, 2 * w + slot + 1)
                return slot

            def norm(n, bufs, groups, col):
                SQ, XN, RS = bufs
                for g, (k0, k1) in enumerate(groups):
                    dve.wait_ge(root_ready, n + g + (n > 1) + 1)
                    V.reciprocal(RS[:, g, :], RS[:, g, :])
                dve.drain()
                for g, (k0, k1) in enumerate(groups):
                    with dve.Fori(k0 // 2, k1 // 2) as j:
                        dve.wait_ge(xl_ready, KD * n + 2 * j)
                        for s in range(2):
                            k = 2 * j + s
                            V.scalar_tensor_tensor(XN[:, s, :], A[:, one(k), :].rearrange("p a t -> p (a t)"),
                                                   PRM[:, one(col + k)], RS[:, g, :], ALU.mult, ALU.mult).then_inc(xn_ready, 1)
                        for s in range(2):
                            k = 2 * j + s
                            dve.wait_ge(xh_ready, KD * n + k + 1)
                            V.tensor_tensor(XL[:, one(k), :].rearrange("p a t -> p (a t)"), XN[:, s, :],
                                            XH[:, one(k), :].rearrange("p a t -> p (a t)").bitcast(F32), ALU.subtract)\
                                .then_inc(xl_ready, 1)

            for k in range(1, KD, 2):
                dve.wait_ge(x_t, k + 1)
                V.tensor_copy(A[:, k, 0:SEQ], PS[:, 5, :]).then_inc(x_ready[1], 1)
            split_lo(0, 0)
            dve.wait_ge(table_ready, 1)
            norm(0, nbuf0, [(0, KD)], R_GMIX)
            split_lo(1, 0)

            V.memset(YF[:, :, :], 0.0)
            slot = tile_wait(0, 0)
            dve.wait_ge(bf_in, 16)
            V.tensor_scalar(YH[:, :].rearrange("p (a t) -> p a t", a=2), pair_view(slot)[0:NH], BF[:, 0:1], None, ALU.add)\
                .then_inc(tile_out[slot], 1)
            dve.drain()
            V.tensor_copy(YF[:, TT + 1, :], PRM[:, R_LAM:R_LAM + NL]).then_inc(yh_ready, 1)
            dve.wait_ge(logit_t, 1)
            V.tensor_copy(YF[:, 0:TT, :], PS[:, 4, 0:TT * NH].rearrange("p (j h) -> p j h", j=TT))
            V.tensor_copy(YF[0:NB, TT, :], PS[0:NB, 4, TT * NH:(TT + 1) * NH])
            dve.drain()
            V.scalar_tensor_tensor(Z0[:, :, :], YF[:, :, :], -1.0, YF[:, :, :], ALU.mult, ALU.min).then_inc(absneg_ready, 1)
            dve.wait_ge(expneg_ready, 1)
            V.tensor_scalar(Z0[:, :, :], Z1[:, :, :], 2.0, None, ALU.add)
            dve.drain()
            V.reciprocal(Z0[:, :, :], Z0[:, :, :])
            dve.drain()
            V.tensor_tensor(Z1[:, :, :], Z1[:, :, :], Z0[:, :, :], ALU.mult)
            dve.drain()
            V.tensor_tensor(Z0[:, :, :], Z1[:, :, :], Z1[:, :, :], ALU.mult)
            dve.drain()
            V.tensor_scalar(Z2[:, :, :], Z0[:, :, :], 2.0 / 17, None, ALU.mult)
            for n in range(15, 1, -2):
                dve.drain()
                V.scalar_tensor_tensor(Z2[:, :, :], Z2[:, :, :], 2.0 / n, Z0[:, :, :], ALU.add, ALU.mult)
            dve.drain()
            V.scalar_tensor_tensor(Z2[:, :, :], Z2[:, :, :], 2.0, Z1[:, :, :], ALU.add, ALU.mult)
            dve.drain()
            V.scalar_tensor_tensor(LS[:, :, :], YF[:, :, :], 0.0, Z2[:, :, :], ALU.min, ALU.subtract).then_inc(logf_ready, 1)
            dve.drain()
            V.tensor_scalar(CPOS[:, :], LS[:, TT + 1, :], -LRU_C, None, ALU.mult)
            V.tensor_scalar(CNEG[:, :], LS[:, TT + 1, :], LRU_C, None, ALU.mult).then_inc(logf_ready, 1)
            dve.wait_ge(state_t, 1)
            V.tensor_copy(H0[:, :, :], PS[:, 7, 0:NL * NB].rearrange("p (n b) -> p n b", n=NL)).then_inc(state_ready, 1)
            V.tensor_copy(CST[:, :, :], PS[:, 7, NL * NB:NL * NB * CW].rearrange("p (n r) -> p n r", n=NL))\
                .then_inc(state_ready, 1)
            dve.wait_ge(gather_in, 32)
            V.tensor_reduce(TOT[:, :], LG[:, :, :].rearrange("p k h -> p h k"), AX.X, ALU.add)
            dve.drain()
            dve.wait_ge(masks_ready, 3)
            V.tensor_tensor(MT[:, :, :], later[:, :].unsqueeze(1).to_broadcast([P, NH, P]),
                            TOT[:, :].unsqueeze(2).to_broadcast([P, NH, P]), ALU.mult).then_inc(tot_ready, 1)
            with dve.Fori(0, NH // 2) as j:
                for s in range(2):
                    split_lo(U_Q + 1 + s, j)
            dve.wait_ge(cum_ready, 3)
            V.memset(XW[:, 0:CW - 1], 0.0)

            def score(i, pages):
                for b in pages:
                    if b % 2:
                        dve.wait_ge(pool_prod, NPG // 2 * i + b // 2 + 1)
                    else:
                        dve.wait_ge(k_full[b % NKS], 16 * (NPG // NKS * i + b // NKS + 1))
                        V.tensor_tensor(KR[:, b % NKS, :], KR[:, b % NKS, :], QB[:, :], ALU.mult).then_inc(dve_prod, 1)
                        dve.wait_ge(dve_prod, NPG // 2 * i + b // 2 + 1)
                    V.tensor_reduce(SC[:, :, b], KR[:, b % NKS, :].rearrange("p (h d) -> p h d", h=NH), AX.X, ALU.add)\
                        .then_inc(k_scored, 1)

            def recurrence(h):
                R, I, TH, U = PR[:, 0:T], PR[:, T:2 * T], PT[:, 0:T], XW[:, CW - 1:CW - 1 + T]
                dve.wait_ge(sig_done, h + 1)
                V.tensor_tensor(I, I, XC[:, :], ALU.mult)
                dve.wait_ge(decay_done, h + 1)
                V.tensor_tensor(U, R, R, ALU.mult)
                dve.drain()
                V.scalar_tensor_tensor(TH, U, 1.0, TH, ALU.add, ALU.mult).then_inc(ratio_ready, 1)
                dve.wait_ge(root_done, h + 1)
                V.tensor_tensor(I, I, TH, ALU.mult)
                dve.drain()
                V.tensor_tensor_scan(XC[:, 0:SEQ], PR[:, 0:SEQ], PR[:, T:T + SEQ], 0.0, ALU.mult, ALU.add)
                V.tensor_tensor(XC[:, SEQ:T], PR[:, SEQ:T], H0[:, one(h), :].rearrange("p a b -> p (a b)"), ALU.mult)
                dve.drain()
                V.tensor_tensor(XC[:, SEQ:T], XC[:, SEQ:T], PR[:, T + SEQ:2 * T], ALU.add)
                dve.drain()
                dve.wait_ge(tile_out[0], at(U_L + 3, 2 * h)[1] + 1)
                V.tensor_copy(HALL[:, :, one(h)].rearrange("p r a -> p (r a)"), XC[:, SEQ - 1:T])
                V.tensor_tensor(A[:, one(NH + h), :].rearrange("p a t -> p (a t)"), XC[:, :], PT[:, T:2 * T], ALU.mult)\
                    .then_inc(lru_done, 1)

            def conv(i):
                V.tensor_copy(XW[:, CW - 1 + SEQ:].rearrange("p (b j) -> p b j", j=CW)[:, :, 0:CW - 1],
                              CST[:, one(i), :].rearrange("p a (b j) -> p (a b) j", b=NB))
                dve.drain()
                dve.wait_ge(tile_out[1], at(U_L + 2, 2 * i)[1] + 1)
                tails = XW[:, CW - 1 + SEQ:].rearrange("p (b j) -> p b j", j=CW)
                for j in range(CW):
                    w = PRM[:, one(R_CONV + j * NL + i)]
                    for dst, src in ((XC[:, 0:SEQ], XW[:, j:j + SEQ]), (XC[:, SEQ:T], tails[:, :, j])):
                        if j == 0:
                            V.tensor_scalar(dst, src, w, PRM[:, one(R_BCONV + i)], ALU.mult, ALU.add)
                        else:
                            ins = V.scalar_tensor_tensor(dst, src, w, dst, ALU.mult, ALU.add)
                    dve.drain()
                V.tensor_copy(CVALL[:, 0:CW - 1, one(i)].rearrange("p r a -> p (r a)"), XW[:, SEQ:SEQ + CW - 1])
                V.tensor_copy(CVALL[:, CW - 1:, one(i)].rearrange("p (b j) a -> p b (j a)", b=NB), tails[:, :, 1:CW])\
                    .then_inc(conv_done, 1)

            def step(i, head, prev):
                h = i - 1
                if head:
                    split_lo(U_L + 1, 2 * i)
                    if not prev:
                        for s, v in out_of_banks(U_L):
                            dve.wait_ge(s, v)
                    V.tensor_copy(QCOL[:, :], A[:, 0:NH, SEQ + i] if isinstance(i, int) else
                                  A[:, 0:NH, one(SEQ + i)].rearrange("p h a -> p (h a)")).then_inc(diag_ready, 1)
                if prev:
                    recurrence(h)
                    V.tensor_tensor(PT[:, 0:SEQ].rearrange("p (j k) -> p j k", j=TT), ident[:, :].unsqueeze(1).to_broadcast([P, TT, P]),
                                    FT[:, :, one(h)].to_broadcast([P, TT, P]), ALU.mult)
                    dve.wait_ge(k_out, 16 * i)
                    V.tensor_copy(qcur[:, :], A[:, one(h), 0:SEQ].rearrange("p a t -> p (a t)")).then_inc(qdf_ready, 1)
                if head:
                    dve.wait_ge(qb_ready, i + 1)
                    score(i, range(0, 4))
                    split_lo(U_L + 2, 2 * i)
                if prev:
                    dve.wait_ge(s_done, h + 1)
                    for t in range(TT):
                        bank, c = S_AT[t]
                        V.tensor_reduce(NM[:, t:t + 1], PS[:, bank, c:c + (t + 1) * P], AX.X, ALU.max, negate=True)
                    dve.drain()
                    V.tensor_scalar(NMS[:, :], NM[:, :], SCALE, None, ALU.mult).then_inc(nm_ready, 1)
                if head:
                    score(i, range(4, 6))
                if prev:
                    dve.wait_ge(exp_done, h + 1)
                    V.reciprocal(RSUM[:, :], SUMS[:, :])
                    dve.drain()
                    for t in range(TT):
                        row = PR[:, P_AT[t]:P_AT[t] + (t + 1) * P]
                        ins = V.tensor_scalar(row, row, RSUM[:, t:t + 1], None, ALU.mult)
                    ins.then_inc(p_norm, 1)
                if head:
                    score(i, range(6, 10))
                    split_lo(U_L + 3, 2 * i)
                    score(i, range(10, 14))
                    conv(i)
                    split_lo(U_L + 4, 2 * i)
                    score(i, range(14, NPG))
                    dve.drain()
                    V.tensor_tensor(SC[:, :, :], SC[:, :, :], SUF[:, :, one(i), :].rearrange("p h a n -> p h (a n)"), ALU.add)
                    dve.drain()
                    V.tensor_reduce(M8[:, :], SC[:, :, :], AX.X, ALU.max).then_inc(m8_ready, 1)
                    dve.wait_ge(mall_ready, i + 1)
                    V.tensor_copy(MX[:, :, one(i)].rearrange("p h a -> p (h a)"), MALL[:, :])
                    V.tensor_tensor(SC[:, :, :], SC[:, :, :], MALL[:, :].unsqueeze(2).to_broadcast([P, NH, NPG]), ALU.subtract)\
                        .then_inc(shifted, 1)

            step(0, True, False)
            with dve.Fori(1, NH) as i:
                step(i, True, True)
            step(NH, False, True)
            dve.wait_ge(pp_ready, NB)
            V.tensor_reduce(DEN[:, :, :], SUF[:, :, :, :], AX.X, ALU.add)

            prod, lfd, SN, DR, MM = mrg[0:5]
            E1, E2 = mrg[5:7]
            tmp = mrg[7]
            q_s = A[:, 0:NH, SEQ:T]
            dve.wait_ge(s_done, NH)
            dve.wait_ge(k_out, 16 * NH)
            V.tensor_tensor(prod, q_s, KS[:, :, :], ALU.mult)
            V.tensor_tensor(lfd[0:NB], LS[0:NB, TT, :].unsqueeze(2).to_broadcast([NB, NH, NB]),
                            ident[0:NB, 0:NB].unsqueeze(1).to_broadcast([NB, NH, NB]), ALU.mult)
            dve.drain()
            V.tensor_scalar(lfd[0:NB], lfd[0:NB], -1.0 / SCALE, None, ALU.mult).then_inc(merge_in, 1)
            dve.wait_ge(merge_ps, 1)
            V.tensor_scalar(SN, PS[:, 5, 0:NH * NB].rearrange("p (h b) -> p h b", h=NH), SCALE, None, ALU.mult)
            V.tensor_copy(DR, PS[:, 6, 0:NH * NB].rearrange("p (h b) -> p h b", h=NH)).then_inc(merge_in, 1)
            dve.drain()
            V.tensor_tensor(MM, MX[:, :, :], SN, ALU.max)
            dve.drain()
            V.tensor_tensor(E1, MX[:, :, :], MM, ALU.subtract)
            V.tensor_tensor(E2, SN, MM, ALU.subtract).then_inc(merge_sub, 1)
            dve.wait_ge(merge_exp, 1)
            dve.wait_ge(pvs_ready, 1)
            V.tensor_tensor(DR, DR, E1, ALU.mult)
            V.tensor_tensor(prod, PVS[:, :, :], E1, ALU.mult)
            V.tensor_tensor(tmp, VS[:, :, :], E2, ALU.mult)
            dve.drain()
            V.tensor_tensor(DR, DR, E2, ALU.add)
            V.tensor_tensor(prod, prod, tmp, ALU.add)
            dve.drain()
            V.reciprocal(DR, DR)
            dve.drain()
            V.tensor_tensor(q_s, prod, DR, ALU.mult).then_inc(merged, 1)
            hr = (CW - 1) * NL * (NB + 1) // 2
            dve.wait_ge(tail_t, 1)
            V.tensor_copy(KR[0:NL * (NB + 1), 1, 0:P], PS[0:NL * (NB + 1), 2, 0:P])
            V.tensor_copy(KR[0:hr, 1, P:3 * P], PS[0:hr, 3, 0:2 * P]).then_inc(tail_rows, 1)

            norm(1, nbuf1, [(0, NH), (NH, KD)], R_GATT)
            dve.wait_ge(respilled, 16)
            with dve.Fori(0, KD // 2) as j:
                for s in range(2):
                    split_lo(U_O + 1 + s, j)
                    slot = tile_wait(U_O + s, j)
                    a = A[:, one(2 * j + s), :].rearrange("p a (c t) -> p (a c) t", c=2)
                    V.tensor_tensor(a, pair_view(slot), a, ALU.add).then_inc(tile_out[slot], 1)
            norm(2, nbuf1, [(0, KD)], R_GFFN)

            def up(c, j):
                for s in range(2):
                    split_lo(U_F + 1 + s, c * (UC // 2) + j)
                    dve.wait_ge(h_ready, CH * c + 2 * j + s + 1)
                    V.tensor_tensor(HL[:, one(2 * j + s), :].rearrange("p a t -> p (a t)"), HF[:, :],
                                    HH[:, one(2 * j + s), :].rearrange("p a t -> p (a t)").bitcast(F32), ALU.subtract)\
                        .then_inc(sq_h_ready, 1)

            def down(c, j, units, split):
                for s in units:
                    if split(s):
                        split_lo(U_F + CH + 1 + s, c * (UC // 2) + j)
                    for m in range(2):
                        slot = tile_wait(U_F + CH + 2 * s + m, c * (TC // 2) + 2 * j)
                        a = A[:, one(4 * j + 2 * s + m), :].rearrange("p a (c t) -> p (a c) t", c=2)
                        V.tensor_tensor(a, pair_view(slot), a, ALU.add).then_inc(tile_out[slot], 1)

            with dve.Fori(0, NC - 1) as c:
                with dve.Fori(0, CH // 2) as j:
                    up(c, j)
                with dve.Fori(0, CH // 2) as j:
                    down(c, j, range(2), lambda s: True)
            with dve.Fori(0, CH // 2) as j:
                up(NC - 1, j)
            with dve.Fori(0, CH // 2 - 1) as j:
                down(NC - 1, j, range(2), lambda s: True)
            down(NC - 1, CH // 2 - 1, range(2), lambda s: s == 0)

            SQ, XN, RS = nbuf1
            dve.wait_ge(root_ready, 5)
            V.reciprocal(RS[:, 0, :], RS[:, 0, :])
            dve.drain()
            for k in range(KD + 2):
                if k < KD:
                    if k >= 2:
                        dve.wait_ge(y_t, k - 1)
                    V.scalar_tensor_tensor(XN[:, k % 2, :], A[:, k, :], PRM[:, R_GFIN + k:R_GFIN + k + 1], RS[:, 0, :],
                                           ALU.mult, ALU.mult).then_inc(yn_ready, 1)
                m = k - 2
                if m >= 0 and m % 2:
                    dve.wait_ge(y_t, m + 1)
                    V.tensor_copy(YT[:, :, m * P:(m + 1) * P], PS[:, 5, :].rearrange("p (j f) -> p j f", j=TT))\
                        .then_inc(yt_ready[1], 1)

        @block.tensor
        def _(pe):
            mm = nc.tensor.matmul

            def products(xh, xl, wh, wl, dsts, kts, insert={}):
                for n, k in enumerate(kts):
                    for x in (xh, xl):
                        for c in range(2):
                            mm(dsts[c], wh(n), x[:, k, c * HT:(c + 1) * HT], start=n == 0 and x is xh, stop=False)
                    for f in insert.get(2 * n, ()):
                        f()
                    for c in range(2):
                        ins = mm(dsts[c], wl(n), xh[:, k, c * HT:(c + 1) * HT], start=False, stop=n == len(kts) - 1)
                    if n < len(kts) - 1:
                        for f in insert.get(2 * n + 1, ()):
                            f()
                return ins

            def unit(n, half, tile, tile_half, insert={}):
                slot, w = at(n, half)
                pair, tw = at(tile, tile_half)
                pe.wait_ge(lo_done, 2 * w + slot + 1)
                if not (isinstance(tw, int) and tw == 0):
                    pe.wait_ge(tile_out[pair], tw)
                ins = products(XH, XL, lambda k: WH[slot][:, k * P:(k + 1) * P], lambda k: WL[slot][:, k * P:(k + 1) * P],
                               [PS[:, 2 * pair + c, 0:HT] for c in range(2)], range(KD), insert)
                ins.then_inc(tile_done, 1)
                for f in insert.get(2 * KD - 1, ()):
                    f()
                return pair

            def norm_sums(n, bufs, groups):
                SQ = bufs[0]
                for g, (k0, k1) in enumerate(groups):
                    for k in range(k0, k1):
                        pe.wait_ge(sq_ready, KD * n + k + 1)
                        for c in range(2):
                            ins = mm(PS[:, 4 + 2 * g + c, 0:HT], ones[:, :], SQ[:, k % 2, c * HT:(c + 1) * HT],
                                     start=k == k0, stop=k == k1 - 1)
                        ins.then_inc(sq_used, 1)
                        if k == k1 - 1:
                            pe.wait_ge(sq_used, KD * n + k + 1)
                            pe.sem_inc(ss_done, 1)

            tr = nc.tensor.transpose
            pe.wait_ge(consts_ready, 5)
            pe.wait_ge(table_in, 16 * 10)
            tr(PS[:, 7, 0:P], PRW[:, :], ident[:, :]).then_inc(table_t, 1)
            pe.wait_ge(x_in, 16 * (TT + 1))
            for k in range(KD):
                if k >= 2:
                    pe.wait_ge(x_ready[k % 2], k // 2)
                for j in range(TT):
                    ins = tr(PS[:, 4 + k % 2, j * P:(j + 1) * P], XT[:, j, k * P:(k + 1) * P], ident[:, :])
                ins.then_inc(x_t, 1)
            for k in range(KD):
                ins = tr(PS[:, 6, k * NB:(k + 1) * NB], XS[:, k * P:(k + 1) * P], ident[0:NB, 0:NB])
            ins.then_inc(x_t, 1)
            pe.wait_ge(x_ready[0], KD // 2)
            pe.wait_ge(x_ready[1], KD // 2)
            norm_sums(0, nbuf0, [(0, KD)])
            pe.wait_ge(xl_ready, KD)
            unit(0, 0, 0, 0)
            pe.wait_ge(setup_in, 32)
            for n in range(NL):
                tr(PS[:, 7, n * NB:(n + 1) * NB], SHW[:, n * P:(n + 1) * P], ident[0:NB, 0:NB])
            r = NB * (CW - 1)
            for n in range(NL):
                ins = tr(PS[:, 7, NL * NB + n * r:NL * NB + (n + 1) * r], SCW[:, n * P:(n + 1) * P], ident[0:r, 0:r])
            ins.then_inc(state_t, 1)
            pe.wait_ge(yh_ready, 1)
            pe.wait_ge(root_ready, 1)
            for j in range(TT):
                tr(PS[:, 4, j * NH:(j + 1) * NH], YH[:, j * P:(j + 1) * P], ident[0:NH, 0:NH])
            tr(PS[0:NB, 4, TT * NH:(TT + 1) * NH], YH[:, SEQ:T], ident[0:NH, 0:NH]).then_inc(logit_t, 1)
            with pe.Fori(0, NH // 2) as j:
                for s in range(2):
                    unit(U_Q + s, j, U_Q + s, j)
            pe.wait_ge(gather_in, 32)
            pe.wait_ge(absneg_ready, 1)
            for h in range(NH):
                ins = tr(PS[:, 4 + h // 4, (h % 4) * P:(h % 4 + 1) * P], LG[:, :, h], ident[:, :])
                if h % 4 == 3:
                    ins.then_inc(past_t, 1)
            pe.wait_ge(logf_ready, 1)
            pe.wait_ge(masks_ready, 3)
            cum = PS[:, 6, 0:TT * NH].rearrange("p (j h) -> p j h", j=TT)
            mm(cum, tri[:, :], LS[:, 0:TT, :], start=True, stop=False)
            for j in range(TT - 1):
                n = TT - 1 - j
                ins = mm(cum[:, j + 1:, :], ones[:, :], LS[:, j:j + 1, :].to_broadcast([P, n, NH]), start=False, stop=j == TT - 2)
            ins.then_inc(cum_ps, 1)
            pe.wait_ge(tot_ready, 1)
            for g in range(2):
                pe.wait_ge(past_ready, g + 1)
                mm(PS[:, 4 + g, :], low[:, :], LT[:, 4 * g:4 * g + 4, :].rearrange("p h n -> p (h n)"), start=True, stop=False)
                mm(PS[:, 4 + g, :], ones[:, :], MT[:, 4 * g:4 * g + 4, :].rearrange("p h n -> p (h n)"), start=False, stop=True)\
                    .then_inc(suf_ps, 1)

            def value(h, n):
                m, head = n // NHH, n % NH
                b = m // 2
                if n == 0:
                    pe.wait_ge(pp_ready, h + 1)
                if n % NHH == 0:
                    pe.wait_ge(v_full[m % NVS], 16 * (2 * NPG // NVS * h + m // NVS + 1))
                ins = mm(PS[:, 7, one(NH * h + head)], VR[:, m % NVS, (n % NHH) * HD:(n % NHH + 1) * HD],
                         SUF[:, head, one(h), b],
                         start=n == 0, stop=b == NPG - 1, skip_group_check=True)
                if n % NHH == NHH - 1:
                    ins.then_inc(v_used, 1)

            def scores(h):
                pe.wait_ge(qdf_ready, h + 1)
                for t in range(TT):
                    bank, c = S_AT[t]
                    n = (t + 1) * P
                    dst = PS[:, bank, c:c + n]
                    mm(dst, qcur[:, t * P:(t + 1) * P], kT[:, 0:n], start=True, stop=False)
                    mm(dst, ones[:, :], PT[:, 0:n], start=False, stop=False)
                    ins = mm(dst[:, n - P:n], ident[:, :], maskneg[:, :], start=False, stop=True)
                ins.then_inc(s_done, 1)

            def transpose_probs(h):
                pe.wait_ge(p_norm, h + 1)
                for j in range(TT):
                    bank, c = PT_BANK[j]
                    for t in range(j, TT):
                        ins = tr(PS[:, bank, c + (t - j) * P:c + (t - j + 1) * P],
                                 PR[:, P_AT[t] + j * P:P_AT[t] + (j + 1) * P], ident[:, :])
                    if j != 2:
                        ins.then_inc(pt_ps, 1)

            def attend(h):
                pe.wait_ge(vtok_ready, h + 1)
                for j in range(TT):
                    pe.wait_ge(pt_ready, 3 * h + min(j + 1, 3))
                    ins = mm(PS[:, 4, j * P:SEQ], vtok[:, j, :], PT[:, PT_AT[j]:PT_AT[j] + (TT - j) * P],
                             start=j == 0, stop=j == TT - 1)
                ins.then_inc(att_ps, 1)

            def step(i, head, prev):
                def queries():
                    pe.wait_ge(diag_ready, i + 1)
                    if prev:
                        pe.wait_ge(sig_done, i)
                    for n in range(NH):
                        ins = mm(PS[:, 4 + n // 4, n % 4 * P:(n % 4 + 1) * P], QCOL[:, n:n + 1].to_broadcast([P, P]), ident[:, :],
                                 start=True, stop=True)
                    ins.then_inc(qb_ps, 1)

                def head_scores():
                    if head:
                        pe.wait_ge(qb_ready, i + 1)
                    scores(i - 1)

                def rows():
                    pe.wait_ge(tile_out[1], at(U_L, 2 * i)[1] + 1)
                    if prev:
                        pe.wait_ge(pt_ready, 3 * i)
                    for j in range(TT):
                        ins = tr(PS[:, 5, j * P:(j + 1) * P], kT[:, j * P:(j + 1) * P], ident[:, :])
                    ins.then_inc(ktr_ps, 1)
                    pe.wait_ge(tile_out[0], at(U_L + 1, 2 * i)[1] + 1)
                    for j in range(TT):
                        ins = tr(PS[:, 6, j * P:(j + 1) * P], vT[:, j * P:(j + 1) * P], ident[:, :])
                    ins.then_inc(vtr_ps, 1)

                extra = {}
                if head:
                    extra[0, 7] = queries
                    extra[3, 7] = rows
                if prev:
                    extra[1, 5] = head_scores
                    extra[2, 3] = lambda: transpose_probs(i - 1)
                    extra[2, 15] = lambda: attend(i - 1)

                def product(q, n):
                    return lambda: value(i - 1, 2 * KD * q + n)

                for q in range(4):
                    insert = {n: ([product(q, n)] if prev else []) + ([extra[q, n]] if (q, n) in extra else [])
                              for n in range(2 * KD)}
                    if head:
                        unit(U_L + q, 2 * i, U_L + q, 2 * i, insert)
                    else:
                        for n in range(2 * KD):
                            for f in insert[n]:
                                f()
                if head:
                    pe.wait_ge(gw_full, 32 * (i + 1))
                    pe.wait_ge(conv_done, i + 1)
                    if prev:
                        pe.wait_ge(att_ready, i)
                    pe.wait_ge(ktok_ready, i + 1)
                    pe.wait_ge(vtok_ready, i + 1)
                    for g in range(2):
                        mm(PS[:, 4 + g, :], GW[:, g, :], XC[:, 0:SEQ], start=True, stop=True)
                    for g in range(2):
                        ins = mm(PS[:, 6, g * NB:(g + 1) * NB], GW[:, g, :], XC[:, SEQ:T], start=True, stop=True)
                    ins.then_inc(gates_ps, 1)

            pe.wait_ge(cum_ready, 3)
            step(0, True, False)
            with pe.Fori(1, NH) as i:
                step(i, True, True)
            step(NH, False, True)

            pe.wait_ge(merge_in, 1)
            new_s = PS[:, 5, 0:NH * NB]
            mm(new_s, ones[:, :], qcur[:, 0:64], start=True, stop=False)
            mm(new_s, ones[0:NB, :], qcur[0:NB, 64:128], start=False, stop=True)
            mm(PS[:, 6, 0:NH * NB], ones[:, :], DEN[:, :, :].rearrange("p h b -> p (h b)"), start=True, stop=True)\
                .then_inc(merge_ps, 1)
            pe.wait_ge(merge_in, 2)
            pe.wait_ge(pvs_ready, 1)
            pe.wait_ge(att_ready, NH)
            pe.wait_ge(lru_done, NL)
            for src, b0 in ((KS, 4), (VS, 6)):
                for h in range(NH):
                    tr(PS[0:NB, b0 + h // 4, (h % 4) * P:(h % 4 + 1) * P], src[:, h, :], ident[:, :])
            hr = (CW - 1) * NL * (NB + 1) // 2
            cv = CVALL[:, :, :].rearrange("p r n -> p (r n)")
            tr(PS[0:NL * (NB + 1), 2, 0:P], HALL[:, :, :].rearrange("p r n -> p (r n)"), ident[:, :])
            for g in range(2):
                ins = tr(PS[0:hr, 3, g * P:(g + 1) * P], cv[:, g * hr:(g + 1) * hr], ident[:, :])
            ins.then_inc(tail_t, 1)
            pe.wait_ge(tail_ready, 1)
            norm_sums(1, nbuf1, [(0, NH), (NH, KD)])
            pe.wait_ge(tail_rows, 1)
            pe.wait_ge(xl_ready, 2 * KD)
            with pe.Fori(0, KD // 2) as j:
                for s in range(2):
                    unit(U_O + s, j, U_O + s, j)
            norm_sums(2, nbuf1, [(0, KD)])
            pe.wait_ge(xl_ready, 3 * KD)
            with pe.Fori(0, NC) as c:
                with pe.Fori(0, CH // 2) as j:
                    for s in range(2):
                        unit(U_F + s, c * (UC // 2) + j, U_F + s, c * (TC // 2) + j)
                with pe.Fori(0, CH // 2) as j:
                    for s in range(2):
                        slot, w = at(U_F + CH + s, c * (UC // 2) + j)
                        pe.wait_ge(lo_done, 2 * w + slot + 1)
                        pe.wait_ge(sq_h_ready, CH * (c + 1))
                        for m in range(2):
                            pair, tw = at(U_F + CH + 2 * s + m, c * (TC // 2) + 2 * j)
                            pe.wait_ge(tile_out[pair], tw)
                            ins = products(HH, HL, lambda k: WH[slot][:, (2 * k + m) * P:(2 * k + m + 1) * P],
                                           lambda k: WL[slot][:, (2 * k + m) * P:(2 * k + m + 1) * P],
                                           [PS[:, 2 * pair + c, 0:HT] for c in range(2)], range(CH))
                            ins.then_inc(tile_done, 1)
            norm_sums(3, nbuf1, [(0, KD)])
            XN = nbuf1[1]
            for k in range(KD):
                pe.wait_ge(yn_ready, k + 1)
                if k >= 2:
                    pe.wait_ge(yt_ready[k % 2], k // 2)
                else:
                    pe.wait_ge(root_ready, 5)
                g = k // 4
                if k % 4 == 0 and g >= 2:
                    pe.wait_ge(ys_ready, g - 1)
                ins = tr(PS[0:NB, 6 + g % 2, (k % 4) * P:(k % 4 + 1) * P], XN[:, k % 2, SEQ:T], ident[:, :])
                if k % 4 == 3:
                    ins.then_inc(ys_t, 1)
                for j in range(TT):
                    ins = tr(PS[:, 4 + k % 2, j * P:(j + 1) * P], XN[:, k % 2, j * P:(j + 1) * P], ident[:, :])
                ins.then_inc(y_t, 1)


_INS = ['x_prompt', 'x_sample', 'cache_k', 'cache_v', 'cache_logf', 'state_conv', 'state_h', 'page_table',
        'g_mix', 'w_in', 'b_f', 'w_conv', 'b_conv', 'w_gate_a', 'b_gate_a', 'w_gate_x', 'b_gate_x', 'lru_lambda',
        'g_att_out', 'g_lru_out', 'w_out', 'g_ffn', 'w_up', 'w_down', 'g_final']


def kernel(**inputs):
    import numpy as np
    import concourse.bacc as bacc
    from concourse.bass_utils import run_bass_kernel_spmd

    a = {n: np.ascontiguousarray(inputs[n]) for n in _INS}
    B, S, D = a['x_prompt'].shape
    NB, S1 = a['x_sample'].shape[:2]
    L, _, _, H, HD = a['cache_k'].shape
    CW1, DL = a['state_conv'].shape[2:]
    outs = [(B, S, D), (NB, S1, D),
            (L, B, S, H, HD), (L, B, S, H, HD), (L, B, S, H), (L, B, CW1, DL), (L, B, DL),
            (L, NB, S1, H, HD), (L, NB, S1, H, HD), (L, NB, S1, H), (L, NB, CW1, DL), (L, NB, DL)]
    nc = bacc.Bacc("TRN2", target_bir_lowering=False, num_devices=1)
    args = [nc.dram_tensor(f"in_{n}", a[n].shape, mybir.dt.from_np(a[n].dtype), kind="ExternalInput").ap() for n in _INS]
    args += [nc.dram_tensor(f"out_{i}", s, F32, kind="ExternalOutput").ap() for i, s in enumerate(outs)]
    hymba_step(nc, *args)
    r = run_bass_kernel_spmd(nc, [{f"in_{n}": a[n] for n in _INS}], core_ids=[0])
    return tuple(r.results[0][f"out_{i}"] for i in range(len(outs)))
```

```python
from contextlib import ExitStack

import concourse.bass as bass
from concourse import mybir

F32 = mybir.dt.float32
F32R = mybir.dt.float32r
I32 = mybir.dt.int32
U32 = mybir.dt.uint32
ALU = mybir.AluOpType
ACT = mybir.ActivationFunctionType
AX = mybir.AxisListType
RED = bass.bass_isa.ReduceOp

P = 128
EPS = 1e-6
NEG = -1e30
LRU_C = 8.0


def hymba_step(nc, x_prompt, x_sample, cache_k, cache_v, cache_logf, state_conv, state_h, page_table,
               g_mix, w_in, b_f, w_conv, b_conv, w_gate_a, b_gate_a, w_gate_x, b_gate_x, lru_lambda,
               g_att_out, g_lru_out, w_out, g_ffn, w_up, w_down, g_final,
               y_prompt, y_sample, new_k_p, new_v_p, new_f_p, new_conv_p, new_h_p,
               new_k_s, new_v_s, new_f_s, new_conv_s, new_h_s):
    SEQ, D = x_prompt.shape[1], x_prompt.shape[2]
    NB = x_sample.shape[0]
    T = SEQ + NB
    HT = T // 2
    HB = SEQ - HT
    KD = D // P
    NH, HD = cache_k.shape[3], cache_k.shape[4]
    DA = NH * HD
    NL = (D - DA) // P
    NPG = page_table.shape[1]
    FF = w_up.shape[2]
    CW = w_conv.shape[1]
    TT = SEQ // P
    SCALE = float(HD) ** -0.5
    CH = 8
    NC = FF // P // CH
    NKS, NVS = 4, 4
    NHH = NH // 2
    LAG = 6
    assert HD == P and NH == NL == NB == CH == 8 and KD == 16 and T % 4 == 0 and NPG % 4 == 0 and TT == 4

    w_in_v = w_in[0].rearrange("(k p) c -> p k c", p=P)
    w_out_v = w_out[0].rearrange("(k p) c -> p k c", p=P)
    w_up_v = w_up[0].rearrange("(k p) c -> p k c", p=P)
    w_down_v = w_down[0].rearrange("(g k p) c -> g p k c", p=P, k=CH)
    k_pages = cache_k[0].rearrange("g p h d -> g p (h d)")
    v_pages = cache_v[0].rearrange("g p h d -> g p (h d)")
    COL_F, COL_X, COL_G = 3 * DA, 3 * DA + NH, 3 * DA + NH + NL * P

    U_Q, U_L = 1, 1 + NH
    U_O = U_L + 4 * NH
    U_F = U_O + KD
    UC = 2 * CH
    TC = CH + 2 * CH
    N_UNITS = U_F + NC * UC

    R_CONV, R_BCONV = 0, CW * NL
    R_BA, R_BX, R_LAM = R_BCONV + NL, R_BCONV + 2 * NL, R_BCONV + 3 * NL
    R_GATT, R_GLRU = R_LAM + NL, R_LAM + 2 * NL
    R_GMIX = R_GLRU + NL
    R_GFFN, R_GFIN = R_GMIX + KD, R_GMIX + 2 * KD
    assert R_GFIN + KD == P

    xT_spill = nc.dram_tensor("xT_spill", [P, KD, T], F32, kind="Internal").ap()

    with ExitStack() as ctx:
        def sb(name, shape, dt=F32, scope=ctx):
            return scope.enter_context(nc.sbuf_tensor(name, shape, dt))

        def sem(name):
            return ctx.enter_context(nc.semaphore(name))

        PS = ctx.enter_context(nc.psum_tensor("PS", [P, 8, 512], F32))

        A = sb("A", [P, KD, T])
        RAW = sb("RAW", [P, 2, 2048])
        WH = [sb(f"WH{s}", [P, 2048], F32R) for s in range(2)]
        WL = [sb(f"WL{s}", [P, 2048], F32R) for s in range(2)]
        ident = sb("ident", [P, P])
        ones = sb("ones", [P, P])
        PRM = sb("PRM", [P, P])

        first_scope, mix_scope, ffn_scope, x_scope = ExitStack(), ExitStack(), ExitStack(), ExitStack()
        XH = sb("XH", [P, KD, T], F32R, x_scope)
        XL = sb("XL", [P, KD, T], F32R, x_scope)
        loop_scope = ExitStack()
        PGT = sb("PGT", [1, NB * NPG], I32, loop_scope)
        SUF = sb("SUF", [P, NH, NB, NPG], scope=loop_scope)
        maskneg = sb("maskneg", [P, P], scope=loop_scope)
        FT = sb("FT", [P, TT, NH], scope=loop_scope)
        LS = sb("LS", [P, TT + 2, NH], scope=loop_scope)
        CPOS = sb("CPOS", [P, NL], scope=loop_scope)
        CNEG = sb("CNEG", [P, NL], scope=loop_scope)
        H0 = sb("H0", [P, NL, NB], scope=loop_scope)
        CST = sb("CST", [P, NL, NB * (CW - 1)], scope=loop_scope)

        XT = sb("XT", [P, TT, D], scope=first_scope)
        XS = sb("XS", [NB, D], scope=first_scope)
        PRW = sb("PRW", [P, P], scope=first_scope)
        XN0 = sb("XN0", [P, 2, T], scope=first_scope)
        RS0 = sb("RS0", [P, T], scope=first_scope)
        DG = sb("DG", [P, TT, P], scope=first_scope)
        DGS = sb("DGS", [NB, NB], scope=first_scope)
        MS0 = sb("MS0", [P, TT + 1], scope=first_scope)
        RK0 = sb("RK0", [P, TT + 1], scope=first_scope)
        first_scope.close()
        LG = sb("LG", [P, P, NH], scope=first_scope)
        LT = sb("LT", [P, NH, P], scope=first_scope)
        MT = sb("MT", [P, NH, P], scope=first_scope)
        SHW = sb("SHW", [NB, NL * P], scope=first_scope)
        SCW = sb("SCW", [NB * (CW - 1), NL * P], scope=first_scope)
        YH = sb("YH", [NH, T], scope=first_scope)
        IDX = sb("IDX", [P, 1], U32, first_scope)
        TOT = sb("TOT", [P, NH], scope=first_scope)
        low = sb("low", [P, P], scope=first_scope)
        tri = sb("tri", [P, P], scope=first_scope)
        later = sb("later", [P, P], scope=first_scope)
        YF = sb("YF", [P, TT + 2, NH], scope=first_scope)
        Z0, Z1, Z2 = (sb(f"Z{n}", [P, TT + 2, NH], scope=first_scope) for n in range(3))
        BF = sb("BF", [NH, 1], scope=first_scope)
        first_scope.close()

        KR = sb("KR", [P, NKS, NH * HD], scope=mix_scope)
        VR = sb("VR", [P, NVS, NHH * HD], scope=mix_scope)
        QB = sb("QB", [P, NH * HD], scope=mix_scope)
        QCOL = sb("QCOL", [P, NH], scope=mix_scope)
        GW = sb("GW", [P, 2, P], scope=mix_scope)
        qcur = sb("qcur", [P, SEQ], scope=mix_scope)
        kT = sb("kT", [P, SEQ], scope=mix_scope)
        AV = sb("AV", [P, NHH * HD], scope=mix_scope)
        ktok = qcur[:, :].rearrange("p (j d) -> p j d", j=TT)
        vtok = sb("vtok", [P, TT, HD], scope=mix_scope)
        PR = sb("PR", [P, 1280], scope=mix_scope)
        vT = PR[:, 0:SEQ]
        PT = sb("PT", [P, 1280], scope=mix_scope)
        XC = sb("XC", [P, T], scope=mix_scope)
        XW = sb("XW", [P, CW - 1 + SEQ + NB * CW], scope=mix_scope)
        SC = sb("SC", [P, NH, NPG], scope=mix_scope)
        KS = sb("KS", [P, NH, NB], scope=mix_scope)
        VS = sb("VS", [P, NH, NB], scope=mix_scope)
        MX = sb("MX", [P, NH, NB], scope=mix_scope)
        M8 = sb("M8", [P, NH], scope=mix_scope)
        MALL = sb("MALL", [P, NH], scope=mix_scope)
        NM = sb("NM", [P, TT], scope=mix_scope)
        NMS = sb("NMS", [P, TT], scope=mix_scope)
        SUMS = sb("SUMS", [P, TT], scope=mix_scope)
        RSUM = sb("RSUM", [P, TT], scope=mix_scope)
        HALL = sb("HALL", [P, 1 + NB, NL], scope=mix_scope)
        CVALL = sb("CVALL", [P, (1 + NB) * (CW - 1), NL], scope=mix_scope)
        mix_scope.close()
        loop_scope.close()

        kr = KR[:, :, :].rearrange("p s f -> p (s f)")
        NSQ, NXN, NRS, NMEAN = (kr[:, 0:2 * T].rearrange("p (s t) -> p s t", s=2), kr[:, 2 * T:4 * T].rearrange("p (s t) -> p s t", s=2),
                 kr[:, 4 * T:6 * T].rearrange("p (s t) -> p s t", s=2), kr[:, 6 * T:7 * T])
        DEN = kr[:, 7 * T:7 * T + NH * NB].rearrange("p (h b) -> p h b", h=NH)
        PVS = kr[:, 7 * T + NH * NB:7 * T + 2 * NH * NB].rearrange("p (h b) -> p h b", h=NH)
        KROW = VR[0:NB, 0:2, :].rearrange("p s f -> p (s f)")
        VROW = VR[0:NB, 2:4, :].rearrange("p s f -> p (s f)")

        SQ = sb("SQ", [P, 2, T], scope=ffn_scope)
        ACC = sb("ACC", [P, T], scope=ffn_scope)
        GA = sb("GA", [P, 2, T], scope=ffn_scope)
        RS = sb("RS", [P, T], scope=ffn_scope)
        RT = sb("RT", [P, 2, T], scope=ffn_scope)
        HF = sb("HF", [P, 2, T], scope=ffn_scope)
        MS = sb("MS", [P, TT + 1], scope=ffn_scope)
        RK = sb("RK", [P, TT + 1], scope=ffn_scope)
        HH = sb("HH", [P, CH, T], F32R, ffn_scope)
        HL = sb("HL", [P, CH, T], F32R, ffn_scope)
        ffn_scope.close()
        x_scope.close()
        YT = sb("YT", [P, TT, D])
        YS = sb("YS", [NB, D])
        raw_full = [sem(f"raw_full{s}") for s in range(2)]
        hi_done, lo_done = sem("hi_done"), sem("lo_done")
        tile_done = sem("tile_done")
        tile_out = [sem(f"tile_out{s}") for s in range(2)]
        consts_ready, table_in, xs_in = sem("consts_ready"), sem("table_in"), sem("xs_in")
        x_in = [sem(f"x_in{j}") for j in range(TT)]
        table_t, table_ready = sem("table_t"), sem("table_ready")
        x_t, x_ready = sem("x_t"), [sem(f"x_ready{s}") for s in range(2)]
        xs_t, xs_ready = sem("xs_t"), sem("xs_ready")
        ss0_clear, ss0_ready, ms0_ready, root0_ready = sem("ss0_clear"), sem("ss0_ready"), sem("ms0_ready"), sem("root0_ready")
        rk0_ready, dg_ready, rs0_ps, rs0_ready = sem("rk0_ready"), sem("dg_ready"), sem("rs0_ps"), sem("rs0_ready")
        spilled, respilled = sem("spilled"), sem("respilled")
        sq_ready, sq_used, ss_done, root_ready = sem("sq_ready"), sem("sq_used"), sem("ss_done"), sem("root_ready")
        xn_ready, xh_ready, xl_ready = sem("xn_ready"), sem("xh_ready"), sem("xl_ready")
        setup_in, gather_in, bf_in = sem("setup_in"), sem("gather_in"), sem("bf_in")
        masks_ready = sem("masks_ready")
        yh_ready, logit_t, state_t, past_t = sem("yh_ready"), sem("logit_t"), sem("state_t"), sem("past_t")
        absneg_ready, expneg_ready, logf_ready = sem("absneg_ready"), sem("expneg_ready"), sem("logf_ready")
        state_ready, past_ready, tot_ready = sem("state_ready"), sem("past_ready"), sem("tot_ready")
        cum_ps, suf_ps, cum_ready = sem("cum_ps"), sem("suf_ps"), sem("cum_ready")
        logf_out, pgt_in = sem("logf_out"), sem("pgt_in")
        qcol_ready, qb_ps, qb_ready = sem("qcol_ready"), sem("qb_ps"), sem("qb_ready")
        k_full = [sem(f"k_full{s}") for s in range(NKS)]
        v_full = [sem(f"v_full{s}") for s in range(NVS)]
        v_used0 = sem("v_used0")
        v_acc, v_summed = sem("v_acc"), sem("v_summed")
        pool_prod, k_scored, v_used = sem("pool_prod"), sem("k_scored"), sem("v_used")
        dve_prod = sem("dve_prod")
        qdf_ready, s_done, nm_ready, exp_done = sem("qdf_ready"), sem("s_done"), sem("nm_ready"), sem("exp_done")
        p_norm, pt_ps, pt_ready, att_ps, att_ready = sem("p_norm"), sem("pt_ps"), sem("pt_ready"), sem("att_ps"), sem("att_ready")
        ktr_ps, vtr_ps, ktok_ready, vtok_ready = sem("ktr_ps"), sem("vtr_ps"), sem("ktok_ready"), sem("vtok_ready")
        k_out, v_out = sem("k_out"), sem("v_out")
        gw_full, conv_done, gates_ps = sem("gw_full"), sem("conv_done"), sem("gates_ps")
        sig_done, decay_done, ratio_ready, root_done, lru_done = (
            sem("sig_done"), sem("decay_done"), sem("ratio_ready"), sem("root_done"), sem("lru_done"))
        m8_ready, mall_ready, shifted, pp_ready, pvs_ready = (
            sem("m8_ready"), sem("mall_ready"), sem("shifted"), sem("pp_ready"), sem("pvs_ready"))
        m8_seen = sem("m8_seen")
        merge_in, merge_ps, merge_sub, merge_exp, merged = (
            sem("merge_in"), sem("merge_ps"), sem("merge_sub"), sem("merge_exp"), sem("merged"))
        tail_t, tail_ready, tail_rows, tail_out = sem("tail_t"), sem("tail_ready"), sem("tail_rows"), sem("tail_out")
        tail_h = sem("tail_h")
        ms_read = sem("ms_read")
        acc_sq, acc_used, acc_zero = sem("acc_sq"), sem("acc_used"), sem("acc_zero")
        h_ready, hl_ready = sem("h_ready"), sem("hl_ready")
        yn_ready, y_t, yt_ready, ys_ready, y_out = (
            sem("yn_ready"), sem("y_t"), [sem(f"yt_ready{s}") for s in range(2)], [sem(f"ys_ready{s}") for s in range(2)],
            sem("y_out"))
        tok_ss, tok_ms, tok_root, tok_inv = sem("tok_ss"), sem("tok_ms"), sem("tok_root"), sem("tok_inv")
        y_scaled = [sem(f"y_scaled{s}") for s in range(2)]

        def at(n, half):
            return n % 2, n // 2 + half

        def out_of_banks(t):
            return [(tile_out[0], (t + 1) // 2), (tile_out[1], t // 2)]

        def one(i):
            return bass.ds(i, 1)

        def pair_view(pair):
            return PS[:, 2 * pair:2 * pair + 2, 0:HT]

        S_AT = [(4, 0), (4, 128), (5, 0), (6, 0)]
        P_AT = [0, 128, 384, 768]
        PT_BANK = [(4, 0), (5, 0), (6, 0), (6, 256)]
        PT_AT = [0, 512, 896, 1152]
        K_Q = NPG // 4
        last_halves = [(2, NPG - 8, v_acc, NPG // 2 * NB - 4), (3, NPG - 6, v_used0, NPG // 2 * NB),
                       (0, NPG - 4, v_used, NPG * NB - 1), (1, NPG - 2, v_used, NPG * NB)]

        mrg = [qcur[:, 64 * n:64 * n + 64].rearrange("p (h b) -> p h b", h=NH) for n in range(8)]
        merge_e = qcur[:, 5 * 64:7 * 64]

        block = ctx.enter_context(nc.Block())

        @block.sync
        def _(sp):
            def load_unit(n, half, src, peeled=False):
                slot, w = at(n, half)
                if not peeled:
                    sp.wait_ge(lo_done, 2 * w + slot - 1)
                for part in range(2):
                    load_part(slot, src, part)

            def load_part(slot, src, part):
                raw = RAW[:, slot, :].rearrange("p (k c) -> p k c", c=src.shape[2])
                n = src.shape[1] // 2
                ks = slice(part * n, (part + 1) * n)
                sp.dma_start(raw[:, ks, :], src[:, ks, :]).then_inc(raw_full[slot], 16)

            def cols(view, c):
                return view[:, :, bass.ds(c, P)]

            rows = [(w_conv[0], R_CONV), (b_conv, R_BCONV), (b_gate_a, R_BA), (b_gate_x, R_BX), (lru_lambda, R_LAM),
                    (g_att_out, R_GATT), (g_lru_out, R_GLRU), (g_mix, R_GMIX), (g_ffn, R_GFFN),
                    (g_final.rearrange("(a n) -> a n", a=1), R_GFIN)]
            sp.dma_start(XS[:, :], x_sample[:, 0, :]).then_inc(xs_in, 16)
            for j in range(TT):
                sp.dma_start(XT[:, j, :], x_prompt[0, j * P:(j + 1) * P, :]).then_inc(x_in[j], 16)
                for src, r in rows[3 * j:3 * j + 3]:
                    n = src.shape[0] * src.shape[1] // P
                    sp.dma_start(PRW[r:r + n, :], src.rearrange("a (n q) -> (a n) q", q=P)).then_inc(table_in, 16)
            load_unit(0, 0, cols(w_in_v, COL_F), True)
            sp.wait_ge(ss0_ready, 1)
            load_unit(1, 0, cols(w_in_v, 0), True)
            load_unit(2, 0, cols(w_in_v, P))
            sp.dma_start(PGT[:, :], page_table.rearrange("(a b) n -> a (b n)", a=1)).then_inc(pgt_in, 16)
            sp.wait_ge(x_ready[0], KD // 2)
            sp.wait_ge(x_ready[1], KD // 2)
            sp.wait_ge(xs_ready, 1)
            sp.dma_start(xT_spill, A[:, :, :]).then_inc(spilled, 16)
            sp.dma_start(SHW[:, :], state_h[0]).then_inc(setup_in, 16)
            sp.dma_start(SCW[:, :], state_conv[0].rearrange("b j c -> (b j) c")).then_inc(setup_in, 16)
            sp.dma_start(BF[:, :], b_f.rearrange("a h -> h a")).then_inc(bf_in, 16)
            load_unit(3, 0, cols(w_in_v, 2 * P))
            with sp.Fori(1, (NH - 2) // 2) as j:
                load_unit(2, j, cols(w_in_v, P * (2 * j + 1)))
                load_unit(3, j, cols(w_in_v, P * (2 * j + 2)))
            load_unit(U_Q + NH - 1, 0, cols(w_in_v, P * (NH - 1)))
            load_unit(U_L, 0, cols(w_in_v, DA))
            load_unit(U_L + 1, 0, cols(w_in_v, 2 * DA))
            sp.wait_ge(logf_ready, 1)
            sp.dma_start(new_f_p[0, 0].rearrange("(j p) h -> p j h", p=P), LS[:, 0:TT, :]).then_inc(logf_out, 16)
            sp.dma_start(new_f_s[0, :, 0, :], LS[0:NB, TT, :]).then_inc(logf_out, 16)
            sp.wait_ge(cum_ready, 3)
            sp.wait_ge(state_ready, 2)
            sp.wait_ge(pgt_in, 16)

            def step(i, head, prev, nxt, first_v=False):
                for q in range(4):
                    if head:
                        src = [lambda: cols(w_in_v, COL_X + P * i), lambda: cols(w_in_v, COL_G + P * i),
                               lambda: cols(w_in_v, DA + P * (i + 1)) if nxt else cols(w_out_v, 0),
                               lambda: cols(w_in_v, 2 * DA + P * (i + 1)) if nxt else cols(w_out_v, P)][q]()
                        slot, w = at(U_L + 2 + q, 2 * i)
                    if head and q == 1:
                        if prev:
                            sp.wait_ge(gates_ps, i)
                        sp.dma_start(GW[:, 0, :], w_gate_a[0, one(i), :, :].rearrange("a p c -> p (a c)")).then_inc(gw_full, 16)
                        sp.dma_start(GW[:, 1, :], w_gate_x[0, one(i), :, :].rearrange("a p c -> p (a c)")).then_inc(gw_full, 16)
                    for part in range(4):
                        if head:
                            if part == 0:
                                sp.wait_ge(lo_done, 2 * w + slot - 1)
                            if part % 2 == 0:
                                load_part(slot, src, part // 2)
                        if prev:
                            b = K_Q * q + part
                            value_half(i - 1, b, 1, first_v)
                            if b % 2:
                                value_half(i - 1, b, 0, first_v)
                            elif b >= LAG:
                                if head or b - LAG < NPG // 2:
                                    value_half(i - 1, b - LAG, 0, first_v)
                            elif not first_v:
                                value_half(i - 2, b + NPG - LAG, 0, False)

            def value_half(h, b, half, first):
                g = page(h, b)
                slot = b % 2 if half else 2 + b % 2
                if not first or b >= 2:
                    if half:
                        sp.wait_ge(v_used, NPG * h + b - 1)
                    else:
                        sp.wait_ge(v_used0 if b % 2 else v_acc, NPG // 2 * h + b // 2)
                sp.dma_start(VR[:, slot, :],
                             v_pages[one(g), :, half * NHH * HD:(half + 1) * NHH * HD].rearrange("a p f -> p (a f)"))\
                  .then_inc(v_full[slot], 16)

            def page(i, b):
                return sp.value_load(PGT[0:1, one(i * NPG + b)], min_val=0, max_val=cache_k.shape[1] - 1)

            step(0, True, False, True)
            step(1, True, True, True, True)
            with sp.Fori(2, NB - 1) as i:
                step(i, True, True, True)
            step(NB - 1, True, True, False)
            step(NB, False, True, False)
            for slot, b, used, count in last_halves:
                g = page(NB - 1, b)
                sp.wait_ge(used, count)
                sp.dma_start(VR[:, slot, :], v_pages[one(g), :, 0:NHH * HD].rearrange("a p f -> p (a f)")).then_inc(v_full[slot], 16)

            sp.wait_ge(xn_ready, KD + NL)
            sp.dma_start(A[:, NH:KD, :], xT_spill[:, NH:KD, :]).then_inc(respilled, 16)
            sp.wait_ge(tail_rows, 1)
            hr = (CW - 1) * NL
            sp.dma_start(new_h_p[0].rearrange("a (n q) -> (a n) q", q=P), QB[0:NL, 0:P]).then_inc(tail_out, 16)
            sp.dma_start(new_h_s[0].rearrange("a (n q) -> (a n) q", q=P), QB[NL:NL * (NB + 1), 0:P]).then_inc(tail_out, 16)
            cv_rows = new_conv_s[0].rearrange("b j (n q) -> (b j n) q", q=P)
            half = hr * (NB + 1) // 2
            sp.dma_start(new_conv_p[0].rearrange("b j (n q) -> (b j n) q", q=P), QB[0:hr, P:2 * P]).then_inc(tail_out, 16)
            sp.dma_start(cv_rows[0:half - hr, :], QB[hr:half, P:2 * P]).then_inc(tail_out, 16)
            sp.dma_start(cv_rows[half - hr:, :], QB[0:half, 2 * P:3 * P]).then_inc(tail_out, 16)
            sp.wait_ge(tail_ready, 1)
            sp.dma_start(new_k_s[0, :, 0, :, :].rearrange("b h d -> b (h d)"), KROW).then_inc(tail_out, 16)
            sp.dma_start(new_v_s[0, :, 0, :, :].rearrange("b h d -> b (h d)"), VROW).then_inc(tail_out, 16)
            for k in range(0, NH, 2):
                sp.wait_ge(xn_ready, KD + NL + k + 2)
                sp.dma_start(A[:, k:k + 2, :], xT_spill[:, k:k + 2, :]).then_inc(respilled, 16)
            with sp.Fori(0, (KD - 2) // 2) as j:
                load_unit(U_O + 2, j, cols(w_out_v, P * (2 * j + 2)))
                load_unit(U_O + 3, j, cols(w_out_v, P * (2 * j + 3)))
            with sp.Fori(0, NC) as c:
                with sp.Fori(0, CH // 2) as j:
                    load_unit(U_F, c * (UC // 2) + j, cols(w_up_v, P * (CH * c + 2 * j)))
                    load_unit(U_F + 1, c * (UC // 2) + j, cols(w_up_v, P * (CH * c + 2 * j + 1)))
                with sp.Fori(0, CH // 2) as j:
                    for s in range(2):
                        load_unit(U_F + CH + s, c * (UC // 2) + j,
                                  w_down_v[one(c), :, :, bass.ds(2 * P * (2 * j + s), 2 * P)].rearrange("a p k c -> p (a k) c"))
            for j in (0, 2, 1, 3):
                sp.wait_ge(y_scaled[j // 2], j % 2 + 1)
                sp.dma_start(y_prompt[0, j * P:(j + 1) * P, :], YT[:, j, :]).then_inc(y_out, 16)
            sp.wait_ge(y_scaled[0], 3)
            sp.dma_start(y_sample[:, 0, :], YS[:, :]).then_inc(y_out, 16)
            sp.wait_ge(y_out, (TT + 1) * 16)
            sp.wait_ge(logf_out, 2 * 16)
            sp.wait_ge(tail_out, 7 * 16)
            sp.wait_ge(k_out, NH * 16)
            sp.wait_ge(v_out, NH * 16)

        @block.gpsimd
        def _(pool):
            pool.memset(ident[:, :], 0.0).then_inc(consts_ready, 1)
            pool.memset(ones[:, :], 1.0).then_inc(consts_ready, 1)
            pool.memset(maskneg[:, :], 0.0).then_inc(consts_ready, 1)
            pool.wait_ge(consts_ready, 3)
            pool.affine_select(out=ident[:, :], in_=ident[:, :], compare_op=ALU.not_equal, fill=1.0, base=0,
                               pattern=[[-1, P]], channel_multiplier=1).then_inc(consts_ready, 1)
            pool.affine_select(out=maskneg[:, :], in_=maskneg[:, :], compare_op=ALU.is_ge, fill=NEG, base=0,
                               pattern=[[-1, P]], channel_multiplier=1).then_inc(consts_ready, 1)
            pool.wait_ge(x_t, KD)
            pool.wait_ge(xs_t, 1)
            pool.affine_select(out=low[:, :], in_=ones[:, :], compare_op=ALU.is_gt, fill=0.0, base=0,
                               pattern=[[-1, P]], channel_multiplier=1).then_inc(masks_ready, 1)
            pool.affine_select(out=tri[:, :], in_=ones[:, :], compare_op=ALU.is_ge, fill=0.0, base=0,
                               pattern=[[1, P]], channel_multiplier=-1).then_inc(masks_ready, 1)
            later_v = later[:, :].rearrange("p (b n) -> p b n", b=NB)
            pool.wait_ge(masks_ready, 2)
            pool.affine_select(out=later_v, in_=low[:, :].rearrange("p (b n) -> p b n", b=NB), compare_op=ALU.is_gt,
                               fill=0.0, base=NPG, pattern=[[NPG, NB], [0, NPG]], channel_multiplier=-1)\
                .then_inc(masks_ready, 1)
            pool.dma_start(IDX[:, :], page_table.rearrange("b (n a) -> (b n) a", a=1).bitcast(U32)).then_inc(gather_in, 16)
            pool.wait_ge(gather_in, 16)
            pool.indirect_dma_start(LG[:, :, :].rearrange("p k h -> p (k h)"), None,
                                    cache_logf[0].rearrange("g k h -> g (k h)"),
                                    bass.IndirectOffsetOnAxis(ap=IDX[:, 0:1], axis=0)).then_inc(gather_in, 16)

            def load_keys(i, b):
                g = pool.value_load(PGT[0:1, one(i * NPG + b)], min_val=0, max_val=cache_k.shape[1] - 1)
                pool.dma_start(KR[:, b % NKS, :], k_pages[one(g), :, :].rearrange("a p f -> p (a f)")).then_inc(k_full[b % NKS], 16)

            def step(i, first, last):
                for m in range(NPG // 2):
                    def loads():
                        for b in (2 * m + 2, 2 * m + 3):
                            if last and b >= NPG:
                                continue
                            if not first or b >= NKS:
                                pool.wait_ge(k_scored, NPG * i + b - NKS + 1)
                            load_keys(i, b)
                    loads()
                    if m == 0:
                        pool.wait_ge(qb_ready, i + 1)
                    b = 2 * m + 1
                    pool.wait_ge(k_full[b % NKS], 16 * (NPG // NKS * i + b // NKS + 1))
                    pool.tensor_tensor(KR[:, b % NKS, :], KR[:, b % NKS, :], QB[:, :], ALU.mult).then_inc(pool_prod, 1)
                pool.wait_ge(m8_ready, i + 1)
                pool.sem_inc(m8_seen, 1)
                pool.partition_all_reduce(MALL[:, :], M8[:, :], P, RED.max).then_inc(mall_ready, 1)
            pool.wait_ge(cum_ready, 3)
            pool.wait_ge(state_ready, 2)
            pool.wait_ge(pgt_in, 16)
            load_keys(0, 0)
            load_keys(0, 1)
            step(0, True, False)
            with pool.Fori(1, NB - 1) as i:
                step(i, False, False)
            step(NB - 1, False, True)

            def accumulate(n):
                with pool.Fori(0, KD // 2) as j:
                    for s in range(2):
                        g = KD * n + 2 * j + s
                        pool.wait_ge(acc_sq, g + 1)
                        pool.wait_ge(acc_used, g + 2)
                        pool.tensor_tensor(ACC[:, :], ACC[:, :], SQ[:, s, :], ALU.add).then_inc(acc_used, 1)

            pool.wait_ge(xl_ready, 2 * KD)
            pool.wait_ge(tail_out, 7 * 16)
            pool.wait_ge(k_out, 16 * NH)
            pool.wait_ge(v_out, 16 * NH)
            pool.wait_ge(logf_out, 2 * 16)
            pool.memset(ACC[:, :], 0.0).then_inc(acc_used, 2)
            accumulate(0)
            pool.wait_ge(ss_done, 3)
            pool.memset(ACC[:, :], 0.0).then_inc(acc_zero, 1)
            pool.wait_ge(acc_zero, 1)
            accumulate(1)

        @block.scalar
        def _(act):
            def split_hi(n, half, tiles=None, peeled=False):
                slot, w = at(n, half)
                act.wait_ge(raw_full[slot], 32 * (w + 1))
                if not peeled:
                    act.wait_ge(tile_done, 2 * w + slot - 1 if tiles is None else tiles)
                nc.scalar.activation(WH[slot][:, :], RAW[:, slot, :], ACT.Copy).then_inc(hi_done, 1)

            def tile_wait(n, half):
                slot, w = at(n, half)
                act.wait_ge(tile_done, 2 * w + slot + 1)
                return slot

            def squares(base, k0, k1, SQ):
                for k in range(k0, k1):
                    if base + k >= 2:
                        act.wait_ge(sq_used, base + k - 1)
                    nc.scalar.activation(SQ[:, k % 2, :], A[:, k, :], ACT.Square).then_inc(sq_ready, 1)

            def root(g, dst, banks, tiles):
                act.wait_ge(ss_done, g)
                nc.scalar.activation(dst.rearrange("p (a t) -> p a t", a=2), PS[:, banks:banks + 2, 0:HT],
                                     ACT.Sqrt, scale=1.0 / (P * tiles), bias=EPS).then_inc(root_ready, 1)

            def hi_parts(base, k0, k1, XN):
                with act.Fori(k0 // 2, k1 // 2) as j:
                    for s in range(2):
                        act.wait_ge(xn_ready, base + 2 * j + s + 1)
                        nc.scalar.activation(XH[:, one(2 * j + s), :], XN[:, s, :], ACT.Copy).then_inc(xh_ready, 1)

            act.wait_ge(ss0_clear, 1)
            act.wait_ge(xs_in, 16)
            nc.scalar.activation(RAW[0:NB, 1, :], XS[:, :], ACT.Square, accum_out=MS0[0:NB, TT:TT + 1])
            for j in range(TT):
                if j == TT - 1:
                    act.wait_ge(table_t, 1)
                    nc.scalar.activation(PRM[:, :], PS[:, 7, 0:P], ACT.Copy).then_inc(table_ready, 1)
                act.wait_ge(x_in[j], 16)
                act.drain()
                ins = nc.scalar.activation(RAW[:, 1, :], XT[:, j, :], ACT.Square, accum_out=MS0[:, j:j + 1])
            ins.then_inc(ss0_ready, 1)
            act.wait_ge(xs_t, 1)
            nc.scalar.activation(A[:, :, SEQ:T], PS[:, 6, 0:KD * NB].rearrange("p (k b) -> p k b", k=KD), ACT.Copy)\
                .then_inc(xs_ready, 1)

            def x_out(k):
                act.wait_ge(x_t, k + 1)
                nc.scalar.activation(A[:, k, 0:SEQ], PS[:, 4, :], ACT.Copy).then_inc(x_ready[0], 1)

            x_out(0)
            act.wait_ge(ms0_ready, 1)
            nc.scalar.activation(RK0[:, :], MS0[:, :], ACT.Sqrt).then_inc(root0_ready, 1)
            x_out(2)
            x_out(4)
            x_out(6)
            act.wait_ge(rs0_ps, 1)
            nc.scalar.activation(RS0[:, 0:SEQ], PS[:, 7, :], ACT.Copy)
            nc.scalar.activation(RS0[:, SEQ:T], PS[:, 6, KD * NB:(KD + 1) * NB], ACT.Copy).then_inc(rs0_ready, 1)
            split_hi(0, 0, peeled=True)
            for k in range(KD):
                if k % 2 == 0 and k + 8 < KD:
                    x_out(k + 8)
                if k == 4:
                    split_hi(1, 0, peeled=True)
                act.wait_ge(xn_ready, k + 1)
                nc.scalar.activation(XH[:, k, :], XN0[:, k % 2, :], ACT.Copy).then_inc(xh_ready, 1)

            def query_out(n, half, k):
                slot = tile_wait(n, half)
                nc.scalar.activation(A[:, one(k), :].rearrange("p a (c t) -> p (a c) t", c=2),
                                     pair_view(slot), ACT.Copy).then_inc(tile_out[slot], 1)

            split_hi(U_Q + 1, 0)
            act.wait_ge(spilled, 16)
            query_out(U_Q, 0, 0)
            split_hi(U_Q + 2, 0)
            act.wait_ge(absneg_ready, 1)
            nc.scalar.activation(Z1[:, :, :], Z0[:, :, :], ACT.Exp).then_inc(expneg_ready, 1)
            query_out(U_Q + 1, 0, 1)
            with act.Fori(0, NH // 2 - 2) as j:
                for s in range(2):
                    split_hi(U_Q + 3 + s, j)
                    query_out(U_Q + 2 + s, j, 2 * j + s + 2)
            for g in range(2):
                act.wait_ge(past_t, g + 1)
                nc.scalar.activation(LT[:, 4 * g:4 * g + 4, :], PS[:, 4 + g, :], ACT.Copy).then_inc(past_ready, 1)
            split_hi(U_L - 1, 0)
            query_out(U_L - 2, 0, NH - 2)
            for g in range(2):
                act.wait_ge(suf_ps, g + 1)
                nc.scalar.activation(SUF[:, 4 * g:4 * g + 4, :, :], PS[:, 4 + g, :].rearrange("p (h b n) -> p h b n", h=4, b=NB),
                                     ACT.Copy).then_inc(cum_ready, 1)
            act.wait_ge(cum_ps, 1)
            nc.scalar.activation(FT[:, :, :], PS[:, 6, 0:TT * NH].rearrange("p (j h) -> p j h", j=TT), ACT.Copy,
                                 scale=-1.0 / SCALE).then_inc(cum_ready, 1)
            split_hi(U_L, 0)
            query_out(U_L - 1, 0, NH - 1)
            act.wait_ge(state_ready, 2)

            def gates(h, after_sigmoids, between):
                act.wait_ge(gates_ps, h + 1)
                ba, bx = PRM[:, one(R_BA + h)], PRM[:, one(R_BX + h)]
                nc.scalar.activation(PR[:, 0:SEQ], PS[:, 4, :], ACT.Sigmoid, bias=ba)
                nc.scalar.activation(PR[:, SEQ:T], PS[:, 6, 0:NB], ACT.Sigmoid, bias=ba)
                nc.scalar.activation(PR[:, T:T + SEQ], PS[:, 5, :], ACT.Sigmoid, bias=bx)
                nc.scalar.activation(PR[:, T + SEQ:2 * T], PS[:, 6, NB:2 * NB], ACT.Sigmoid, bias=bx).then_inc(sig_done, 1)
                after_sigmoids()
                act.wait_ge(sig_done, h + 1)
                nc.scalar.activation(PT[:, 0:T], PR[:, 0:T], ACT.Tanh, scale=CPOS[:, one(h)])
                nc.scalar.activation(PR[:, 0:T], PR[:, 0:T], ACT.Exp, scale=CNEG[:, one(h)]).then_inc(decay_done, 1)
                between()
                act.wait_ge(ratio_ready, h + 1)
                nc.scalar.activation(PT[:, 0:T], PT[:, 0:T], ACT.Sqrt).then_inc(root_done, 1)

            def softmax(h):
                act.wait_ge(nm_ready, h + 1)
                for t in range(TT):
                    bank, c = S_AT[t]
                    n = (t + 1) * P
                    ins = nc.scalar.activation(PR[:, P_AT[t]:P_AT[t] + n], PS[:, bank, c:c + n], ACT.Exp,
                                               scale=SCALE, bias=NMS[:, t:t + 1], accum_out=SUMS[:, t:t + 1])
                ins.then_inc(exp_done, 1)

            def transposed(h):
                for n, (c0, c1, bank) in enumerate(((0, 512, 4), (512, 896, 5), (896, 1280, 6))):
                    act.wait_ge(pt_ps, 3 * h + n + 1)
                    nc.scalar.activation(PT[:, c0:c1], PS[:, bank, 0:c1 - c0], ACT.Copy).then_inc(pt_ready, 1)

            def attended(h):
                act.wait_ge(att_ps, h + 1)
                nc.scalar.activation(A[:, one(h), 0:SEQ].rearrange("p a t -> p (a t)"), PS[:, 4, :], ACT.Copy)\
                    .then_inc(att_ready, 1)

            def rows_out(full, dst, samples, i):
                nc.scalar.activation(dst[:, 0:HT], PS[:, 2 * full, 0:HT], ACT.Copy)
                nc.scalar.activation(dst[:, HT:SEQ], PS[:, 2 * full + 1, 0:HB], ACT.Copy)
                nc.scalar.activation(samples[:, one(i), :].rearrange("p a b -> p (a b)"), PS[:, 2 * full + 1, HB:HT], ACT.Copy)\
                    .then_inc(tile_out[full], 1)

            def step(i, head, prev):
                def broadcast_query():
                    if head:
                        act.wait_ge(qb_ps, i + 1)
                        if prev:
                            act.wait_ge(k_scored, NPG * i)
                        nc.scalar.activation(QB[:, :].rearrange("p (a n) -> p a n", a=2), PS[:, 4:6, :], ACT.Copy,
                                             scale=SCALE).then_inc(qb_ready, 1)

                def next_hi():
                    if head:
                        split_hi(U_L + 1, 2 * i)

                if prev:
                    gates(i - 1, next_hi, broadcast_query)
                else:
                    next_hi()
                    broadcast_query()
                if head:
                    slot = tile_wait(U_L, 2 * i)
                    split_hi(U_L + 2, 2 * i)
                    if prev:
                        act.wait_ge(s_done, i)
                    rows_out(slot, kT, KS, i)
                if prev:
                    softmax(i - 1)
                if prev:
                    transposed(i - 1)
                if head:
                    rows_out(tile_wait(U_L + 1, 2 * i), vT, VS, i)
                    split_hi(U_L + 3, 2 * i)
                if prev:
                    attended(i - 1)
                if head:
                    slot = tile_wait(U_L + 2, 2 * i)
                    if prev:
                        act.wait_ge(lru_done, i)
                    W3 = CW - 1
                    nc.scalar.activation(XW[:, W3:W3 + HT], PS[:, 2 * slot, 0:HT], ACT.Copy)
                    nc.scalar.activation(XW[:, W3 + HT:W3 + SEQ], PS[:, 2 * slot + 1, 0:HB], ACT.Copy)
                    nc.scalar.activation(XW[:, W3 + SEQ:].rearrange("p (b j) -> p b j", j=CW)[:, :, W3],
                                         PS[:, 2 * slot + 1, HB:HT], ACT.Copy).then_inc(tile_out[slot], 1)
                    split_hi(U_L + 4, 2 * i)
                    for tr, tok, ready, stored, bank, dst in ((ktr_ps, ktok, ktok_ready, k_out, 5, new_k_p),
                                                              (vtr_ps, vtok[:, :, :], vtok_ready, v_out, 6, new_v_p)):
                        act.wait_ge(tr, i + 1)
                        if prev:
                            act.wait_ge(stored, 16 * i)
                        nc.scalar.activation(tok, PS[:, bank, :].rearrange("p (j d) -> p j d", j=TT), ACT.Copy)\
                            .then_inc(ready, 1)
                        act.wait_ge(ready, i + 1)
                        act.dma_start(dst[0, 0, :, one(i), :].rearrange("(j p) a d -> p j (a d)", p=P), tok)\
                            .then_inc(stored, 16)
                    act.wait_ge(shifted, i + 1)
                    nc.scalar.activation(SUF[:, :, one(i), :].rearrange("p h a n -> p h (a n)"), SC[:, :, :], ACT.Exp)\
                        .then_inc(pp_ready, 1)
                    slot = tile_wait(U_L + 3, 2 * i)
                    nc.scalar.activation(PT[:, T:2 * T].rearrange("p (a t) -> p a t", a=2), pair_view(slot),
                                         ACT.Gelu_apprx_tanh).then_inc(tile_out[slot], 1)

            step(0, True, False)
            with act.Fori(1, NH) as i:
                step(i, True, True)
            step(NH, False, True)
            act.wait_ge(k_scored, NPG * NB)
            act.wait_ge(lru_done, NL)
            squares(-NH, NH, KD, NSQ)
            act.wait_ge(merge_sub, 1)
            nc.scalar.activation(merge_e[:, :], merge_e[:, :], ACT.Exp).then_inc(merge_exp, 1)
            root(1, NRS[:, 1, :], 0, NL)
            hi_parts(KD - NH, NH, KD, NXN)
            act.wait_ge(v_used, NPG * NB)
            act.wait_ge(v_summed, NB)
            nc.scalar.activation(PVS[:, :, :], PS[:, 7, 0:NB * NH].rearrange("p (b h) -> p h b", b=NB), ACT.Copy)\
                .then_inc(pvs_ready, 1)
            split_hi(U_O + 1, 0)
            act.wait_ge(tail_t, 1)
            nc.scalar.activation(KROW.rearrange("p (a n) -> p a n", a=2), PS[0:NB, 4:6, :], ACT.Copy)
            nc.scalar.activation(VROW.rearrange("p (a n) -> p a n", a=2), PS[0:NB, 6:8, :], ACT.Copy).then_inc(tail_ready, 1)
            act.wait_ge(merged, 1)
            act.wait_ge(att_ready, NH)
            squares(NL, 0, NH, NSQ)
            root(2, NRS[:, 0, :], 4, NH)
            hi_parts(KD + NL, 0, NH, NXN)

            def square_out(n, k, s, tile, tile_half):
                slot, w = at(tile, tile_half)
                act.wait_ge(tile_out[slot], w + 1)
                act.wait_ge(acc_used, KD * n + k + 1)
                nc.scalar.activation(SQ[:, s, :], A[:, one(k), :].rearrange("p a t -> p (a t)"), ACT.Square).then_inc(acc_sq, 1)

            square_out(0, 0, 0, U_O, 0)
            with act.Fori(0, KD // 2 - 1) as j:
                for s in range(2):
                    split_hi(U_O + 2 + s, j)
                    square_out(0, 2 * j + s + 1, 1 - s, U_O + 1 + s, j)
            split_hi(U_F, 0)
            square_out(0, KD - 1, 1, U_F - 1, 0)
            act.wait_ge(tile_done, U_F)
            with act.Fori(0, KD // 2) as j:
                for s in range(2):
                    nc.scalar.activation(XH[:, one(2 * j + s), :], A[:, one(2 * j + s), :], ACT.Copy,
                                         scale=PRM[:, one(R_GFFN + 2 * j + s)]).then_inc(xh_ready, 1)

            def up(c, j, first=False):
                for s in range(2):
                    split_hi(U_F + 1 + s, c * (UC // 2) + j, TC * c + 2 * j + (U_F + s))
                    if first and s == 0:
                        root(3, RS[:, :], 4, KD)
                    slot, w = at(U_F + s, c * (TC // 2) + j)
                    act.wait_ge(tile_out[slot], w + 1)
                    act.wait_ge(hl_ready, CH * c + 2 * j + s + 1)
                    nc.scalar.activation(HF[:, s, :], RT[:, s, :], ACT.Square)
                    act.drain()
                    nc.scalar.activation(HH[:, one(2 * j + s), :].rearrange("p a t -> p (a t)"), HF[:, s, :], ACT.Copy)\
                        .then_inc(h_ready, 1)

            def chunk(c, first=False):
                if first:
                    up(c, 0, True)
                with act.Fori(1 if first else 0, CH // 2) as j:
                    up(c, j)
                with act.Fori(0, CH // 2) as j:
                    for s in range(2):
                        split_hi(U_F + CH + 1 + s, c * (UC // 2) + j, TC * c + 4 * j + (U_F + CH + 2 * s))

            chunk(0, True)
            with act.Fori(1, NC - 1) as c:
                chunk(c)
            with act.Fori(0, CH // 2) as j:
                up(NC - 1, j)

            def y_rows(k):
                act.wait_ge(y_t, k + 3)
                nc.scalar.activation(YT[:, :, k * P:(k + 1) * P], PS[:, 4, :].rearrange("p (j f) -> p j f", j=TT), ACT.Copy)\
                    .then_inc(yt_ready[0], 1)

            def ys_rows(k):
                bank = 6 + k % 4 // 2
                act.wait_ge(y_t, k + 4)
                nc.scalar.activation(YS[:, k * P:(k + 2) * P], PS[0:NB, bank, 0:2 * P], ACT.Copy).then_inc(ys_ready[bank - 6], 1)

            for k in range(KD):
                if k % 2 == 0 and k < KD - 2:
                    n = k // 2
                    split_hi(U_F + CH + 1 + n, (NC - 1) * (UC // 2), TC * (NC - 1) + U_F + CH + 2 * n)
                square_out(1, k, k % 2, U_F + CH + k, (NC - 1) * (TC // 2))
                act.wait_ge(y_t, k + 1)
                nc.scalar.activation(GA[:, k % 2, :], A[:, k, :], ACT.Copy, scale=PRM[:, R_GFIN + k:R_GFIN + k + 1])\
                    .then_inc(yn_ready, 1)
                if k % 2:
                    y_rows(k - 1)
                if k % 4 == 3:
                    ys_rows(k - 3)
                if k % 4 == 1 and k > 1:
                    ys_rows(k - 3)
            act.wait_ge(tok_ms, 1)
            nc.scalar.activation(RK[:, :], MS[:, :], ACT.Sqrt).then_inc(tok_root, 1)
            ys_rows(KD - 2)
            act.wait_ge(yt_ready[0], KD // 2)
            act.wait_ge(yt_ready[1], KD // 2)
            act.wait_ge(ys_ready[0], KD // 4)
            act.wait_ge(ys_ready[1], KD // 4)
            act.wait_ge(tok_inv, 1)
            for j in range(2):
                nc.scalar.activation(YT[:, j, :], YT[:, j, :], ACT.Copy, scale=RK[:, j:j + 1]).then_inc(y_scaled[0], 1)
            nc.scalar.activation(YS[:, :], YS[:, :], ACT.Copy, scale=RK[0:NB, TT:TT + 1]).then_inc(y_scaled[0], 1)

        @block.vector
        def _(dve):
            V = nc.vector

            def split_lo(n, half):
                slot, w = at(n, half)
                dve.wait_ge(hi_done, 2 * w + slot + 1)
                V.tensor_tensor(WL[slot][:, :], RAW[:, slot, :], WH[slot][:, :].bitcast(F32), ALU.subtract)\
                    .then_inc(lo_done, 1)

            def tile_wait(n, half):
                slot, w = at(n, half)
                dve.wait_ge(tile_done, 2 * w + slot + 1)
                return slot

            def inverse(y, m):
                V.reciprocal(y, y)
                dve.drain()
                V.tensor_tensor(m, m, y, ALU.mult)
                dve.drain()
                V.scalar_tensor_tensor(m, m, -0.5, y, ALU.mult, ALU.mult)
                dve.drain()
                return V.scalar_tensor_tensor(y, m, 1.5, y, ALU.add, ALU.mult)

            def inverse_root(g, y, m, banks, tiles):
                dve.wait_ge(root_ready, g)
                V.tensor_scalar(m.rearrange("p (a t) -> p a t", a=2), PS[:, banks:banks + 2, 0:HT], 1.0 / (P * tiles), EPS,
                                ALU.mult, ALU.add).then_inc(ms_read, 1)
                return inverse(y, m)

            def add_tile(k, tile, tile_half):
                slot = tile_wait(tile, tile_half)
                a = A[:, one(k), :].rearrange("p a (c t) -> p (a c) t", c=2)
                V.tensor_tensor(a, pair_view(slot), a, ALU.add).then_inc(tile_out[slot], 1)

            def normalize(base, k0, k1, XN, y, col):
                dve.drain()
                with dve.Fori(k0 // 2, k1 // 2) as j:
                    dve.wait_ge(xl_ready, base + 2 * j)
                    for s in range(2):
                        k = 2 * j + s
                        V.scalar_tensor_tensor(XN[:, s, :], A[:, one(k), :].rearrange("p a t -> p (a t)"),
                                               PRM[:, one(col + k)], y, ALU.mult, ALU.mult).then_inc(xn_ready, 1)
                    for s in range(2):
                        k = 2 * j + s
                        dve.wait_ge(xh_ready, base + k + 1)
                        V.tensor_tensor(XL[:, one(k), :].rearrange("p a t -> p (a t)"), XN[:, s, :],
                                        XH[:, one(k), :].rearrange("p a t -> p (a t)").bitcast(F32), ALU.subtract)\
                            .then_inc(xl_ready, 1)

            V.memset(MS0[:, :], 1.0).then_inc(ss0_clear, 1)

            def x_out(k):
                dve.wait_ge(x_t, k + 1)
                V.tensor_copy(A[:, k, 0:SEQ], PS[:, 5, :]).then_inc(x_ready[1], 1)

            dve.wait_ge(ss0_ready, 1)
            V.tensor_scalar(MS0[:, :], MS0[:, :], 1.0 / D, EPS, ALU.mult, ALU.add).then_inc(ms0_ready, 1)
            x_out(1)
            dve.wait_ge(root0_ready, 1)
            inverse(RK0[:, :], MS0[:, :]).then_inc(rk0_ready, 1)
            dve.wait_ge(rk0_ready, 1)
            V.tensor_tensor(DG[:, :, :], ident[:, :].unsqueeze(1).to_broadcast([P, TT, P]),
                            RK0[:, 0:TT].unsqueeze(2).to_broadcast([P, TT, P]), ALU.mult)
            V.tensor_scalar(DGS[:, :], ident[0:NB, 0:NB], RK0[0:NB, TT:TT + 1], None, ALU.mult).then_inc(dg_ready, 1)
            x_out(3)
            x_out(5)
            x_out(7)
            split_lo(0, 0)
            dve.wait_ge(rs0_ready, 1)
            dve.wait_ge(table_ready, 1)
            dve.wait_ge(xs_ready, 1)
            for k in range(0, KD, 2):
                if k + 9 < KD:
                    x_out(k + 9)
                if k == 6:
                    split_lo(1, 0)
                dve.wait_ge(x_ready[0], k // 2 + 1)
                if k:
                    dve.wait_ge(xl_ready, k)
                for n in (k, k + 1):
                    V.scalar_tensor_tensor(XN0[:, n % 2, :], A[:, n, :], PRM[:, R_GMIX + n:R_GMIX + n + 1], RS0[:, :],
                                           ALU.mult, ALU.mult).then_inc(xn_ready, 1)
                for n in (k, k + 1):
                    dve.wait_ge(xh_ready, n + 1)
                    V.tensor_tensor(XL[:, n, :], XN0[:, n % 2, :], XH[:, n, :].bitcast(F32), ALU.subtract).then_inc(xl_ready, 1)
            split_lo(U_Q + 1, 0)

            V.memset(YF[:, :, :], 0.0)
            slot = tile_wait(0, 0)
            dve.wait_ge(bf_in, 16)
            V.tensor_scalar(YH[:, :].rearrange("p (a t) -> p a t", a=2), pair_view(slot)[0:NH], BF[:, 0:1], None, ALU.add)\
                .then_inc(tile_out[slot], 1)
            dve.drain()
            V.tensor_copy(YF[:, TT + 1, :], PRM[:, R_LAM:R_LAM + NL]).then_inc(yh_ready, 1)
            split_lo(U_Q + 2, 0)
            dve.wait_ge(logit_t, 1)
            V.tensor_copy(YF[:, 0:TT, :], PS[:, 4, 0:TT * NH].rearrange("p (j h) -> p j h", j=TT))
            V.tensor_copy(YF[0:NB, TT, :], PS[0:NB, 4, TT * NH:(TT + 1) * NH])
            dve.drain()
            V.scalar_tensor_tensor(Z0[:, :, :], YF[:, :, :], -1.0, YF[:, :, :], ALU.mult, ALU.min).then_inc(absneg_ready, 1)
            dve.wait_ge(expneg_ready, 1)
            V.tensor_scalar(Z0[:, :, :], Z1[:, :, :], 2.0, None, ALU.add)
            dve.drain()
            V.reciprocal(Z0[:, :, :], Z0[:, :, :])
            dve.drain()
            V.tensor_tensor(Z1[:, :, :], Z1[:, :, :], Z0[:, :, :], ALU.mult)
            dve.drain()
            V.tensor_tensor(Z0[:, :, :], Z1[:, :, :], Z1[:, :, :], ALU.mult)
            dve.drain()
            V.tensor_scalar(Z2[:, :, :], Z0[:, :, :], 2.0 / 17, None, ALU.mult)
            for n in range(15, 1, -2):
                dve.drain()
                V.scalar_tensor_tensor(Z2[:, :, :], Z2[:, :, :], 2.0 / n, Z0[:, :, :], ALU.add, ALU.mult)
            dve.drain()
            V.scalar_tensor_tensor(Z2[:, :, :], Z2[:, :, :], 2.0, Z1[:, :, :], ALU.add, ALU.mult)
            dve.drain()
            V.scalar_tensor_tensor(LS[:, :, :], YF[:, :, :], 0.0, Z2[:, :, :], ALU.min, ALU.subtract).then_inc(logf_ready, 1)
            dve.drain()
            V.tensor_scalar(CPOS[:, :], LS[:, TT + 1, :], -LRU_C, None, ALU.mult)
            V.tensor_scalar(CNEG[:, :], LS[:, TT + 1, :], LRU_C, None, ALU.mult).then_inc(logf_ready, 1)
            dve.wait_ge(state_t, 1)
            V.tensor_copy(H0[:, :, :], PS[:, 7, 0:NL * NB].rearrange("p (n b) -> p n b", n=NL)).then_inc(state_ready, 1)
            V.tensor_copy(CST[:, :, :], PS[:, 7, NL * NB:NL * NB * CW].rearrange("p (n r) -> p n r", n=NL))\
                .then_inc(state_ready, 1)
            dve.wait_ge(gather_in, 32)
            V.tensor_reduce(TOT[:, :], LG[:, :, :].rearrange("p k h -> p h k"), AX.X, ALU.add)
            dve.drain()
            dve.wait_ge(masks_ready, 3)
            V.tensor_tensor(MT[:, :, :], later[:, :].unsqueeze(1).to_broadcast([P, NH, P]),
                            TOT[:, :].unsqueeze(2).to_broadcast([P, NH, P]), ALU.mult).then_inc(tot_ready, 1)
            with dve.Fori(0, NH // 2 - 1) as j:
                for s in range(2):
                    split_lo(U_Q + 3 + s, j)
            dve.wait_ge(cum_ready, 3)
            V.memset(XW[:, 0:CW - 1], 0.0)

            def score(i, pages):
                for b in pages:
                    if b % 2:
                        dve.wait_ge(pool_prod, NPG // 2 * i + b // 2 + 1)
                    else:
                        dve.wait_ge(k_full[b % NKS], 16 * (NPG // NKS * i + b // NKS + 1))
                        V.tensor_tensor(KR[:, b % NKS, :], KR[:, b % NKS, :], QB[:, :], ALU.mult).then_inc(dve_prod, 1)
                        dve.wait_ge(dve_prod, NPG // 2 * i + b // 2 + 1)
                    V.tensor_reduce(SC[:, :, b], KR[:, b % NKS, :].rearrange("p (h d) -> p h d", h=NH), AX.X, ALU.add)\
                        .then_inc(k_scored, 1)

            def add_values(h, pages, first=False):
                for b in pages:
                    if b == 0:
                        dve.wait_ge(pp_ready, h + 1)
                        if not first:
                            dve.wait_ge(v_summed, h)
                    else:
                        dve.wait_ge(v_acc, NPG // 2 * h + b // 2)
                    dve.wait_ge(v_full[2], 16 * (NPG // 2 * h + b // 2 + 1))
                    for n in range(NHH):
                        cols = slice(n * HD, (n + 1) * HD)
                        p = SUF[:, n, one(h), b]
                        if b == 0:
                            ins = V.tensor_scalar(AV[:, cols], VR[:, 2, cols], p, None, ALU.mult)
                        else:
                            ins = V.scalar_tensor_tensor(AV[:, cols], VR[:, 2, cols], p, AV[:, cols], ALU.mult, ALU.add)
                    ins.then_inc(v_acc, 1)

            def recurrence(h, meanwhile):
                R, I, TH, U = PR[:, 0:T], PR[:, T:2 * T], PT[:, 0:T], XW[:, CW - 1:CW - 1 + T]
                dve.wait_ge(sig_done, h + 1)
                V.tensor_tensor(I, I, XC[:, :], ALU.mult)
                dve.wait_ge(decay_done, h + 1)
                V.tensor_tensor(U, R, R, ALU.mult)
                dve.drain()
                V.scalar_tensor_tensor(TH, U, 1.0, TH, ALU.add, ALU.mult).then_inc(ratio_ready, 1)
                meanwhile()
                dve.wait_ge(root_done, h + 1)
                V.tensor_tensor(I, I, TH, ALU.mult)
                dve.drain()
                V.tensor_tensor_scan(XC[:, 0:SEQ], PR[:, 0:SEQ], PR[:, T:T + SEQ], 0.0, ALU.mult, ALU.add)
                V.tensor_tensor(XC[:, SEQ:T], PR[:, SEQ:T], H0[:, one(h), :].rearrange("p a b -> p (a b)"), ALU.mult)
                dve.drain()
                V.tensor_tensor(XC[:, SEQ:T], XC[:, SEQ:T], PR[:, T + SEQ:2 * T], ALU.add)
                dve.drain()
                dve.wait_ge(tile_out[0], at(U_L + 3, 2 * h)[1] + 1)
                V.tensor_copy(HALL[:, :, one(h)].rearrange("p r a -> p (r a)"), XC[:, SEQ - 1:T])
                V.tensor_tensor(A[:, one(NH + h), :].rearrange("p a t -> p (a t)"), XC[:, :], PT[:, T:2 * T], ALU.mult)\
                    .then_inc(lru_done, 1)

            def conv(i):
                V.tensor_copy(XW[:, CW - 1 + SEQ:].rearrange("p (b j) -> p b j", j=CW)[:, :, 0:CW - 1],
                              CST[:, one(i), :].rearrange("p a (b j) -> p (a b) j", b=NB))
                dve.drain()
                dve.wait_ge(tile_out[1], at(U_L + 2, 2 * i)[1] + 1)
                tails = XW[:, CW - 1 + SEQ:].rearrange("p (b j) -> p b j", j=CW)
                for j in range(CW):
                    w = PRM[:, one(R_CONV + j * NL + i)]
                    for dst, src in ((XC[:, 0:SEQ], XW[:, j:j + SEQ]), (XC[:, SEQ:T], tails[:, :, j])):
                        if j == 0:
                            V.tensor_scalar(dst, src, w, PRM[:, one(R_BCONV + i)], ALU.mult, ALU.add)
                        else:
                            ins = V.scalar_tensor_tensor(dst, src, w, dst, ALU.mult, ALU.add)
                    dve.drain()
                V.tensor_copy(CVALL[:, 0:CW - 1, one(i)].rearrange("p r a -> p (r a)"), XW[:, SEQ:SEQ + CW - 1])
                V.tensor_copy(CVALL[:, CW - 1:, one(i)].rearrange("p (b j) a -> p b (j a)", b=NB), tails[:, :, 1:CW])\
                    .then_inc(conv_done, 1)

            def step(i, head, prev, older=True):
                h = i - 1

                def add(pages):
                    if prev:
                        add_values(h, pages, not older)

                def add_older(pages):
                    if prev and older:
                        add_values(h - 1, pages)

                if head:
                    if not prev:
                        split_lo(U_L + 1, 0)
                        for s, v in out_of_banks(U_L):
                            dve.wait_ge(s, v)
                    V.tensor_copy(QCOL[:, :], A[:, 0:NH, SEQ + i] if isinstance(i, int) else
                                  A[:, 0:NH, one(SEQ + i)].rearrange("p h a -> p (h a)")).then_inc(qcol_ready, 1)
                add_older([10])
                if prev:
                    recurrence(h, lambda: split_lo(U_L + 1, 2 * i) if head else None)
                    V.tensor_tensor(PT[:, 0:SEQ].rearrange("p (j k) -> p j k", j=TT), ident[:, :].unsqueeze(1).to_broadcast([P, TT, P]),
                                    FT[:, :, one(h)].to_broadcast([P, TT, P]), ALU.mult)
                    dve.wait_ge(k_out, 16 * i)
                    V.tensor_copy(qcur[:, :], A[:, one(h), 0:SEQ].rearrange("p a t -> p (a t)")).then_inc(qdf_ready, 1)
                add_older([12])
                if head:
                    dve.wait_ge(qb_ready, i + 1)
                    score(i, range(0, 2))
                add_older([14])
                if head:
                    score(i, range(2, 4))
                    split_lo(U_L + 2, 2 * i)
                if prev:
                    dve.wait_ge(s_done, h + 1)
                    for t in range(TT):
                        bank, c = S_AT[t]
                        V.tensor_reduce(NM[:, t:t + 1], PS[:, bank, c:c + (t + 1) * P], AX.X, ALU.max, negate=True)
                    dve.drain()
                    V.tensor_scalar(NMS[:, :], NM[:, :], SCALE, None, ALU.mult).then_inc(nm_ready, 1)
                if head:
                    score(i, range(4, 6))
                add([0])
                if prev:
                    dve.wait_ge(exp_done, h + 1)
                    V.reciprocal(RSUM[:, :], SUMS[:, :])
                    dve.drain()
                    for t in range(TT):
                        row = PR[:, P_AT[t]:P_AT[t] + (t + 1) * P]
                        ins = V.tensor_scalar(row, row, RSUM[:, t:t + 1], None, ALU.mult)
                    ins.then_inc(p_norm, 1)
                if head:
                    score(i, range(6, 8))
                add([2])
                if head:
                    if prev:
                        score(i, range(8, 10))
                    split_lo(U_L + 3, 2 * i)
                    if not prev:
                        score(i, range(8, 10))
                add([4])
                if head:
                    score(i, range(10, 12))
                add([6])
                if head:
                    if prev:
                        score(i, range(12, 14))
                    conv(i)
                    split_lo(U_L + 4, 2 * i)
                    if not prev:
                        score(i, range(12, 14))
                if head:
                    score(i, range(14, NPG))
                    dve.drain()
                    V.tensor_tensor(SC[:, :, :], SC[:, :, :], SUF[:, :, one(i), :].rearrange("p h a n -> p h (a n)"), ALU.add)
                    dve.drain()
                    V.tensor_reduce(M8[:, :], SC[:, :, :], AX.X, ALU.max).then_inc(m8_ready, 1)
                    dve.wait_ge(mall_ready, i + 1)
                    V.tensor_copy(MX[:, :, one(i)].rearrange("p h a -> p (h a)"), MALL[:, :])
                    V.tensor_tensor(SC[:, :, :], SC[:, :, :], MALL[:, :].unsqueeze(2).to_broadcast([P, NH, NPG]), ALU.subtract)\
                        .then_inc(shifted, 1)
                if head:
                    add([8])

            step(0, True, False)
            step(1, True, True, False)
            with dve.Fori(2, NH) as i:
                step(i, True, True)
            step(NH, False, True)
            dve.wait_ge(pp_ready, NB)
            V.tensor_reduce(DEN[:, :, :], SUF[:, :, :, :], AX.X, ALU.add)

            prod, lfd, SN, DR, MM = mrg[0:5]
            E1, E2 = mrg[5:7]
            tmp = mrg[7]
            q_s = A[:, 0:NH, SEQ:T]
            dve.wait_ge(s_done, NH)
            dve.wait_ge(k_out, 16 * NH)
            V.tensor_tensor(prod, q_s, KS[:, :, :], ALU.mult)
            V.tensor_tensor(lfd[0:NB], LS[0:NB, TT, :].unsqueeze(2).to_broadcast([NB, NH, NB]),
                            ident[0:NB, 0:NB].unsqueeze(1).to_broadcast([NB, NH, NB]), ALU.mult)
            dve.drain()
            V.tensor_scalar(lfd[0:NB], lfd[0:NB], -1.0 / SCALE, None, ALU.mult).then_inc(merge_in, 1)
            hr = (CW - 1) * NL * (NB + 1) // 2
            dve.wait_ge(tail_h, 1)
            V.tensor_copy(QB[0:NL * (NB + 1), 0:P], PS[0:NL * (NB + 1), 5, 0:P])
            V.tensor_copy(QB[0:hr, P:3 * P], PS[0:hr, 5, P:3 * P]).then_inc(tail_rows, 1)
            dve.wait_ge(merge_ps, 1)
            V.tensor_scalar(SN, PS[:, 4, 0:NH * NB].rearrange("p (h b) -> p h b", h=NH), SCALE, None, ALU.mult)
            V.tensor_copy(DR, PS[:, 6, 0:NH * NB].rearrange("p (h b) -> p h b", h=NH)).then_inc(merge_in, 1)
            dve.drain()
            V.tensor_tensor(MM, MX[:, :, :], SN, ALU.max)
            dve.drain()
            V.tensor_tensor(E1, MX[:, :, :], MM, ALU.subtract)
            V.tensor_tensor(E2, SN, MM, ALU.subtract).then_inc(merge_sub, 1)
            inverse_root(1, NRS[:, 1, :], NMEAN, 0, NL)
            normalize(KD - NH, NH, KD, NXN, NRS[:, 1, :], R_GATT)
            split_lo(U_O + 1, 0)
            dve.wait_ge(merge_exp, 1)
            dve.wait_ge(pvs_ready, 1)
            V.tensor_tensor(DR, DR, E1, ALU.mult)
            V.tensor_tensor(prod, PVS[:, :, :], E1, ALU.mult)
            V.tensor_tensor(tmp, VS[:, :, :], E2, ALU.mult)
            dve.drain()
            V.tensor_tensor(DR, DR, E2, ALU.add)
            V.tensor_tensor(prod, prod, tmp, ALU.add)
            dve.drain()
            V.reciprocal(DR, DR)
            dve.drain()
            V.tensor_tensor(q_s, prod, DR, ALU.mult).then_inc(merged, 1)
            inverse_root(2, NRS[:, 0, :], NMEAN, 4, NH)
            normalize(KD + NL, 0, NH, NXN, NRS[:, 0, :], R_GATT)
            dve.wait_ge(respilled, 16 * (1 + NH // 2))
            add_tile(0, U_O, 0)
            with dve.Fori(0, KD // 2 - 1) as j:
                for s in range(2):
                    split_lo(U_O + 2 + s, j)
                    add_tile(2 * j + s + 1, U_O + 1 + s, j)
            split_lo(U_F, 0)
            add_tile(KD - 1, U_F - 1, 0)
            with dve.Fori(0, KD // 2) as j:
                for s in range(2):
                    k = 2 * j + s
                    dve.wait_ge(xh_ready, 2 * KD + k + 1)
                    V.scalar_tensor_tensor(XL[:, one(k), :].rearrange("p a t -> p (a t)"), A[:, one(k), :].rearrange("p a t -> p (a t)"),
                                           PRM[:, one(R_GFFN + k)], XH[:, one(k), :].rearrange("p a t -> p (a t)").bitcast(F32),
                                           ALU.mult, ALU.subtract).then_inc(xl_ready, 1)
            dve.sem_inc(hl_ready, 2)

            def up(c, j, first=False):
                for s in range(2):
                    split_lo(U_F + 1 + s, c * (UC // 2) + j)
                    if first and s == 0:
                        inverse_root(3, RS[:, :], GA[:, 0, :], 4, KD)
                        dve.drain()
                    slot = tile_wait(U_F + s, c * (TC // 2) + j)
                    V.scalar_tensor_tensor(RT[:, s, :].rearrange("p (a t) -> p a t", a=2), pair_view(slot), 0.0,
                                           RS[:, :].rearrange("p (a t) -> p a t", a=2), ALU.max, ALU.mult)\
                        .then_inc(tile_out[slot], 1)
                    dve.wait_ge(h_ready, CH * c + 2 * j + s + 1)
                    V.tensor_tensor(HL[:, one(2 * j + s), :].rearrange("p a t -> p (a t)"), HF[:, s, :],
                                    HH[:, one(2 * j + s), :].rearrange("p a t -> p (a t)").bitcast(F32), ALU.subtract)\
                        .then_inc(hl_ready, 1)

            def chunk(c, first=False):
                if first:
                    up(c, 0, True)
                with dve.Fori(1 if first else 0, CH // 2) as j:
                    up(c, j)
                with dve.Fori(0, CH // 2) as j:
                    for s in range(2):
                        split_lo(U_F + CH + 1 + s, c * (UC // 2) + j)
                        for m in range(2):
                            add_tile(4 * j + 2 * s + m, U_F + CH + 2 * s + m, c * (TC // 2) + 2 * j)

            chunk(0, True)
            with dve.Fori(1, NC - 1) as c:
                chunk(c)
            with dve.Fori(0, CH // 2) as j:
                up(NC - 1, j)

            def y_rows(k):
                dve.wait_ge(y_t, k + 3)
                V.tensor_copy(YT[:, :, k * P:(k + 1) * P], PS[:, 5, :].rearrange("p (j f) -> p j f", j=TT)).then_inc(yt_ready[1], 1)

            V.memset(MS[:, :], 1.0)
            for k in range(KD):
                if k % 2 == 0 and k < KD - 2:
                    split_lo(U_F + CH + 1 + k // 2, (NC - 1) * (UC // 2))
                add_tile(k, U_F + CH + k, (NC - 1) * (TC // 2))
                if k % 2 == 0 and k:
                    y_rows(k - 1)
            dve.drain()
            dve.wait_ge(tok_ss, 1)
            V.tensor_scalar(MS[:, 0:TT], PS[:, 6, 2 * P:2 * P + TT], 1.0 / D, EPS, ALU.mult, ALU.add)
            V.tensor_scalar(MS[0:NB, TT:TT + 1], PS[0:NB, 6, 2 * P + TT:2 * P + TT + 1], 1.0 / D, EPS, ALU.mult, ALU.add)\
                .then_inc(tok_ms, 1)
            y_rows(KD - 1)
            dve.wait_ge(tok_root, 1)
            inverse(RK[:, :], MS[:, :]).then_inc(tok_inv, 1)
            dve.wait_ge(tok_inv, 1)
            dve.wait_ge(yt_ready[0], KD // 2)
            dve.wait_ge(yt_ready[1], KD // 2)
            for j in range(2, TT):
                V.tensor_scalar(YT[:, j, :], YT[:, j, :], RK[:, j:j + 1], None, ALU.mult).then_inc(y_scaled[1], 1)

        @block.tensor
        def _(pe):
            mm = nc.tensor.matmul

            def products(xh, xl, wh, wl, dsts, kts, insert={}, first=True, last=True, ready=None):
                for n, k in enumerate(kts):
                    if ready and n in ready:
                        pe.wait_ge(*ready[n])
                    for x in (xh, xl):
                        for c in range(2):
                            mm(dsts[c], wh(k), x[:, k, c * HT:(c + 1) * HT], start=first and n == 0 and x is xh, stop=False)
                    for f in insert.get(2 * n, ()):
                        f()
                    for c in range(2):
                        ins = mm(dsts[c], wl(k), xh[:, k, c * HT:(c + 1) * HT], start=False, stop=last and n == len(kts) - 1)
                    if n < len(kts) - 1:
                        for f in insert.get(2 * n + 1, ()):
                            f()
                return ins

            def unit(n, half, tile, tile_half, insert={}, kts=range(KD), first=True, last=True, ready=None):
                slot, w = at(n, half)
                pair, tw = at(tile, tile_half)
                if first:
                    pe.wait_ge(lo_done, 2 * w + slot + 1)
                    if not (isinstance(tw, int) and tw == 0):
                        pe.wait_ge(tile_out[pair], tw)
                ins = products(XH, XL, lambda k: WH[slot][:, k * P:(k + 1) * P], lambda k: WL[slot][:, k * P:(k + 1) * P],
                               [PS[:, 2 * pair + c, 0:HT] for c in range(2)], kts, insert, first, last, ready)
                if last:
                    ins.then_inc(tile_done, 1)
                for f in insert.get(2 * KD - 1, ()):
                    f()

            def unit_pair(n, kts, base, first=True, last=True, lag=4):
                for t in range(len(kts) + lag):
                    for m, i in ((n, t), (n + 1, t - lag)):
                        if 0 <= i < len(kts):
                            unit(m, 0, m, 0, kts=[kts[i]], ready={0: (xl_ready, base + kts[i] + 1)},
                                 first=first and i == 0, last=last and i == len(kts) - 1)

            def norm_sums(base, k0, k1, SQ, banks):
                for k in range(k0, k1):
                    pe.wait_ge(sq_ready, base + k + 1)
                    for c in range(2):
                        ins = mm(PS[:, banks + c, 0:HT], ones[:, :], SQ[:, k % 2, c * HT:(c + 1) * HT],
                                 start=k == k0, stop=k == k1 - 1)
                    ins.then_inc(sq_used, 1)
                pe.wait_ge(sq_used, base + k1)
                pe.sem_inc(ss_done, 1)

            tr = nc.tensor.transpose
            pe.wait_ge(consts_ready, 5)
            pe.wait_ge(table_in, 16 * 10)
            tr(PS[:, 7, 0:P], PRW[:, :], ident[:, :]).then_inc(table_t, 1)
            pe.wait_ge(xs_in, 16)
            for k in range(KD):
                ins = tr(PS[:, 6, k * NB:(k + 1) * NB], XS[:, k * P:(k + 1) * P], ident[0:NB, 0:NB])
            ins.then_inc(xs_t, 1)
            for j in range(TT):
                pe.wait_ge(x_in[j], 16)
            for k in range(KD):
                if k >= 2:
                    pe.wait_ge(x_ready[k % 2], k // 2)
                for j in range(TT):
                    ins = tr(PS[:, 4 + k % 2, j * P:(j + 1) * P], XT[:, j, k * P:(k + 1) * P], ident[:, :])
                ins.then_inc(x_t, 1)
                if k == 5:
                    pe.wait_ge(dg_ready, 1)
                    pe.wait_ge(table_ready, 1)
                    pe.wait_ge(xs_ready, 1)
                    mm(PS[:, 7, :], ones[:, :], DG[:, :, :].rearrange("p j k -> p (j k)"), start=True, stop=True)
                    mm(PS[:, 6, KD * NB:(KD + 1) * NB], ones[0:NB, :], DGS[:, :], start=True, stop=True).then_inc(rs0_ps, 1)
            unit_pair(0, range(KD), 0)
            unit(U_Q + 1, 0, U_Q + 1, 0)
            pe.wait_ge(setup_in, 32)
            pe.wait_ge(rs0_ready, 1)
            for n in range(NL):
                tr(PS[:, 7, n * NB:(n + 1) * NB], SHW[:, n * P:(n + 1) * P], ident[0:NB, 0:NB])
            r = NB * (CW - 1)
            for n in range(NL):
                ins = tr(PS[:, 7, NL * NB + n * r:NL * NB + (n + 1) * r], SCW[:, n * P:(n + 1) * P], ident[0:r, 0:r])
            ins.then_inc(state_t, 1)
            pe.wait_ge(yh_ready, 1)
            pe.wait_ge(x_ready[0], KD // 2)
            for j in range(TT):
                tr(PS[:, 4, j * NH:(j + 1) * NH], YH[:, j * P:(j + 1) * P], ident[0:NH, 0:NH])
            tr(PS[0:NB, 4, TT * NH:(TT + 1) * NH], YH[:, SEQ:T], ident[0:NH, 0:NH]).then_inc(logit_t, 1)
            with pe.Fori(0, NH // 2 - 2) as j:
                for s in range(2):
                    unit(U_Q + 2 + s, j, U_Q + 2 + s, j)
            pe.wait_ge(gather_in, 32)
            pe.wait_ge(absneg_ready, 1)
            for h in range(NH):
                ins = tr(PS[:, 4 + h // 4, (h % 4) * P:(h % 4 + 1) * P], LG[:, :, h], ident[:, :])
                if h % 4 == 3:
                    ins.then_inc(past_t, 1)
            unit(U_L - 2, 0, U_L - 2, 0)
            pe.wait_ge(logf_ready, 1)
            pe.wait_ge(masks_ready, 3)
            cum = PS[:, 6, 0:TT * NH].rearrange("p (j h) -> p j h", j=TT)
            mm(cum, tri[:, :], LS[:, 0:TT, :], start=True, stop=False)
            for j in range(TT - 1):
                n = TT - 1 - j
                ins = mm(cum[:, j + 1:, :], ones[:, :], LS[:, j:j + 1, :].to_broadcast([P, n, NH]), start=False, stop=j == TT - 2)
            ins.then_inc(cum_ps, 1)
            pe.wait_ge(tot_ready, 1)
            for g in range(2):
                pe.wait_ge(past_ready, g + 1)
                mm(PS[:, 4 + g, :], low[:, :], LT[:, 4 * g:4 * g + 4, :].rearrange("p h n -> p (h n)"), start=True, stop=False)
                mm(PS[:, 4 + g, :], ones[:, :], MT[:, 4 * g:4 * g + 4, :].rearrange("p h n -> p (h n)"), start=False, stop=True)\
                    .then_inc(suf_ps, 1)
            unit(U_L - 1, 0, U_L - 1, 0)

            def value(h, b, n):
                half, m = n // NHH, n % NHH
                slot = b % 2 if half else 2 + b % 2
                first = b == 0 and n == NHH
                if first:
                    pe.wait_ge(pp_ready, h + 1)
                if m == 0:
                    pe.wait_ge(v_full[slot], 16 * (NPG // 2 * h + b // 2 + 1))
                ins = mm(PS[:, 7, one(NH * h + n)], VR[:, slot, m * HD:(m + 1) * HD], SUF[:, n, one(h), b],
                         start=first and isinstance(h, int) and h == 0, stop=b == NPG - 1 and half == 1, skip_group_check=True)
                if m == NHH - 1:
                    ins.then_inc(v_used if half else v_used0, 1)

            def sum_values(h, pages=None):
                pe.wait_ge(v_acc, pages or NPG // 2 * (h + 1))
                for n in range(NHH):
                    ins = mm(PS[:, 7, one(NH * h + n)], AV[:, n * HD:(n + 1) * HD], ones[:, 0:1], start=False, stop=True,
                             skip_group_check=True)
                ins.then_inc(v_summed, 1)

            def scores(h):
                pe.wait_ge(qdf_ready, h + 1)
                for t in range(TT):
                    bank, c = S_AT[t]
                    n = (t + 1) * P
                    dst = PS[:, bank, c:c + n]
                    mm(dst, qcur[:, t * P:(t + 1) * P], kT[:, 0:n], start=True, stop=False)
                    mm(dst, ones[:, :], PT[:, 0:n], start=False, stop=False)
                    ins = mm(dst[:, n - P:n], ident[:, :], maskneg[:, :], start=False, stop=True)
                ins.then_inc(s_done, 1)

            def transpose_probs(h):
                pe.wait_ge(p_norm, h + 1)
                for j in range(TT):
                    bank, c = PT_BANK[j]
                    for t in range(j, TT):
                        ins = tr(PS[:, bank, c + (t - j) * P:c + (t - j + 1) * P],
                                 PR[:, P_AT[t] + j * P:P_AT[t] + (j + 1) * P], ident[:, :])
                    if j != 2:
                        ins.then_inc(pt_ps, 1)

            def attend(h):
                pe.wait_ge(vtok_ready, h + 1)
                for j in range(TT):
                    pe.wait_ge(pt_ready, 3 * h + min(j + 1, 3))
                    ins = mm(PS[:, 4, j * P:SEQ], vtok[:, j, :], PT[:, PT_AT[j]:PT_AT[j] + (TT - j) * P],
                             start=j == 0, stop=j == TT - 1)
                ins.then_inc(att_ps, 1)

            def last_sums():
                pe.wait_ge(lru_done, NL)
                hr = (CW - 1) * NL * (NB + 1) // 2
                cv = CVALL[:, :, :].rearrange("p r n -> p (r n)")
                pe.wait_ge(pt_ready, 3 * NH)
                tr(PS[0:NL * (NB + 1), 5, 0:P], HALL[:, :, :].rearrange("p r n -> p (r n)"), ident[:, :])
                for g in range(2):
                    ins = tr(PS[0:hr, 5, (g + 1) * P:(g + 2) * P], cv[:, g * hr:(g + 1) * hr], ident[:, :])
                ins.then_inc(tail_h, 1)
                pe.wait_ge(merge_in, 1)
                pe.wait_ge(att_ready, NH)
                new_s = PS[:, 4, 0:NH * NB]
                mm(new_s, ones[:, :], qcur[:, 0:64], start=True, stop=False)
                mm(new_s, ones[0:NB, :], qcur[0:NB, 64:128], start=False, stop=True)
                mm(PS[:, 6, 0:NH * NB], ones[:, :], DEN[:, :, :].rearrange("p h b -> p (h b)"), start=True, stop=True)\
                    .then_inc(merge_ps, 1)
                for s, v in out_of_banks(U_O):
                    pe.wait_ge(s, v)
                norm_sums(-NH, NH, KD, NSQ, 0)

            def step(i, head, prev, sums=True):
                def queries():
                    pe.wait_ge(qcol_ready, i + 1)
                    if prev:
                        pe.wait_ge(sig_done, i)
                    for n in range(NH):
                        ins = mm(PS[:, 4 + n // 4, n % 4 * P:(n % 4 + 1) * P], QCOL[:, n:n + 1].to_broadcast([P, P]), ident[:, :],
                                 start=True, stop=True)
                    ins.then_inc(qb_ps, 1)

                def head_scores():
                    if head:
                        pe.wait_ge(qb_ready, i + 1)
                    scores(i - 1)

                def rows():
                    pe.wait_ge(tile_out[1], at(U_L, 2 * i)[1] + 1)
                    if prev:
                        pe.wait_ge(pt_ready, 3 * i)
                    for j in range(TT):
                        ins = tr(PS[:, 5, j * P:(j + 1) * P], kT[:, j * P:(j + 1) * P], ident[:, :])
                    ins.then_inc(ktr_ps, 1)
                    pe.wait_ge(tile_out[0], at(U_L + 1, 2 * i)[1] + 1)
                    for j in range(TT):
                        ins = tr(PS[:, 6, j * P:(j + 1) * P], vT[:, j * P:(j + 1) * P], ident[:, :])
                    ins.then_inc(vtr_ps, 1)

                extra = {}
                if head:
                    extra[0, 7] = queries
                    extra[3, 7] = rows
                if prev and sums:
                    extra[1, 13] = lambda: sum_values(i - 2)
                if prev:
                    extra[1, 5] = head_scores
                    extra[2, 7] = lambda: transpose_probs(i - 1)
                    extra[2, 19] = lambda: attend(i - 1)

                def places(q, n):
                    f = []
                    if prev and n % 8 < (NH if n // 8 % 2 else NHH):
                        f.append(lambda: value(i - 1, K_Q * q + n // 8, (n + NHH) % NH))
                    if (q, n) in extra:
                        f.append(extra[q, n])
                    return f

                for q in range(4):
                    insert = {n: places(q, n) for n in range(2 * KD)}
                    if head:
                        unit(U_L + q, 2 * i, U_L + q, 2 * i, insert)
                    else:
                        if q == 3:
                            last_sums()
                        for n in range(2 * KD):
                            for f in insert[n]:
                                f()
                if head:
                    pe.wait_ge(gw_full, 32 * (i + 1))
                    pe.wait_ge(conv_done, i + 1)
                    if prev:
                        pe.wait_ge(att_ready, i)
                    pe.wait_ge(ktok_ready, i + 1)
                    pe.wait_ge(vtok_ready, i + 1)
                    for g in range(2):
                        mm(PS[:, 4 + g, :], GW[:, g, :], XC[:, 0:SEQ], start=True, stop=True)
                    for g in range(2):
                        ins = mm(PS[:, 6, g * NB:(g + 1) * NB], GW[:, g, :], XC[:, SEQ:T], start=True, stop=True)
                    ins.then_inc(gates_ps, 1)

            pe.wait_ge(cum_ready, 3)
            step(0, True, False)
            step(1, True, True, False)
            with pe.Fori(2, NH) as i:
                step(i, True, True)
            step(NH, False, True)
            for slot, b, _, _ in last_halves:
                pe.wait_ge(v_full[slot], 16 * (NPG // 2 * NB + (1 if slot != 2 else -3)))
                for n in range(NHH):
                    mm(PS[:, 7, NH * (NB - 1) + n:NH * (NB - 1) + n + 1], VR[:, slot, n * HD:(n + 1) * HD],
                       SUF[:, n, NB - 1, b:b + 1], start=False, stop=True, skip_group_check=True)
            sum_values(NB - 1, NPG // 2 * NB - 4)

            unit(U_O, 0, U_O, 0, kts=range(NH, KD), last=False, ready={n: (xl_ready, KD + n + 1) for n in range(NL)})
            pe.wait_ge(merge_in, 2)
            pe.wait_ge(tail_rows, 1)
            pe.wait_ge(pvs_ready, 1)
            for src, b0 in ((KS, 4), (VS, 6)):
                for h in range(NH):
                    ins = tr(PS[0:NB, b0 + h // 4, (h % 4) * P:(h % 4 + 1) * P], src[:, h, :], ident[:, :])
            ins.then_inc(tail_t, 1)
            pe.wait_ge(ms_read, 1)
            pe.wait_ge(tail_ready, 1)
            norm_sums(NL, 0, NH, NSQ, 4)
            unit(U_O + 1, 0, U_O + 1, 0, kts=range(NH, KD), last=False)
            unit_pair(U_O, range(NH), KD + NL, first=False)
            with pe.Fori(0, KD // 2 - 1) as j:
                for s in range(2):
                    unit(U_O + 2 + s, j, U_O + 2 + s, j)

            def residual_sums():
                pe.wait_ge(acc_used, KD + 2)
                pe.wait_ge(ms_read, 2)
                for c in range(2):
                    ins = mm(PS[:, 4 + c, 0:HT], ones[:, :], ACC[:, c * HT:(c + 1) * HT], start=True, stop=True)
                ins.then_inc(ss_done, 1)

            def up(c, j, first=False):
                for s in range(2):
                    if first and s == 0:
                        unit(U_F, 0, U_F, 0, {9: [residual_sums]}, ready={k: (xl_ready, 2 * KD + k + 1) for k in range(KD)})
                    else:
                        unit(U_F + s, c * (UC // 2) + j, U_F + s, c * (TC // 2) + j)

            def down(c, j, rows=None):
                for s in range(2):
                    slot, w = at(U_F + CH + s, c * (UC // 2) + j)
                    pe.wait_ge(lo_done, 2 * w + slot + 1)
                    for m in range(2):
                        pair, tw = at(U_F + CH + 2 * s + m, c * (TC // 2) + 2 * j)
                        pe.wait_ge(tile_out[pair], tw)
                        ready = {0: (hl_ready, CH * c + CH + 1), CH - 1: (hl_ready, CH * c + CH + 2)} if s == 0 and m == 0 else None
                        ins = products(HH, HL, lambda k: WH[slot][:, (2 * k + m) * P:(2 * k + m + 1) * P],
                                       lambda k: WL[slot][:, (2 * k + m) * P:(2 * k + m + 1) * P],
                                       [PS[:, 2 * pair + c2, 0:HT] for c2 in range(2)], range(CH),
                                       insert=rows(2 * s + m) if rows else {}, ready=ready)
                        ins.then_inc(tile_done, 1)

            def chunk(c, first=False):
                if first:
                    up(c, 0, True)
                with pe.Fori(1 if first else 0, CH // 2) as j:
                    up(c, j)
                if not (isinstance(c, int) and c == NC - 1):
                    with pe.Fori(0, CH // 2) as j:
                        down(c, j)

            def y_rows(j, n):
                bank = 6 + n // 2
                pe.wait_ge(yn_ready, 4 * j + n + 1)
                if not (isinstance(j, int) and 4 * j + n < 2):
                    pe.wait_ge(yt_ready[n % 2], 2 * j + n // 2)
                if n % 2 == 0 and not (isinstance(j, int) and j == 0):
                    pe.wait_ge(ys_ready[bank - 6], j)
                tr(PS[0:NB, bank, (n % 2) * P:(n % 2 + 1) * P], GA[:, n % 2, SEQ:T], ident[:, :])
                for t in range(TT):
                    ins = tr(PS[:, 4 + n % 2, t * P:(t + 1) * P], GA[:, n % 2, t * P:(t + 1) * P], ident[:, :])
                ins.then_inc(y_t, 1)

            chunk(0, True)
            with pe.Fori(1, NC - 1) as c:
                chunk(c)
            chunk(NC - 1)
            pe.wait_ge(ms_read, 3)
            pe.sem_inc(y_t, 2)
            down(NC - 1, 0, lambda n: {9: [lambda: y_rows(0, n - 1)]} if n else {})
            with pe.Fori(1, CH // 2) as j:
                down(NC - 1, j, lambda n: {9: [lambda: y_rows(j, n - 1) if n else y_rows(j - 1, 3)]})
            y_rows(CH // 2 - 1, 3)
            pe.wait_ge(acc_used, 2 * KD + 2)
            pe.wait_ge(ys_ready[0], KD // 4)
            for t in range(TT):
                mm(PS[:, 6, 2 * P + t:2 * P + t + 1], ACC[:, t * P:(t + 1) * P], ones[:, 0:1], start=True, stop=True)
            mm(PS[0:NB, 6, 2 * P + TT:2 * P + TT + 1], ACC[:, SEQ:T], ones[:, 0:1], start=True, stop=True).then_inc(tok_ss, 1)



_INS = ['x_prompt', 'x_sample', 'cache_k', 'cache_v', 'cache_logf', 'state_conv', 'state_h', 'page_table',
        'g_mix', 'w_in', 'b_f', 'w_conv', 'b_conv', 'w_gate_a', 'b_gate_a', 'w_gate_x', 'b_gate_x', 'lru_lambda',
        'g_att_out', 'g_lru_out', 'w_out', 'g_ffn', 'w_up', 'w_down', 'g_final']


def kernel(**inputs):
    import numpy as np
    import concourse.bacc as bacc
    from concourse.bass_utils import run_bass_kernel_spmd

    a = {n: np.ascontiguousarray(inputs[n]) for n in _INS}
    B, S, D = a['x_prompt'].shape
    NB, S1 = a['x_sample'].shape[:2]
    L, _, _, H, HD = a['cache_k'].shape
    CW1, DL = a['state_conv'].shape[2:]
    outs = [(B, S, D), (NB, S1, D),
            (L, B, S, H, HD), (L, B, S, H, HD), (L, B, S, H), (L, B, CW1, DL), (L, B, DL),
            (L, NB, S1, H, HD), (L, NB, S1, H, HD), (L, NB, S1, H), (L, NB, CW1, DL), (L, NB, DL)]
    nc = bacc.Bacc("TRN2", target_bir_lowering=False, num_devices=1)
    args = [nc.dram_tensor(f"in_{n}", a[n].shape, mybir.dt.from_np(a[n].dtype), kind="ExternalInput").ap() for n in _INS]
    args += [nc.dram_tensor(f"out_{i}", s, F32, kind="ExternalOutput").ap() for i, s in enumerate(outs)]
    hymba_step(nc, *args)
    r = run_bass_kernel_spmd(nc, [{f"in_{n}": a[n] for n in _INS}], core_ids=[0])
    return tuple(r.results[0][f"out_{i}"] for i in range(len(outs)))
```
